# Optimizing a Trainium2 kernel written in Bass

```python
import math
import jax
import jax.numpy as jnp
from jax import lax
import numpy as np

D_MODEL = 1024
BATCH = 1
SEQ = 256
DEPTH = 2

SSD_HEADS = 16
SSD_HEAD_DIM = 64
SSD_INNER = SSD_HEADS * SSD_HEAD_DIM
SSD_GROUPS = 2
SSD_STATE = 128
SSD_CONV = 4
SSD_CHUNK = 128
SSD_CONV_CH = SSD_INNER + 2 * SSD_GROUPS * SSD_STATE
DT_MIN = 1e-3
DT_MAX = 1e-1

SGU_WIDTH = 1024
SGU_GROUPS = 8
SGU_GROUP_DIM = SGU_WIDTH // SGU_GROUPS
SGU_CHUNK = 128

MLA_HEADS = 16
MLA_Q_RANK = 256
MLA_KV_RANK = 128
MLA_NOPE = 64
MLA_ROPE = 32
MLA_V = 64
MLA_QK = MLA_NOPE + MLA_ROPE
MLA_WIDTH = MLA_HEADS * MLA_V
ATTN_BLOCK = 128
ROPE_BASE = 10000.0

N_BRANCH = 3
IN_SSD = 2 * SSD_INNER + 2 * SSD_GROUPS * SSD_STATE + SSD_HEADS
IN_SGU = 2 * SGU_WIDTH
IN_MLA = MLA_Q_RANK + MLA_KV_RANK + MLA_ROPE
IN_GATE = N_BRANCH * D_MODEL
N_IN = IN_SSD + IN_SGU + IN_MLA + IN_GATE

FFN_DENSE = 2816
N_EXPERTS = 8
TOP_K = 2
FFN_EXPERT = 3584
N_DENSE = (DEPTH + 1) // 2
N_MOE = DEPTH // 2

EPS = 1e-6
LN_EPS = 1e-5

kernel_name = 'hybrid_ssd_sgu_mla_moe_block'

def rms_norm(x, g, eps=EPS):
    xf = x.astype(jnp.float32)
    y = xf * lax.rsqrt(jnp.mean(xf * xf, axis=-1, keepdims=True) + eps)
    return (y * g.astype(jnp.float32)).astype(x.dtype)

def layer_norm(x, g, b, eps=LN_EPS):
    xf = x.astype(jnp.float32)
    mu = jnp.mean(xf, axis=-1, keepdims=True)
    xc = xf - mu
    y = xc * lax.rsqrt(jnp.mean(xc * xc, axis=-1, keepdims=True) + eps)
    return (y * g.astype(jnp.float32) + b.astype(jnp.float32)).astype(x.dtype)

def causal_depthwise_conv(x, w, b):
    ch = x.shape[-1]
    y = lax.conv_general_dilated(
        x, w[:, None, :].astype(x.dtype), window_strides=(1,),
        padding=[(SSD_CONV - 1, 0)], dimension_numbers=('NWC', 'WIO', 'NWC'),
        feature_group_count=ch)
    return y + b.astype(x.dtype)

def segsum_exp(a):
    l = a.shape[-1]
    cs = jnp.cumsum(a, axis=-1)
    diff = cs[..., :, None] - cs[..., None, :]
    mask = jnp.tril(jnp.ones((l, l), dtype=bool))
    return jnp.where(mask, jnp.exp(jnp.where(mask, diff, 0.0)), 0.0)

def ssd_scan(x, dt, a, b, c):
    bsz, s, h, p = x.shape
    g, n = b.shape[-2], b.shape[-1]
    k = h // g
    l = SSD_CHUNK
    nc = s // l
    xs = (x * dt[..., None]).reshape(bsz, nc, l, g, k, p)
    adt = jnp.moveaxis((dt * a).reshape(bsz, nc, l, g, k), 2, -1)
    a_cs = jnp.cumsum(adt, axis=-1)
    bc = b.reshape(bsz, nc, l, g, n)
    cc = c.reshape(bsz, nc, l, g, n)
    decay = segsum_exp(adt)
    cb = jnp.einsum('bclgn,bcsgn->bcgls', cc, bc)
    y_diag = jnp.einsum('bcgls,bcgkls,bcsgkp->bclgkp', cb, decay, xs)
    decay_states = jnp.exp(a_cs[..., -1:] - a_cs)
    states = jnp.einsum('bclgn,bcgkl,bclgkp->bcgkpn', bc, decay_states, xs)
    chunk_decay = jnp.exp(a_cs[..., -1])

    def step(carry, inp):
        st, dec = inp
        return carry * dec[..., None, None] + st, carry

    init = jnp.zeros((bsz, g, k, p, n), x.dtype)
    _, prev = lax.scan(step, init, (jnp.moveaxis(states, 1, 0), jnp.moveaxis(chunk_decay, 1, 0)))
    prev = jnp.moveaxis(prev, 0, 1)
    y_off = jnp.einsum('bclgn,bcgkpn,bcgkl->bclgkp', cc, prev, jnp.exp(a_cs))
    return (y_diag + y_off).reshape(bsz, s, h, p)

def ssd_branch(zxbcdt, conv_w, conv_b, dt_bias, a_log, d_skip, norm_g):
    bsz, s, _ = zxbcdt.shape
    f32 = jnp.float32
    z, xbc, dt = jnp.split(zxbcdt, [SSD_INNER, SSD_INNER + SSD_CONV_CH], axis=-1)
    xbc = jax.nn.silu(causal_depthwise_conv(xbc, conv_w, conv_b))
    xh, bm, cm = jnp.split(xbc, [SSD_INNER, SSD_INNER + SSD_GROUPS * SSD_STATE], axis=-1)
    xh = xh.reshape(bsz, s, SSD_HEADS, SSD_HEAD_DIM).astype(f32)
    bm = bm.reshape(bsz, s, SSD_GROUPS, SSD_STATE).astype(f32)
    cm = cm.reshape(bsz, s, SSD_GROUPS, SSD_STATE).astype(f32)
    dt = jax.nn.softplus(dt.astype(f32) + dt_bias.astype(f32))
    a = -jnp.exp(a_log.astype(f32))
    y = ssd_scan(xh, dt, a, bm, cm) + xh * d_skip.astype(f32)[:, None]
    yg = (y.reshape(bsz, s, SSD_INNER) * jax.nn.silu(z.astype(f32)))
    yg = yg.reshape(bsz, s, SSD_GROUPS, SSD_INNER // SSD_GROUPS)
    yg = yg * lax.rsqrt(jnp.mean(yg * yg, axis=-1, keepdims=True) + EPS)
    return (yg.reshape(bsz, s, SSD_INNER) * norm_g.astype(f32)).astype(zxbcdt.dtype)

def sgu_branch(uv, ln_g, ln_b, w_s, b_s):
    bsz, s, _ = uv.shape
    uv = jax.nn.gelu(uv, approximate=False)
    u, v = jnp.split(uv, 2, axis=-1)
    v = layer_norm(v, ln_g, ln_b)
    nc = s // SGU_CHUNK
    v = v.reshape(bsz, nc, SGU_CHUNK, SGU_GROUPS, SGU_GROUP_DIM)
    w = w_s * jnp.tril(jnp.ones((SGU_CHUNK, SGU_CHUNK), w_s.dtype))
    mixed = jnp.einsum('gts,bcsgd->bctgd', w, v) + jnp.swapaxes(b_s, 0, 1)[None, None, :, :, None]
    return u * mixed.reshape(bsz, s, SGU_WIDTH)

def rope_tables(s, dim):
    inv = 1.0 / (ROPE_BASE ** (jnp.arange(0, dim, 2, dtype=jnp.float32) / dim))
    ang = jnp.arange(s, dtype=jnp.float32)[:, None] * inv[None, :]
    return jnp.cos(ang), jnp.sin(ang)

def apply_rope(x, cos, sin):
    x1, x2 = jnp.split(x.astype(jnp.float32), 2, axis=-1)
    c = cos[None, :, None, :]
    sn = sin[None, :, None, :]
    return jnp.concatenate([x1 * c - x2 * sn, x1 * sn + x2 * c], axis=-1).astype(x.dtype)

def causal_attention(q, k, v):
    bsz, s, h, dq = q.shape
    nb = s // ATTN_BLOCK
    scale = dq ** -0.5
    qb = jnp.moveaxis(q.reshape(bsz, nb, ATTN_BLOCK, h, dq), 1, 0)
    k_pos = jnp.arange(s)

    def one_block(args):
        qi, start = args
        sc = jnp.einsum('bqhd,bkhd->bhqk', qi, k).astype(jnp.float32) * scale
        q_pos = start + jnp.arange(ATTN_BLOCK)
        mask = k_pos[None, :] <= q_pos[:, None]
        p = jax.nn.softmax(jnp.where(mask, sc, -jnp.inf), axis=-1)
        return jnp.einsum('bhqk,bkhd->bqhd', p.astype(v.dtype), v)

    out = lax.map(one_block, (qb, jnp.arange(nb) * ATTN_BLOCK))
    return jnp.moveaxis(out, 0, 1).reshape(bsz, s, h, v.shape[-1])

def mla_branch(lat, q_norm_g, w_uq, kv_norm_g, w_ukv, q_head_g, k_head_g):
    bsz, s, _ = lat.shape
    q_lat, kv_lat, k_pe = jnp.split(lat, [MLA_Q_RANK, MLA_Q_RANK + MLA_KV_RANK], axis=-1)
    q = (rms_norm(q_lat, q_norm_g) @ w_uq).reshape(bsz, s, MLA_HEADS, MLA_QK)
    kv = (rms_norm(kv_lat, kv_norm_g) @ w_ukv).reshape(bsz, s, MLA_HEADS, MLA_NOPE + MLA_V)
    k_nope, v = jnp.split(kv, [MLA_NOPE], axis=-1)
    k_pe_h = jnp.broadcast_to(k_pe[:, :, None, :], (bsz, s, MLA_HEADS, MLA_ROPE))
    k = jnp.concatenate([k_nope, k_pe_h], axis=-1)
    q = rms_norm(q, q_head_g)
    k = rms_norm(k, k_head_g)
    cos, sin = rope_tables(s, MLA_ROPE)
    q = jnp.concatenate([q[..., :MLA_NOPE], apply_rope(q[..., MLA_NOPE:], cos, sin)], axis=-1)
    k = jnp.concatenate([k[..., :MLA_NOPE], apply_rope(k[..., MLA_NOPE:], cos, sin)], axis=-1)
    out = causal_attention(q, k, v)
    return out.reshape(bsz, s, MLA_WIDTH)

def swiglu(x, wg, wu, wd):
    return (jax.nn.silu(x @ wg) * (x @ wu)) @ wd

def moe_ffn(x, router_w, wg, wu, wd):
    bsz, s, d = x.shape
    t = x.reshape(-1, d)
    logits = (t @ router_w).astype(jnp.float32)
    top_v, top_i = lax.top_k(logits, TOP_K)
    top_w = jax.nn.softmax(top_v, axis=-1)
    combine = jnp.sum(jax.nn.one_hot(top_i, N_EXPERTS, dtype=jnp.float32) * top_w[..., None], axis=1)
    y = jnp.zeros_like(t)
    for e in range(N_EXPERTS):
        y = y + combine[:, e:e + 1].astype(t.dtype) * swiglu(t, wg[e], wu[e], wd[e])
    return y.reshape(bsz, s, d)

def setup_inputs(seed: int = 0) -> dict:
    key = jax.random.key(seed)
    keys = iter(jax.random.split(key, 48))
    f32 = jnp.float32

    def normal(shape, scale):
        return jax.random.normal(next(keys), shape, f32) * scale

    def gain(shape):
        return 1.0 + 0.02 * jax.random.normal(next(keys), shape, f32)

    L = DEPTH
    dt = jnp.exp(jax.random.uniform(next(keys), (L, SSD_HEADS), f32, math.log(DT_MIN), math.log(DT_MAX)))
    inputs = {}
    inputs['x'] = normal((BATCH, SEQ, D_MODEL), 1.0)
    inputs['mix_norm_g'] = gain((L, D_MODEL))
    inputs['w_in'] = normal((L, D_MODEL, N_IN), D_MODEL ** -0.5)
    inputs['conv_w'] = normal((L, SSD_CONV, SSD_CONV_CH), SSD_CONV ** -0.5)
    inputs['conv_b'] = normal((L, SSD_CONV_CH), 0.02)
    inputs['dt_bias'] = dt + jnp.log(-jnp.expm1(-dt))
    inputs['a_log'] = jnp.log(jax.random.uniform(next(keys), (L, SSD_HEADS), f32, 1.0, 16.0))
    inputs['d_skip'] = gain((L, SSD_HEADS))
    inputs['ssd_norm_g'] = gain((L, SSD_INNER))
    inputs['sgu_ln_g'] = gain((L, SGU_WIDTH))
    inputs['sgu_ln_b'] = normal((L, SGU_WIDTH), 0.02)
    inputs['sgu_w'] = normal((L, SGU_GROUPS, SGU_CHUNK, SGU_CHUNK), SGU_CHUNK ** -0.5)
    inputs['sgu_b'] = gain((L, SGU_GROUPS, SGU_CHUNK))
    inputs['q_norm_g'] = gain((L, MLA_Q_RANK))
    inputs['w_uq'] = normal((L, MLA_Q_RANK, MLA_HEADS * MLA_QK), MLA_Q_RANK ** -0.5)
    inputs['kv_norm_g'] = gain((L, MLA_KV_RANK))
    inputs['w_ukv'] = normal((L, MLA_KV_RANK, MLA_HEADS * (MLA_NOPE + MLA_V)), MLA_KV_RANK ** -0.5)
    inputs['q_head_g'] = gain((L, MLA_QK))
    inputs['k_head_g'] = gain((L, MLA_QK))
    inputs['w_br_ssd'] = normal((L, SSD_INNER, D_MODEL), SSD_INNER ** -0.5)
    inputs['w_br_sgu'] = normal((L, SGU_WIDTH, D_MODEL), SGU_WIDTH ** -0.5)
    inputs['w_br_mla'] = normal((L, MLA_WIDTH, D_MODEL), MLA_WIDTH ** -0.5)
    inputs['w_out'] = normal((L, D_MODEL, D_MODEL), D_MODEL ** -0.5)
    inputs['ffn_norm_g'] = gain((L, D_MODEL))
    inputs['ffn_w_gate'] = normal((N_DENSE, D_MODEL, FFN_DENSE), D_MODEL ** -0.5)
    inputs['ffn_w_up'] = normal((N_DENSE, D_MODEL, FFN_DENSE), D_MODEL ** -0.5)
    inputs['ffn_w_down'] = normal((N_DENSE, FFN_DENSE, D_MODEL), FFN_DENSE ** -0.5)
    inputs['router_w'] = normal((N_MOE, D_MODEL, N_EXPERTS), D_MODEL ** -0.5)
    inputs['moe_w_gate'] = normal((N_MOE, N_EXPERTS, D_MODEL, FFN_EXPERT), D_MODEL ** -0.5)
    inputs['moe_w_up'] = normal((N_MOE, N_EXPERTS, D_MODEL, FFN_EXPERT), D_MODEL ** -0.5)
    inputs['moe_w_down'] = normal((N_MOE, N_EXPERTS, FFN_EXPERT, D_MODEL), FFN_EXPERT ** -0.5)
    return inputs

def reference(x, mix_norm_g, w_in, conv_w, conv_b, dt_bias, a_log, d_skip, ssd_norm_g,
              sgu_ln_g, sgu_ln_b, sgu_w, sgu_b, q_norm_g, w_uq, kv_norm_g, w_ukv,
              q_head_g, k_head_g, w_br_ssd, w_br_sgu, w_br_mla, w_out, ffn_norm_g,
              ffn_w_gate, ffn_w_up, ffn_w_down, router_w, moe_w_gate, moe_w_up, moe_w_down):
    for i in range(DEPTH):
        h = rms_norm(x, mix_norm_g[i])
        proj = h @ w_in[i]
        p_ssd, p_sgu, p_mla, p_gate = jnp.split(
            proj, [IN_SSD, IN_SSD + IN_SGU, IN_SSD + IN_SGU + IN_MLA], axis=-1)
        y_ssd = ssd_branch(p_ssd, conv_w[i], conv_b[i], dt_bias[i], a_log[i], d_skip[i], ssd_norm_g[i])
        y_sgu = sgu_branch(p_sgu, sgu_ln_g[i], sgu_ln_b[i], sgu_w[i], sgu_b[i])
        y_mla = mla_branch(p_mla, q_norm_g[i], w_uq[i], kv_norm_g[i], w_ukv[i], q_head_g[i], k_head_g[i])
        g_ssd, g_sgu, g_mla = jnp.split(jax.nn.sigmoid(p_gate), N_BRANCH, axis=-1)
        merged = (g_ssd * (y_ssd @ w_br_ssd[i])
                  + g_sgu * (y_sgu @ w_br_sgu[i])
                  + g_mla * (y_mla @ w_br_mla[i]))
        x = x + merged @ w_out[i]
        h = rms_norm(x, ffn_norm_g[i])
        j = i // 2
        if i % 2 == 0:
            x = x + swiglu(h, ffn_w_gate[j], ffn_w_up[j], ffn_w_down[j])
        else:
            x = x + moe_ffn(h, router_w[j], moe_w_gate[j], moe_w_up[j], moe_w_down[j])
    return x


_drawn_inputs = setup_inputs


def setup_inputs(seed=0):
    import zlib

    import numpy as np

    out = dict(_drawn_inputs(seed))
    spreads = {}
    factors = {'d_skip': 10.228,
     'sgu_ln_g': 4.673,
     'sgu_ln_b': 3.9,
     'sgu_b': 3.057,
     'q_norm_g': 8.0,
     'kv_norm_g': 4.926,
     'q_head_g': 8.0,
     'k_head_g': 8.0,
     'ssd_norm_g': 2.789}
    for name, (base, spread) in spreads.items():
        noise = np.random.default_rng([zlib.crc32(name.encode()), seed]).standard_normal(out[name].shape)
        drawn = base * np.exp(spread * noise) if base else spread * noise
        out[name] = jnp.asarray(drawn.astype(out[name].dtype))
    for name, factor in factors.items():
        out[name] = (out[name] * factor).astype(out[name].dtype)
    return out
```

```python
from contextlib import ExitStack

import concourse.bass as bass
from concourse import mybir

ALU = mybir.AluOpType
ACT = mybir.ActivationFunctionType
F32 = mybir.dt.float32
I32 = mybir.dt.int32
AX = mybir.AxisListType

P = 128
NT = 2
D = 1024
KD = D // P
DEPTH = 2
HEADS = 16
HD = 64
QK = 96
NOPE = 64
HALF_ROPE = 16
CONV_CHUNKS = 12
TAPS = 4
EPS = 1e-6
LN_EPS = 1e-5
SCALE = QK ** -0.5
N = 512
SLOT = KD * N
FFN_DENSE = 2816
FFN_EXPERT = 3584
EXPERTS = 8
MAX_ITEMS = 11
ITEM_SLOTS = 16

C_Z, C_XBC, C_DT, C_U, C_V, C_LAT, C_GATE = 0, 1024, 2560, 2576, 3600, 4624, 5040
LAT = 416

ROWS = {}
_at = 0
for _name, _n in (("mix", 8), ("ffn", 8), ("conv_b", 12), ("conv_w", 48), ("ssd", 8), ("q", 2), ("kv", 1),
                  ("sgu_b", 8), ("ln_g", 8), ("ln_b", 8)):
    ROWS[_name] = _at
    _at += _n
N_ROWS = _at

CONST = {}
_at = 0
for _name, _n in (("ident", P), ("tri", P), ("before", P), ("slot", P), ("mask", 2 * P), ("cos", 2 * HALF_ROPE),
                  ("sin", 2 * HALF_ROPE), ("item", ITEM_SLOTS * EXPERTS), ("expert", ITEM_SLOTS * EXPERTS)):
    CONST[_name] = _at
    _at += _n
N_CONST = _at


def mixer_panels():
    out = [(f"xbc{n}", "in", C_XBC + N * n, N) for n in range(3)]
    out += [("lat", "in", C_LAT, LAT)]
    out += [(f"z{n}", "in", C_Z + N * n, N) for n in range(2)]
    out += [("uq", "uq", 0, HEADS * QK), ("ukv", "ukv", 0, HEADS * 2 * HD)]
    out += [(f"u{n}", "in", C_U + N * n, N) for n in range(2)]
    out += [(f"v{n}", "in", C_V + N * n, N) for n in range(2)]
    for b, br in enumerate(("ssd", "sgu", "mla")):
        for n in range(2):
            out += [(f"gate_{br}{n}", "in", C_GATE + D * b + N * n, N), (f"br_{br}{n}", br, N * n, N)]
    out += [(f"out{n}", "out", N * n, N) for n in range(2)]
    return out


def psum_jobs():
    j = ["vec"] + [f"ht{t}{h}" for t in range(NT) for h in range(2)]
    j += [f"xbc{i}" for i in range(6)] + ["dt"] + ["lat0", "lat1"]
    j += [f"z{n}{t}" for n in range(2) for t in range(NT)]
    j += ["cs"] + [f"xt{t}{h}" for t in range(NT) for h in range(2)] + ["bt", "cb", "latT0", "latT1"]
    j += [f"q{t}{n}" for t in range(NT) for n in range(3)]
    j += [f"kv{t}{n}" for t in range(NT) for n in range(4)]
    j += [f"u{n}{t}" for n in range(2) for t in range(NT)]
    j += ["st0", "st1", "yo0", "yo1"] + [f"rb0{q}" for q in range(4)]
    j += ["v00", "v01", "yd00", "yd01"] + [f"rb1{q}" for q in range(4)]
    j += ["v10", "v11", "yd10", "yd11"] + ["wt0", "wt1", "lng0", "lng1", "lnb0", "lnb1"]
    j += closing("ssd")
    j += [f"qT{t}{i}" for t in range(NT) for i in range(4)] + [f"kT{t}{i}" for t in range(NT) for i in range(4)]
    j += [f"mx{t}{h}" for t in range(NT) for h in range(2)]
    for kind, i in attention_order():
        if kind == "close":
            j += closing_part("sgu", i)
        else:
            j += [f"{kind}{i}"]
    j += closing("mla")
    j += [f"mT{t}{h}" for t in range(NT) for h in range(2)]
    j += [f"out{n}{t}" for n in range(2) for t in range(NT)]
    j += [f"ft{t}{h}" for t in range(NT) for h in range(2)]
    return j


def closing_part(br, i):
    if i == 1:
        return [f"yT_{br}{t}{h}" for t in range(NT) for h in range(2)]
    what, n = (("gate", 0), None, ("br", 0), ("gate", 1), ("br", 1))[i]
    return [f"{what}_{br}{n}{t}" for t in range(NT)]


def closing(br):
    return [x for i in range(5) for x in closing_part(br, i)]


GROUPS = [(0, 4 * q, 4) for q in range(4)] + [(1, 2 * q, 2) for q in range(8)]


def attention_order():
    out = []
    for s in range(len(GROUPS) + 2):
        if s < len(GROUPS):
            out.append(("sc", s))
        if s in (0, 2, 4, 6, 8):
            out.append(("close", s // 2))
        if 1 <= s <= len(GROUPS):
            out.append(("pt", s - 1))
        if s >= 2:
            out.append(("o", s - 2))
    return out


PANELS = mixer_panels()
JOBS = psum_jobs()
JOB = {name: i for i, name in enumerate(JOBS)}
assert len(JOB) == len(JOBS)
RING = 4
MOE_RING = 7
DENSE_PANELS = [(c, min(N, FFN_DENSE - c)) for c in range(0, FFN_DENSE, N)]
DENSE_UNITS = [(p, t, w) for p, (c, w) in enumerate(DENSE_PANELS) for t in range(NT)]
MOE_PANELS = [(c, N) for c in range(0, FFN_EXPERT, N)]
LAYER_USES = len(PANELS) + 3 * len(DENSE_PANELS)
assert LAYER_USES % RING == 0 and 3 * len(MOE_PANELS) % MOE_RING == 0
ITEM_USES = 3 * len(MOE_PANELS) // MOE_RING


class Chain:

    def __init__(self, eng, sem):
        self.eng, self.sem, self.n = eng, sem, 0

    def mark(self, ins):
        self.n += 1
        ins.then_inc(self.sem, 1)

    def sync(self):
        self.eng.wait_ge(self.sem, self.n)

    def link(self, ins):
        self.mark(ins)
        self.sync()


def hybrid_trunk(nc, A, out):
    with ExitStack() as ctx:
        def sb(name, shape, dt=F32):
            return ctx.enter_context(nc.sbuf_tensor(name, shape, dt))

        x = sb("x", [P, NT, D])
        hT = sb("hT", [P, KD, NT * P])
        const = sb("const", [P, N_CONST])
        vec = sb("vec", [P, P])
        cols = sb("cols", [P, N_ROWS])
        w_dt = sb("w_dt", [P, KD, HEADS])
        heads_b = sb("heads_b", [P, 3, HEADS])
        gain_b = sb("gain_b", [P, 2, QK])
        small = sb("small", [P, 512])
        r_w = sb("r_w", [P, KD, EXPERTS])
        ones = sb("ones", [P, P])
        chosen = sb("chosen", [P, NT, EXPERTS])[:]
        item_tab = sb("item_tab", [1, ITEM_SLOTS + 1], I32)
        free = (nc.sbuf_bytes_remaining() if callable(nc.sbuf_bytes_remaining) else nc.sbuf_bytes_remaining) // 4 - 64
        arena = sb("arena", [P, free])
        ps = ctx.enter_context(nc.psum_tensor("ps", [P, 8, N], F32))

        def piece(at, *shape):
            n = 1
            for s in shape:
                n *= s
            assert at + n <= free, (at, n, free)
            v = arena[:, at:at + n]
            names = "abcd"[:len(shape)]
            if len(shape) > 1:
                v = v.rearrange(f"p ({' '.join(names)}) -> p {' '.join(names)}", **dict(zip(names, shape)))
            return v, at + n

        slots = [arena[:, s * SLOT:(s + 1) * SLOT] for s in range(MOE_RING)]
        at = RING * SLOT
        kT, _ = piece(at, HEADS, NT * P)
        xin, at = piece(at, 2, 2, NT * P + TAPS - 1)
        xc, at = piece(at, CONV_CHUNKS, NT * P)
        qT, _ = piece(at, HEADS, NT * P)
        xh, at = piece(at, NT, D)
        xs, at = piece(at, NT, D)
        z, z_end = piece(at, NT, D)
        tmp, _ = piece(at, HEADS * QK)
        at = z_end
        o, _ = piece(at, NT, D)
        q, at = piece(at, NT, HEADS * QK)
        k, at = piece(at, NT, HEADS * QK)
        v, at = piece(at, NT, HEADS, HD)
        prob, _ = piece(at, 2, N)
        probT, _ = piece(at + 2 * N, 2, N)
        lat, _ = piece(at, NT, LAT)
        sgu_wT, _ = piece(at, 8, P)
        mt, at = piece(at, 4, N)
        xn, _ = piece(at, NT, D)
        u, at = piece(at, NT, D)
        vs, at = piece(at, NT, D)
        sgu_raw, _ = piece(at, 8, P)
        cbm, _ = piece(at + 8 * P, 4, P)
        yT, at = piece(at, KD, NT * P)
        latT, _ = piece(at, 3, NT * P)
        b_tok, _ = piece(at + 3 * NT * P, 2, P)
        gate, at = piece(at, NT, N)
        prev, _ = piece(at, 2, N)
        xd, _ = piece(at + 2 * N, D)
        merged, at = piece(at, NT, D)
        at = MOE_RING * SLOT
        fn, at = piece(at, NT, D)
        sg, at = piece(at, 2, N)
        h, at = piece(at, 2, N)
        hid, at = piece(at, 2, 4, P)
        xg, at = piece(at, KD, P)
        ysb, at = piece(at, D)
        pick, at = piece(at, NT, P)
        wpick, at = piece(at, NT, P)
        wpickT, at = piece(at, NT, P)
        items, at = piece(at, 8, ITEM_SLOTS * EXPERTS)
        pos_item, at = piece(at, NT, ITEM_SLOTS)
        w_item, at = piece(at, NT, ITEM_SLOTS)
        route, at = piece(at, 12, NT, EXPERTS)

        s_at = [0]

        def tiny(n):
            s_at[0] += n
            assert s_at[0] <= 512
            return small[:, s_at[0] - n:s_at[0]]

        def by(ap, **kw):
            (n1, s1), = [(a, b) for a, b in kw.items()]
            return ap.rearrange(f"p (a {n1}) -> p a {n1}", **{n1: s1})

        ss = tiny(2)
        rs = tiny(2)
        dtr = by(tiny(32), h=HEADS)
        dte = by(tiny(32), h=HEADS)
        dtv = by(tiny(32), h=HEADS)
        adt = by(tiny(32), h=HEADS)
        aexp = tiny(16)
        csv = by(tiny(64), h=HEADS)
        expcs = tiny(16)
        decay = tiny(16)
        ssg = by(tiny(4), h=2)
        rsg = by(tiny(4), h=2)
        ssl = by(tiny(4), h=2)
        rsl = by(tiny(4), h=2)
        ssh = tiny(16)
        rsh = tiny(16)
        mx = tiny(4)
        nmx = by(tiny(8), h=4)
        rsum = by(tiny(32), h=HEADS)
        rinv = by(tiny(32), h=HEADS)
        bn = tiny(24).rearrange("p (a b c) -> p a b c", a=NT, b=2)
        mv = by(tiny(4), h=2)
        lrs = tiny(2)
        lss = tiny(2)

        def cst(name, n):
            return const[:, CONST[name]:CONST[name] + n]

        ident = cst("ident", P)
        tri = cst("tri", P)
        before = cst("before", P)
        slot_no = cst("slot", P)
        mask = cst("mask", 2 * P)
        cos = by(cst("cos", 2 * HALF_ROPE), h=HALF_ROPE)
        sin = by(cst("sin", 2 * HALF_ROPE), h=HALF_ROPE)

        def col(name, i, n=1):
            return cols[:, ROWS[name] + i:ROWS[name] + i + n]

        def spread(ap, n):
            return ap.unsqueeze(2).to_broadcast([ap.shape[0], ap.shape[1], n])

        def repeat(ap, n):
            return ap.unsqueeze(1).to_broadcast([ap.shape[0], n, ap.shape[1]])

        def sem(name):
            return ctx.enter_context(nc.semaphore(name))

        const_in = sem("const_in")
        setup_done = sem("setup_done")
        ring_full = [sem(f"ring_full{s}") for s in range(MOE_RING)]
        ring_used = [sem(f"ring_used{s}") for s in range(MOE_RING)]
        go = sem("go")
        begun = sem("begun")
        stored = sem("stored")
        fills_begun = sem("fills_begun")
        routed = sem("routed")

        first_cleared = sem("arrived")
        arrived = first_cleared
        numbers = [arrived.num]

        def local(name):
            s = sem(name)
            numbers.append(s.num)
            return s

        bank_full = local("bank_full")
        bank_free = [local(f"bank_free{b}") for b in range(8)]
        act_steps = local("act_steps")
        dve_steps = local("dve_steps")
        vec_in = local("vec_in")
        small_in = local("small_in")
        S = {name: local(name) for name in (
            "squared", "mean_made", "rooted", "normed", "conv_made", "silu_made", "dt_neg", "dt_log", "a_exp",
            "adt_made", "tail_made", "cs_exp", "xs_made", "xd_made", "decay_made", "mt_made", "y_made", "ysq_made",
            "ymean_made", "yroot_made", "y_normed", "latsq_made", "latmean_made", "latroot_made", "lat_normed",
            "kpe_made", "kv_copied", "gated", "hsq_made", "hmean_made", "hroot_made", "hnorm_made", "max_made",
            "prob_made", "o_made", "var_made", "vroot_made", "v_normed", "merged_made", "fsquared", "fmean_made",
            "frooted", "fnormed", "g_full", "u_full", "sg_made", "h_made", "t_full", "hid_made", "down_done",
            "picked", "gathered", "xg_made", "wpickT_full", "wpickT_made", "y_copied", "scattered",
            "logits", "chosen", "ranks", "gap_made", "gap_exp",
            "zeros_made")}
        assert numbers == list(range(numbers[0], numbers[0] + len(numbers)))
        cleared = range(numbers[0], numbers[-1] + 1)

        bank_uses = [len(JOBS[b::8]) for b in range(8)]

        def take(eng, name):
            eng.wait_ge(bank_full, JOB[name] + 1)
            return ps[:, JOB[name] % 8]

        def give(name, ins):
            ins.then_inc(bank_free[JOB[name] % 8], 1)

        def given(eng, name):
            eng.wait_ge(bank_free[JOB[name] % 8], JOB[name] // 8 + 1)

        def begin(eng, turn):
            eng.wait_ge(go, turn)
            eng.sem_inc(begun, 1)

        def rows(w):
            return w.rearrange("l (k p) n -> l p k n", p=P)

        W = {"in": rows(A["w_in"]), "uq": rows(A["w_uq"]), "ukv": rows(A["w_ukv"]), "ssd": rows(A["w_br_ssd"]),
             "sgu": rows(A["w_br_sgu"]), "mla": rows(A["w_br_mla"]), "out": rows(A["w_out"])}
        chunks_of = {"uq": 2, "ukv": 1}

        def slot_view(s, kchunks, width):
            return slots[s][:, 0:kchunks * width].rearrange("p (k n) -> p k n", k=kchunks)

        uses0 = [LAYER_USES // RING + len(range(s, len(PANELS), RING)) for s in range(RING)] + [0] * (MOE_RING - RING)

        block = ctx.enter_context(nc.Block())

        @block.sync
        def _(sp):
            sp.dma_start(const[:], A["const"]).then_inc(const_in, 16)
            sp.dma_start(r_w[:], A["router_w"][0].rearrange("(k p) e -> p k e", p=P)).then_inc(const_in, 16)
            sp.dma_start(x[:], A["x"][0].rearrange("(t p) d -> p t d", p=P)).then_inc(const_in, 16)

            with sp.Fori(0, DEPTH) as L:
                one = bass.ds(L, 1)

                def panel(use):
                    name, src, c, width = PANELS[use]
                    s, n = use % RING, use // RING
                    kc = chunks_of.get(src, KD)
                    sp.wait_ge(ring_used[s], L * (LAYER_USES // RING) + n + 1)
                    if c == 0:
                        sp.sem_inc(fills_begun, 1)
                    sp.dma_start(slot_view(s, kc, width),
                                 W[src][one, :, :, c:c + width].rearrange("a p k n -> p (a k) n")
                                 ).then_inc(ring_full[s], 16)

                for use in range(RING):
                    panel(use)
                sp.wait_ge(go, L + 1)
                for name, src, n in (("mix", "mix_norm_g", 8), ("ffn", "ffn_norm_g", 8), ("conv_b", "conv_b", 12),
                                     ("ssd", "ssd_norm_g", 8), ("q", "q_norm_g", 2), ("kv", "kv_norm_g", 1),
                                     ("ln_g", "sgu_ln_g", 8), ("ln_b", "sgu_ln_b", 8)):
                    sp.dma_start(vec[ROWS[name]:ROWS[name] + n, :],
                                 A[src][one, :].rearrange("a (r c) -> (a r) c", c=P)).then_inc(vec_in, 16)
                sp.dma_start(vec[ROWS["conv_w"]:ROWS["conv_w"] + 48, :],
                             A["conv_w"][one].rearrange("a k (r c) -> (a k r) c", c=P)).then_inc(vec_in, 16)
                sp.dma_start(vec[ROWS["sgu_b"]:ROWS["sgu_b"] + 8, :],
                             A["sgu_b"][one].rearrange("a r c -> (a r) c")).then_inc(vec_in, 16)
                for i, src in enumerate(("dt_bias", "a_log", "d_skip")):
                    sp.dma_start(heads_b[:, i, :], A[src][one, :].to_broadcast([P, HEADS])).then_inc(small_in, 16)
                for i, src in enumerate(("q_head_g", "k_head_g")):
                    sp.dma_start(gain_b[:, i, :], A[src][one, :].to_broadcast([P, QK])).then_inc(small_in, 16)
                with nc.allow_non_contiguous_dma(reason="sixteen columns of each row"):
                    sp.dma_start(w_dt[:], W["in"][one, :, :, C_DT:C_DT + HEADS].rearrange("a p k n -> p (a k) n")
                                 ).then_inc(small_in, 16)
                sp.dma_start(sgu_raw, A["sgu_w"][one].rearrange("a g t s -> t (a g) s")).then_inc(small_in, 16)
                for use in range(RING, len(PANELS)):
                    panel(use)
                with sp.If(L < 1):
                    for i, (c, width) in enumerate(DENSE_PANELS):
                        for j, (src, down) in enumerate((("ffn_w_gate", 0), ("ffn_w_up", 0), ("ffn_w_down", 1))):
                            use = len(PANELS) + 3 * i + j
                            s, n = use % RING, use // RING
                            sp.wait_ge(ring_used[s], n + 1)
                            if down:
                                dst = slots[s][:, 0:width // P * D].rearrange("p (k n) -> p k n", n=D)
                                w = A[src][0, c:c + width, :].rearrange("(k p) n -> p k n", p=P)
                            else:
                                dst = slot_view(s, KD, width)
                                w = A[src][0].rearrange("(k p) n -> p k n", p=P)[:, :, c:c + width]
                            sp.dma_start(dst, w).then_inc(ring_full[s], 16)

            up_w = [A[n][0].rearrange("e (k p) n -> e p k n", p=P) for n in ("moe_w_gate", "moe_w_up")]
            down_w = A["moe_w_down"][0].rearrange("e (k p) n -> e p k n", p=P)

            sp.wait_ge(routed, 1)
            sp.wait_ge(go, DEPTH + 1)
            n_items = sp.value_load(item_tab[0:1, ITEM_SLOTS:ITEM_SLOTS + 1], min_val=EXPERTS, max_val=MAX_ITEMS)
            with sp.Fori(0, n_items) as i:
                e = sp.value_load(item_tab[0:1, bass.ds(i, 1)], min_val=0, max_val=EXPERTS - 1)
                for p, (c, width) in enumerate(MOE_PANELS):
                    for j in range(3):
                        use = 3 * p + j
                        s, n = use % MOE_RING, use // MOE_RING
                        sp.wait_ge(ring_used[s], i * ITEM_USES + (uses0[s] + n + 1))
                        if j < 2:
                            dst = slot_view(s, KD, width)
                            w = up_w[j][bass.ds(e, 1), :, :, c:c + width]
                        else:
                            dst = slots[s].rearrange("p (k n) -> p k n", n=D)
                            w = down_w[bass.ds(e, 1), :, c // P:c // P + 4, :]
                        sp.dma_start(dst, w.rearrange("a p k n -> p (a k) n")).then_inc(ring_full[s], 16)
            sp.wait_ge(go, n_items + (DEPTH + 2))
            sp.dma_start(out[0].rearrange("(t p) d -> p t d", p=P), x[:]).then_inc(stored, 16)
            sp.wait_ge(stored, 16)

        @block.gpsimd
        def _(pool):
            pool.memset(vec[:], 0.0).then_inc(setup_done, 1)
            pool.memset(xin[:, :, :, 0:TAPS - 1], 0.0).then_inc(setup_done, 1)
            pool.memset(ones[:], 1.0).then_inc(setup_done, 1)
            pool.memset(small[:], 0.0).then_inc(setup_done, 1)
            pool.wait_ge(setup_done, 4)
            for s in range(MOE_RING):
                pool.sem_inc(ring_used[s], 1)
            pool.sem_inc(go, 1)
            with pool.Fori(0, DEPTH):
                pool.wait_ge(arrived, 3)
                pool.memset(xin[:, :, :, 0:TAPS - 1], 0.0).then_inc(S["zeros_made"], 1)
                pool.wait_ge(S["zeros_made"], 1)
                pool.sem_clear(cleared)
                pool.sem_inc(go, 1)
            pool.wait_ge(arrived, 3)
            n_items = pool.value_load(item_tab[0:1, ITEM_SLOTS:ITEM_SLOTS + 1], min_val=EXPERTS, max_val=MAX_ITEMS)
            pool.sem_clear(cleared)
            pool.sem_inc(go, 1)
            with pool.Fori(0, n_items):
                pool.wait_ge(arrived, 3)
                pool.sem_clear(cleared)
                pool.sem_inc(go, 1)

        @block.tensor
        def _(pe):
            turn = [0]
            unreleased = []

            def bank(name):
                i = turn[0]
                assert JOBS[i] == name, (JOBS[i], name)
                turn[0] += 1
                if i >= 8:
                    pe.wait_ge(bank_free[i % 8], i // 8)
                return ps[:, i % 8]

            def done(ins):
                ins.then_inc(bank_full, 1)

            def release():
                while unreleased:
                    s, signal, n = unreleased.pop(0)
                    pe.wait_ge(signal, n)
                    pe.sem_inc(ring_used[s], 1)

            def turn_over(name, parts):
                b = bank(name)
                at = 0
                for a in parts:
                    n, m = a.shape[0], a.shape[1]
                    last = pe.transpose(b[0:m, at:at + n], a, ident[0:n, 0:n])
                    at += n
                done(last)

            def htile(kk, t):
                return hT[:, kk, t * P:(t + 1) * P]

            def ytile(kk, t):
                return yT[:, kk, t * P:(t + 1) * P]

            def ffn(units, filled, lhs, acc):
                last_of = {p: t for p, t, _ in units}

                def up(i, which):
                    p, t, width = units[i]
                    s, w = filled(p, which, width, t == 0)
                    for kk in range(KD):
                        last = pe.matmul(ps[:, 2 * (i % 2) + which, 0:width], lhs(kk, t), w[:, kk, :],
                                         start=(kk == 0), stop=(kk == KD - 1))
                    signal = S["u_full" if which else "g_full"]
                    last.then_inc(signal, 1)
                    if last_of[p] == t:
                        unreleased.append((s, signal, i + 1))

                def turn_hidden(i):
                    width = units[i][2]
                    pe.wait_ge(S["h_made"], i + 1)
                    for j in range(width // P):
                        last = pe.transpose(ps[:, 2 * (i % 2), j * P:(j + 1) * P], h[:, i % 2, j * P:(j + 1) * P], ident)
                    last.then_inc(S["t_full"], 1)

                def down(i):
                    p, t, width = units[i]
                    s, w = filled(p, 2, width, t == 0)
                    pe.wait_ge(S["hid_made"], i + 1)
                    for half in range(2):
                        for j in range(width // P):
                            last = pe.matmul(acc(t, half), hid[:, i % 2, j, :], w[:, j, half * N:(half + 1) * N],
                                             start=(p == 0 and j == 0), stop=(p == units[-1][0] and j == width // P - 1))
                    last.then_inc(S["down_done"], 1)
                    if last_of[p] == t:
                        unreleased.append((s, S["down_done"], i + 1))

                for i in range(len(units)):
                    if i >= 2:
                        pe.wait_ge(S["hid_made"], i - 1)
                    up(i, 0)
                    if i:
                        turn_hidden(i - 1)
                    up(i, 1)
                    release()
                    if i:
                        down(i - 1)
                turn_hidden(len(units) - 1)
                down(len(units) - 1)
                release()

            pe.wait_ge(const_in, 48)
            pe.wait_ge(setup_done, 4)

            with pe.Fori(0, DEPTH) as L:
                turn[0] = 0
                use = [0]

                def panel(name):
                    assert PANELS[use[0]][0] == name, (PANELS[use[0]], name)
                    s, n = use[0] % RING, use[0] // RING
                    src, width = PANELS[use[0]][1], PANELS[use[0]][3]
                    use[0] += 1
                    pe.wait_ge(ring_full[s], L * (16 * (LAYER_USES // RING)) + 16 * (n + 1))
                    return s, slot_view(s, chunks_of.get(src, KD), width), width

                def project(name, lhs):
                    s, w, width = panel(name)
                    for t in range(NT):
                        b = bank(f"{name}{t}")
                        for kk in range(KD):
                            last = pe.matmul(b[:, 0:width], lhs(kk, t), w[:, kk, :], start=(kk == 0), stop=(kk == KD - 1))
                        done(last)
                        if t == 0:
                            release()
                    unreleased.append((s, bank_full, turn[0]))

                def close_part(br, i, y, ready):
                    if i == 1:
                        for t in range(NT):
                            ready(t)
                            for hh in range(2):
                                turn_over(f"yT_{br}{t}{hh}",
                                          [y[:, t, c * P:(c + 1) * P] for c in range(4 * hh, 4 * hh + 4)])
                        return
                    what, n = (("gate", 0), None, ("br", 0), ("gate", 1), ("br", 1))[i]
                    if i == 2:
                        for t in range(NT):
                            for hh in range(2):
                                given(pe, f"yT_{br}{t}{hh}")
                    project(f"{what}_{br}{n}", htile if what == "gate" else ytile)

                begin(pe, L + 1)
                pe.wait_ge(vec_in, 160)
                done(pe.transpose(bank("vec")[:, 0:P], vec[:, :], ident))
                for t in range(NT):
                    pe.wait_ge(S["normed"], t + 1)
                    for hh in range(2):
                        turn_over(f"ht{t}{hh}", [xn[:, t, c * P:(c + 1) * P] for c in range(4 * hh, 4 * hh + 4)])
                for t in range(NT):
                    for hh in range(2):
                        given(pe, f"ht{t}{hh}")
                for n in range(3):
                    s, w, _ = panel(f"xbc{n}")
                    for i in range(2):
                        b = bank(f"xbc{2 * n + i}")
                        for j in range(2):
                            c = (2 * i + j) * P
                            for kk in range(KD):
                                last = pe.matmul(b[:, j * NT * P:(j + 1) * NT * P], w[:, kk, c:c + P], hT[:, kk, :],
                                                 start=(kk == 0), stop=(kk == KD - 1))
                        done(last)
                        release()
                    unreleased.append((s, bank_full, turn[0]))
                pe.wait_ge(small_in, 112)
                b = bank("dt")
                for t in range(NT):
                    for kk in range(KD):
                        last = pe.matmul(b[:, t * HEADS:(t + 1) * HEADS], htile(kk, t), w_dt[:, kk, :],
                                         start=(kk == 0), stop=(kk == KD - 1))
                done(last)
                project("lat", htile)
                project("z0", htile)
                project("z1", htile)
                pe.wait_ge(S["adt_made"], 1)
                b = bank("cs")
                for c in range(NT):
                    pe.matmul(b[:, c * HEADS:(c + 1) * HEADS], tri, adt[:, c, :], start=True, stop=True)
                for c in range(NT):
                    last = pe.matmul(b[:, (2 + c) * HEADS:(3 + c) * HEADS], ones[:], adt[:, c, :],
                                     start=True, stop=True)
                done(last)
                pe.wait_ge(S["silu_made"], 6)
                for t in range(NT):
                    for hh in range(2):
                        turn_over(f"xt{t}{hh}", [xc[:, c, t * P:(t + 1) * P] for c in range(4 * hh, 4 * hh + 4)])
                turn_over("bt", [xc[:, 8 + g, 0:P] for g in range(2)])
                b = bank("cb")
                for c in range(NT):
                    for g in range(2):
                        at = (2 * c + g) * P
                        last = pe.matmul(b[:, at:at + P], xc[:, 8 + g, c * P:(c + 1) * P],
                                         xc[:, 10 + g, c * P:(c + 1) * P], start=True, stop=True)
                done(last)
                for t in range(NT):
                    pe.wait_ge(S["lat_normed"], t + 1)
                    turn_over(f"latT{t}", [lat[:, t, c * P:(c + 1) * P] for c in range(3)])
                s, w, _ = panel("uq")
                for t in range(NT):
                    given(pe, f"latT{t}")
                    for n in range(3):
                        b = bank(f"q{t}{n}")
                        for kk in range(2):
                            last = pe.matmul(b[:], latT[:, kk, t * P:(t + 1) * P], w[:, kk, n * N:(n + 1) * N],
                                             start=(kk == 0), stop=(kk == 1))
                        done(last)
                        release()
                unreleased.append((s, bank_full, turn[0]))
                s, w, _ = panel("ukv")
                for t in range(NT):
                    for n in range(4):
                        b = bank(f"kv{t}{n}")
                        done(pe.matmul(b[:], latT[:, 2, t * P:(t + 1) * P], w[:, 0, n * N:(n + 1) * N],
                                       start=True, stop=True))
                        release()
                unreleased.append((s, bank_full, turn[0]))
                project("u0", htile)
                project("u1", htile)
                pe.wait_ge(S["xd_made"], 1)
                given(pe, "bt")
                for g in range(2):
                    done(pe.matmul(bank(f"st{g}")[:], b_tok[:, g, :], xd[:, g * N:(g + 1) * N], start=True, stop=True))
                for g in range(2):
                    given(pe, f"st{g}")
                    done(pe.matmul(bank(f"yo{g}")[:], xc[:, 10 + g, P:2 * P], prev[:, g, :], start=True, stop=True))
                for c in range(NT):
                    for qd in range(4):
                        b = bank(f"rb{c}{qd}")
                        for i in range(4):
                            hh = 4 * qd + i
                            last = pe.matmul(b[:, i * P:(i + 1) * P], adt[:, c, hh:hh + 1].to_broadcast([P, P]), tri,
                                             start=True, stop=True)
                        done(last)
                    project(f"v{c}", htile)
                    pe.wait_ge(S["xs_made"], c + 1)
                    for g in range(2):
                        pe.wait_ge(S["mt_made"], 4 * c + 2 * g + 2)
                        b = bank(f"yd{c}{g}")
                        for i in range(8):
                            hh = 8 * g + i
                            last = pe.matmul(b[:, i * HD:(i + 1) * HD], mt[:, hh // 4, (hh % 4) * P:(hh % 4 + 1) * P],
                                             xs[:, c, hh * HD:(hh + 1) * HD], start=True, stop=True)
                        done(last)
                for i in range(2):
                    turn_over(f"wt{i}", [sgu_raw[:, g, :] for g in range(4 * i, 4 * i + 4)])
                for what, row in (("lng", "ln_g"), ("lnb", "ln_b")):
                    for hh in range(2):
                        b = bank(f"{what}{hh}")
                        for i in range(4):
                            r = ROWS[row] + 4 * hh + i
                            last = pe.matmul(b[:, i * P:(i + 1) * P], ident[:, r:r + 1].to_broadcast([P, P]), vec[:, :],
                                             start=True, stop=True)
                        done(last)
                for i in range(5):
                    close_part("ssd", i, xh, lambda t: pe.wait_ge(S["y_normed"], t + 1))
                for w_no, (name, src) in enumerate((("qT", q), ("kT", k))):
                    for t in range(NT):
                        pe.wait_ge(S["hnorm_made"], 2 * w_no + t + 1)
                        for i in range(4):
                            turn_over(f"{name}{t}{i}",
                                      [src[:, t, hh * QK:(hh + 1) * QK] for hh in range(4 * i, 4 * i + 4)])
                given(pe, "wt0")
                given(pe, "wt1")
                for t in range(NT):
                    pe.wait_ge(S["v_normed"], t + 1)
                    for hh in range(2):
                        b = bank(f"mx{t}{hh}")
                        for i in range(4):
                            g = 4 * hh + i
                            last = pe.matmul(b[:, i * P:(i + 1) * P], sgu_wT[:, g, :], vs[:, t, g * P:(g + 1) * P],
                                             start=True, stop=True)
                        done(last)
                for name in [f"{w}T{t}{i}" for w in "qk" for t in range(NT) for i in range(4)]:
                    given(pe, name)
                for kind, i in attention_order():
                    if kind == "close":
                        close_part("sgu", i, u, lambda t: (given(pe, f"mx{t}0"), given(pe, f"mx{t}1")))
                        continue
                    t, h0, nh = GROUPS[i]
                    blocks = t + 1
                    b = bank(f"{kind}{i}")
                    if kind == "sc":
                        keys = blocks * P
                        for j in range(nh):
                            last = pe.matmul(b[:, j * keys:(j + 1) * keys], qT[0:QK, h0 + j, t * P:(t + 1) * P],
                                             kT[0:QK, h0 + j, 0:keys], start=True, stop=True)
                    elif kind == "pt":
                        pe.wait_ge(S["prob_made"], i + 1)
                        for j in range(4):
                            last = pe.transpose(b[:, j * P:(j + 1) * P], prob[:, i % 2, j * P:(j + 1) * P], ident)
                    else:
                        given(pe, f"pt{i}")
                        for j in range(nh):
                            for kb in range(blocks):
                                at = (j * blocks + kb) * P
                                last = pe.matmul(b[:, j * HD:(j + 1) * HD], probT[:, i % 2, at:at + P],
                                                 v[:, kb, h0 + j, :], start=(kb == 0), stop=(kb == blocks - 1))
                    done(last)
                for i in range(5):
                    close_part("mla", i, o, lambda t: pe.wait_ge(S["o_made"], (4, 12)[t]))
                pe.wait_ge(S["merged_made"], 8)
                for t in range(NT):
                    for hh in range(2):
                        turn_over(f"mT{t}{hh}", [merged[:, t, c * P:(c + 1) * P] for c in range(4 * hh, 4 * hh + 4)])
                for t in range(NT):
                    for hh in range(2):
                        given(pe, f"mT{t}{hh}")
                project("out0", ytile)
                project("out1", ytile)
                release()
                for t in range(NT):
                    pe.wait_ge(S["fnormed"], t + 1)
                    for hh in range(2):
                        turn_over(f"ft{t}{hh}", [fn[:, t, c * P:(c + 1) * P] for c in range(4 * hh, 4 * hh + 4)])
                for b in range(8):
                    pe.wait_ge(bank_free[b], bank_uses[b])
                with pe.If(L < 1):
                    def filled(p, which, width, first):
                        n_use = len(PANELS) + 3 * p + which
                        s = n_use % RING
                        if first:
                            pe.wait_ge(ring_full[s], 16 * (n_use // RING + 1))
                        if which == 2:
                            return s, slots[s][:, 0:width // P * D].rearrange("p (k n) -> p k n", n=D)
                        return s, slot_view(s, KD, width)

                    ffn(DENSE_UNITS, filled, htile, lambda t, half: ps[:, 4 + 2 * t + half])
                pe.wait_ge(bank_full, len(JOBS))
                pe.sem_inc(arrived, 1)

            begin(pe, DEPTH + 1)
            for t in range(NT):
                for kk in range(KD):
                    last = pe.matmul(ps[:, 0, t * EXPERTS:(t + 1) * EXPERTS], htile(kk, t), r_w[:, kk, :],
                                     start=(kk == 0), stop=(kk == KD - 1))
            last.then_inc(S["logits"], 1)
            pe.wait_ge(S["chosen"], 1)
            E8 = EXPERTS
            pe.matmul(ps[:, 1, 0:E8], before, chosen[:, 0, :], start=True, stop=True)
            pe.matmul(ps[:, 1, E8:2 * E8], before, chosen[:, 1, :], start=True, stop=False)
            pe.matmul(ps[:, 1, E8:2 * E8], ones[:], chosen[:, 0, :], start=False, stop=True)
            pe.matmul(ps[:, 1, 2 * E8:3 * E8], ones[:], chosen[:, 0, :], start=True, stop=False)
            pe.matmul(ps[:, 1, 2 * E8:3 * E8], ones[:], chosen[:, 1, :], start=False, stop=True
                      ).then_inc(S["ranks"], 1)
            pe.wait_ge(S["ranks"], 1)
            pe.sem_inc(arrived, 1)

            pe.wait_ge(routed, 1)
            n_items = pe.value_load(item_tab[0:1, ITEM_SLOTS:ITEM_SLOTS + 1], min_val=EXPERTS, max_val=MAX_ITEMS)
            with pe.Fori(0, n_items) as item:
                begin(pe, item + (DEPTH + 2))
                pe.wait_ge(S["picked"], 1)
                for c in range(KD):
                    for t in range(NT):
                        last = pe.matmul(ps[:, 6 + c // 4, c % 4 * P:(c % 4 + 1) * P], fn[:, t, c * P:(c + 1) * P],
                                         pick[:, t, :], start=(t == 0), stop=(t == NT - 1))
                    if c % 4 == 3:
                        last.then_inc(S["gathered"], 1)
                pe.wait_ge(S["picked"], 2)
                for t in range(NT):
                    last = pe.transpose(ps[:, 3, t * P:(t + 1) * P], wpick[:, t, :], ident)
                last.then_inc(S["wpickT_full"], 1)
                pe.wait_ge(S["xg_made"], 2)
                pe.wait_ge(S["wpickT_made"], 1)

                def filled(p, which, width, first):
                    n_use = 3 * p + which
                    s = n_use % MOE_RING
                    pe.wait_ge(ring_full[s], item * (16 * ITEM_USES) + 16 * (uses0[s] + n_use // MOE_RING + 1))
                    if which == 2:
                        return s, slots[s].rearrange("p (k n) -> p k n", n=D)
                    return s, slot_view(s, KD, width)

                ffn([(p, 0, width) for p, (c, width) in enumerate(MOE_PANELS)], filled, lambda kk, t: xg[:, kk, :],
                    lambda t, half: ps[:, 4 + half])
                pe.wait_ge(S["y_copied"], 2)
                for j in range(4):
                    t, half = j // 2, j % 2
                    pe.matmul(ps[:, (6, 7, 0, 1)[j]], wpickT[:, t, :], ysb[:, half * N:(half + 1) * N],
                              start=True, stop=True).then_inc(S["scattered"], 1)
                pe.wait_ge(S["scattered"], 4)
                pe.sem_inc(arrived, 1)

        @block.scalar
        def _(act):
            def copy_out(name, out_ap, in_ap):
                give(name, act.activation(out_ap, in_ap, ACT.Copy))

            def ffn(n_units, width_of):
                for i in range(n_units):
                    width = width_of(i)
                    act.wait_ge(S["g_full"], i + 1)
                    if i >= 2:
                        act.wait_ge(S["h_made"], i - 1)
                    act.activation(sg[:, i % 2, 0:width], ps[:, 2 * (i % 2), 0:width], ACT.Silu).then_inc(S["sg_made"], 1)
                    if i:
                        hidden(i - 1, width_of(i - 1))
                hidden(n_units - 1, width_of(n_units - 1))

            def hidden(i, width):
                act.wait_ge(S["t_full"], i + 1)
                if i >= 2:
                    act.wait_ge(S["down_done"], i - 1)
                act.activation(hid[:, i % 2, 0:width // P, :], by(ps[:, 2 * (i % 2), 0:width], h=P), ACT.Copy
                               ).then_inc(S["hid_made"], 1)

            act.wait_ge(const_in, 48)
            act.wait_ge(setup_done, 4)
            with act.Fori(0, DEPTH) as L:
                begin(act, L + 1)
                for t in range(NT):
                    act.activation(vs[:, t, :], x[:, t, :], ACT.Square, accum_out=ss[:, t:t + 1]).then_inc(S["squared"], 1)
                act.wait_ge(S["mean_made"], 1)
                act.activation(rs[:], ss[:], ACT.Sqrt).then_inc(S["rooted"], 1)
                for i in range(7):
                    if i < 6:
                        b = take(act, f"xbc{i}")
                        if i >= 2:
                            act.wait_ge(S["conv_made"], i - 1)
                        copy_out(f"xbc{i}", xin[:, i % 2, :, TAPS - 1:], by(b, h=NT * P))
                    if i:
                        act.wait_ge(S["conv_made"], i)
                        piece_ = xc[:, 2 * i - 2:2 * i, :]
                        act.activation(piece_, piece_, ACT.Silu).then_inc(S["silu_made"], 1)
                act.wait_ge(small_in, 112)
                act.activation(aexp, heads_b[:, 1, :], ACT.Exp).then_inc(S["a_exp"], 1)
                act.wait_ge(S["dt_neg"], 1)
                act.activation(dte, dtv, ACT.Exp).then_inc(act_steps, 1)
                act.wait_ge(act_steps, 1)
                act.activation(dte, dte, ACT.Ln, bias=1.0).then_inc(S["dt_log"], 1)
                for t in range(NT):
                    b = take(act, f"lat{t}")
                    copy_out(f"lat{t}", lat[:, t, :], b[:, 0:LAT])
                for t in range(NT):
                    given(act, f"lat{t}")
                    act.activation(vs[:, t, 0:256], lat[:, t, 0:256], ACT.Square, accum_out=ssl[:, t, 0:1])
                    act.activation(vs[:, t, 256:384], lat[:, t, 256:384], ACT.Square, accum_out=ssl[:, t, 1:2]
                                   ).then_inc(S["latsq_made"], 1)
                act.wait_ge(S["latmean_made"], 1)
                act.activation(rsl, ssl, ACT.Sqrt).then_inc(S["latroot_made"], 1)
                for n in range(2):
                    for t in range(NT):
                        b = take(act, f"z{n}{t}")
                        give(f"z{n}{t}", act.activation(z[:, t, n * N:(n + 1) * N], b, ACT.Silu))
                given(act, "z11")
                act.wait_ge(bank_free[JOB["cs"] % 8], JOB["cs"] // 8 + 1)
                act.activation(expcs, csv[:, 1, :], ACT.Exp).then_inc(S["cs_exp"], 1)
                act.wait_ge(S["tail_made"], 1)
                act.activation(decay, decay, ACT.Exp).then_inc(S["cs_exp"], 1)
                for t in range(NT):
                    for hh in range(2):
                        b = take(act, f"xt{t}{hh}")
                        copy_out(f"xt{t}{hh}", xh[:, t, hh * N:(hh + 1) * N], b)
                for t in range(NT):
                    for n in range(3):
                        b = take(act, f"q{t}{n}")
                        copy_out(f"q{t}{n}", q[:, t, n * N:(n + 1) * N], b)
                for t in range(NT):
                    for n in range(4):
                        b = by(take(act, f"kv{t}{n}"), h=2 * HD)
                        act.activation(by(k[:, t, :], h=QK)[:, 4 * n:4 * n + 4, 0:NOPE], b[:, :, 0:NOPE], ACT.Copy
                                       ).then_inc(S["kv_copied"], 1)
                        copy_out(f"kv{t}{n}", v[:, t, 4 * n:4 * n + 4, :], b[:, :, NOPE:])
                for n in range(2):
                    for t in range(NT):
                        b = take(act, f"u{n}{t}")
                        give(f"u{n}{t}", act.activation(u[:, t, n * N:(n + 1) * N], b, ACT.Gelu))
                for g in range(2):
                    b = take(act, f"st{g}")
                    copy_out(f"st{g}", prev[:, g, :], b)
                for c in range(NT):
                    for qd in range(4):
                        given(act, f"rb{c}{qd}")
                        act.activation(mt[:, qd, :], mt[:, qd, :], ACT.Exp).then_inc(S["decay_made"], 1)
                    for t in range(NT):
                        b = take(act, f"v{c}{t}")
                        give(f"v{c}{t}", act.activation(vs[:, t, c * N:(c + 1) * N], b, ACT.Gelu))
                for t in range(NT):
                    act.wait_ge(S["y_made"], 2 * t + 2)
                    for g in range(2):
                        act.activation(xs[:, t, g * N:(g + 1) * N], xh[:, t, g * N:(g + 1) * N], ACT.Square,
                                       accum_out=ssg[:, t, g:g + 1]).then_inc(S["ysq_made"], 1)
                act.wait_ge(S["ymean_made"], 1)
                act.activation(rsg, ssg, ACT.Sqrt).then_inc(S["yroot_made"], 1)
                act.wait_ge(S["var_made"], 1)
                act.activation(lrs, lss, ACT.Sqrt).then_inc(S["vroot_made"], 1)

                gates = [0]

                def gate_panel(br, n):
                    if gates[0]:
                        act.wait_ge(S["gated"], 2 * gates[0])
                    gates[0] += 1
                    for t in range(NT):
                        b = take(act, f"gate_{br}{n}{t}")
                        give(f"gate_{br}{n}{t}", act.activation(gate[:, t, :], b, ACT.Sigmoid))

                def head_squares(i):
                    src, t = (q, k)[i // 2], i % 2
                    if i == 0:
                        for tt in range(NT):
                            given(act, f"q{tt}2")
                    if i == 2:
                        act.wait_ge(S["kv_copied"], 8)
                        act.wait_ge(S["kpe_made"], 2)
                    if i:
                        act.wait_ge(S["hnorm_made"], i)
                    act.activation(tmp, src[:, t, :], ACT.Square).then_inc(S["hsq_made"], 1)
                    act.wait_ge(S["hmean_made"], i + 1)
                    act.activation(rsh, ssh, ACT.Sqrt).then_inc(S["hroot_made"], 1)

                gate_panel("ssd", 0)
                head_squares(0)
                head_squares(1)
                gate_panel("ssd", 1)
                head_squares(2)
                head_squares(3)
                for name, dst in (("qT", qT), ("kT", kT)):
                    for t in range(NT):
                        for i in range(4):
                            b = take(act, f"{name}{t}{i}")
                            copy_out(f"{name}{t}{i}", dst[0:QK, 4 * i:4 * i + 4, t * P:(t + 1) * P], by(b[0:QK, :], h=P))

                def turned(br):
                    for t in range(NT):
                        for hh in range(2):
                            b = take(act, f"yT_{br}{t}{hh}")
                            copy_out(f"yT_{br}{t}{hh}", yT[:, 4 * hh:4 * hh + 4, t * P:(t + 1) * P], by(b, h=P))

                for kind, i in attention_order():
                    if kind == "sc":
                        t, h0, nh = GROUPS[i]
                        keys = (t + 1) * P
                        act.wait_ge(S["max_made"], i + 1)
                        for j in range(nh):
                            p_ = prob[:, i % 2, j * keys:(j + 1) * keys]
                            e_ = act.activation(p_, p_, ACT.Exp, bias=nmx[:, i % 2, j:j + 1], scale=SCALE,
                                                accum_out=rsum[:, t, h0 + j:h0 + j + 1])
                        e_.then_inc(S["prob_made"], 1)
                    elif kind == "pt":
                        b = take(act, f"pt{i}")
                        if i >= 2:
                            act.wait_ge(bank_full, JOB[f"o{i - 2}"] + 1)
                        copy_out(f"pt{i}", probT[:, i % 2, :], b)
                    elif kind == "close":
                        if i == 1:
                            turned("sgu")
                        elif i in (0, 3):
                            gate_panel("sgu", i // 3)
                gate_panel("mla", 0)
                turned("mla")
                gate_panel("mla", 1)
                for t in range(NT):
                    for hh in range(2):
                        b = take(act, f"mT{t}{hh}")
                        copy_out(f"mT{t}{hh}", yT[:, 4 * hh:4 * hh + 4, t * P:(t + 1) * P], by(b, h=P))
                for t in range(NT):
                    given(act, f"out0{t}")
                    given(act, f"out1{t}")
                    act.activation(fn[:, t, :], x[:, t, :], ACT.Square, accum_out=ss[:, t:t + 1]
                                   ).then_inc(S["fsquared"], 1)
                act.wait_ge(S["fmean_made"], 1)
                act.activation(rs[:], ss[:], ACT.Sqrt).then_inc(S["frooted"], 1)
                with act.If(L < 1):
                    ffn(len(DENSE_UNITS), lambda i: DENSE_UNITS[i][2])
                act.activation(small[:, 511:512], small[:, 511:512], ACT.Copy).then_inc(act_steps, 1)
                act.wait_ge(act_steps, 2)
                act.sem_inc(arrived, 1)

            begin(act, DEPTH + 1)
            act.wait_ge(S["gap_made"], 1)
            act.activation(route[:, 4, :, 0:1], route[:, 3, :, 0:1], ACT.Exp).then_inc(S["gap_exp"], 1)
            act.wait_ge(S["gap_exp"], 1)
            act.sem_inc(arrived, 1)
            act.wait_ge(routed, 1)
            n_items = act.value_load(item_tab[0:1, ITEM_SLOTS:ITEM_SLOTS + 1], min_val=EXPERTS, max_val=MAX_ITEMS)
            with act.Fori(0, n_items) as item:
                begin(act, item + (DEPTH + 2))
                act.wait_ge(S["wpickT_full"], 1)
                act.activation(wpickT, by(ps[:, 3, 0:NT * P], h=P), ACT.Copy).then_inc(S["wpickT_made"], 1)
                ffn(len(MOE_PANELS), lambda i: N)
                act.wait_ge(S["down_done"], len(MOE_PANELS))
                act.activation(ysb[:, 0:N], ps[:, 4], ACT.Copy).then_inc(S["y_copied"], 1)
                act.wait_ge(S["y_copied"], 2)
                act.sem_inc(arrived, 1)

        @block.vector
        def _(dve):
            chain = Chain(dve, dve_steps)
            mark, link, sync = chain.mark, chain.link, chain.sync

            def ffn(n_units, width_of):
                for i in range(n_units):
                    width = width_of(i)
                    dve.wait_ge(S["sg_made"], i + 1)
                    dve.wait_ge(S["u_full"], i + 1)
                    if i >= 2:
                        dve.wait_ge(S["t_full"], i - 1)
                    dve.tensor_tensor(h[:, i % 2, 0:width], ps[:, 2 * (i % 2) + 1, 0:width], sg[:, i % 2, 0:width],
                                      ALU.mult).then_inc(S["h_made"], 1)

            def root_mean(sums, n, eps, signal):
                dve.tensor_scalar(sums, sums, 1.0 / n, eps, ALU.mult, ALU.add).then_inc(signal, 1)

            dve.wait_ge(const_in, 48)
            dve.wait_ge(setup_done, 4)
            with dve.Fori(0, DEPTH) as L:
                chain.n = 0
                begin(dve, L + 1)
                b = take(dve, "vec")
                give("vec", dve.tensor_copy(cols[:], b[:, 0:N_ROWS]))
                dve.wait_ge(S["squared"], 2)
                root_mean(ss[:], D, EPS, S["mean_made"])
                dve.wait_ge(S["rooted"], 1)
                link(dve.reciprocal(rs[:], rs[:]))
                for t in range(NT):
                    dve.tensor_scalar(xn[:, t, :], x[:, t, :], rs[:, t:t + 1], None, ALU.mult).then_inc(S["normed"], 1)
                given(dve, "vec")
                for t in range(NT):
                    for hh in range(2):
                        b = take(dve, f"ht{t}{hh}")
                        give(f"ht{t}{hh}", dve.tensor_tensor(hT[:, 4 * hh:4 * hh + 4, t * P:(t + 1) * P], by(b, h=P),
                                                             spread(col("mix", 4 * hh, 4), P), ALU.mult))
                for i in range(6):
                    given(dve, f"xbc{i}")
                    for tap in range(TAPS):
                        for j in range(2):
                            c = 2 * i + j
                            src = xin[:, i % 2, j, tap:tap + NT * P]
                            w = col("conv_w", tap * CONV_CHUNKS + c)
                            if tap == 0:
                                mark(dve.tensor_scalar(xc[:, c, :], src, w, col("conv_b", c), ALU.mult, ALU.add))
                            else:
                                ins = dve.scalar_tensor_tensor(xc[:, c, :], src, w, xc[:, c, :], ALU.mult, ALU.add)
                                if tap == TAPS - 1 and j == 1:
                                    ins.then_inc(S["conv_made"], 1)
                                else:
                                    mark(ins)
                        if tap < TAPS - 1:
                            sync()
                dve.wait_ge(small_in, 112)
                b = take(dve, "dt")
                give("dt", dve.tensor_tensor(dtr, by(b[:, 0:NT * HEADS], h=HEADS), repeat(heads_b[:, 0, :], NT), ALU.add))
                given(dve, "dt")
                dve.scalar_tensor_tensor(dtv, dtr, -1.0, dtr, ALU.mult, ALU.min).then_inc(S["dt_neg"], 1)
                dve.wait_ge(S["dt_neg"], 1)
                dve.wait_ge(S["dt_log"], 1)
                link(dve.scalar_tensor_tensor(dtr, dtr, 0.0, dte, ALU.max, ALU.add))
                dve.wait_ge(S["a_exp"], 1)
                dve.scalar_tensor_tensor(adt, dtr, -1.0, repeat(aexp, NT), ALU.mult, ALU.mult).then_inc(S["adt_made"], 1)
                dve.wait_ge(S["latsq_made"], 2)
                link(dve.tensor_scalar(ssl[:, :, 0:1], ssl[:, :, 0:1], 1.0 / 256, EPS, ALU.mult, ALU.add))
                root_mean(ssl[:, :, 1:2], P, EPS, S["latmean_made"])
                dve.wait_ge(S["latroot_made"], 1)
                link(dve.reciprocal(rsl, rsl))
                for t in range(NT):
                    mark(dve.tensor_scalar(lat[:, t, 0:256], lat[:, t, 0:256], rsl[:, t, 0:1], None, ALU.mult))
                    dve.tensor_scalar(lat[:, t, 256:384], lat[:, t, 256:384], rsl[:, t, 1:2], None, ALU.mult
                                      ).then_inc(S["lat_normed"], 1)
                    dve.tensor_copy(by(k[:, t, :], h=QK)[:, :, NOPE:], repeat(lat[:, t, 384:LAT], HEADS)
                                    ).then_inc(S["kpe_made"], 1)
                b = take(dve, "cs")
                give("cs", dve.tensor_copy(csv, by(b[:, 0:4 * HEADS], h=HEADS)))
                given(dve, "cs")
                dve.tensor_tensor(decay, csv[:, 2, :], csv[:, 0, :], ALU.subtract).then_inc(S["tail_made"], 1)
                for t in range(NT):
                    given(dve, f"xt{t}0")
                    given(dve, f"xt{t}1")
                    dve.tensor_tensor(by(xs[:, t, :], h=HD), by(xh[:, t, :], h=HD), spread(dtr[:, t, :], HD), ALU.mult
                                      ).then_inc(S["xs_made"], 1)
                b = take(dve, "bt")
                give("bt", dve.tensor_copy(b_tok, by(b[:, 0:2 * P], h=P)))
                b = take(dve, "cb")
                give("cb", dve.tensor_tensor(cbm, by(b, h=P), repeat(tri, 4), ALU.mult))
                for t in range(NT):
                    b = take(dve, f"latT{t}")
                    give(f"latT{t}", dve.tensor_tensor(latT[:, :, t * P:(t + 1) * P], by(b[:, 0:3 * P], h=P),
                                                       spread(col("q", 0, 3), P), ALU.mult))
                dve.wait_ge(S["cs_exp"], 2)
                dve.wait_ge(S["xs_made"], 2)
                dve.tensor_tensor(by(xd, h=HD), by(xs[:, 0, :], h=HD), spread(decay, HD), ALU.mult
                                  ).then_inc(S["xd_made"], 1)
                for t in range(NT):
                    mark(dve.tensor_tensor(by(xh[:, t, :], h=HD), by(xh[:, t, :], h=HD), spread(heads_b[:, 2, :], HD),
                                           ALU.mult))
                sync()
                for g in range(2):
                    b = take(dve, f"yo{g}")
                    give(f"yo{g}", dve.tensor_tensor(by(xd[:, g * N:(g + 1) * N], h=HD), by(b, h=HD),
                                                     spread(expcs[:, 8 * g:8 * g + 8], HD), ALU.mult))
                for g in range(2):
                    given(dve, f"yo{g}")
                    cut = xh[:, 1, g * N:(g + 1) * N]
                    mark(dve.tensor_tensor(cut, cut, xd[:, g * N:(g + 1) * N], ALU.add))
                given(dve, "cb")
                for c in range(NT):
                    for qd in range(5):
                        if qd < 4:
                            b = take(dve, f"rb{c}{qd}")
                            if c:
                                dve.wait_ge(bank_full, JOB[f"yd0{qd // 2}"] + 1)
                            for i in range(4):
                                hh = 4 * qd + i
                                ins = dve.tensor_scalar(mt[:, qd, i * P:(i + 1) * P], b[:, i * P:(i + 1) * P],
                                                        csv[:, c, hh:hh + 1], 0.0, ALU.subtract, ALU.min)
                                if i == 3:
                                    give(f"rb{c}{qd}", ins)
                        if qd:
                            dve.wait_ge(S["decay_made"], 4 * c + qd)
                            m = by(mt[:, qd - 1, :], h=P)
                            dve.tensor_tensor(m, m, repeat(cbm[:, 2 * c + (qd - 1) // 2, :], 4), ALU.mult
                                              ).then_inc(S["mt_made"], 1)
                    if c == 0:
                        pass
                    sync()
                    for g in range(2):
                        cut = xh[:, c, g * N:(g + 1) * N]
                        b = take(dve, f"yd{c}{g}")
                        give(f"yd{c}{g}", dve.tensor_tensor(cut, b, cut, ALU.add))
                        given(dve, f"yd{c}{g}")
                        for n in range(2):
                            given(dve, f"z{n}{c}")
                        dve.tensor_tensor(cut, cut, z[:, c, g * N:(g + 1) * N], ALU.mult).then_inc(S["y_made"], 1)
                for i in range(2):
                    b = take(dve, f"wt{i}")
                    give(f"wt{i}", dve.tensor_tensor(sgu_wT[:, 4 * i:4 * i + 4, :], by(b, h=P), repeat(tri, 4), ALU.mult))
                dve.wait_ge(S["ysq_made"], 4)
                root_mean(ssg, N, EPS, S["ymean_made"])
                for t in range(NT):
                    for n in range(2):
                        given(dve, f"v{n}{t}")
                        mark(dve.bn_stats(bn[:, t, n, :], vs[:, t, n * N:(n + 1) * N]))
                sync()
                for t in range(NT):
                    mark(dve.bn_aggr(mv[:, t, :], bn[:, t, :, :].rearrange("p a b -> p (a b)")))
                sync()
                dve.tensor_scalar(by(lss, h=1), mv[:, :, 1:2], LN_EPS, None, ALU.add).then_inc(S["var_made"], 1)
                dve.wait_ge(S["yroot_made"], 1)
                link(dve.reciprocal(rsg, rsg))
                for t in range(NT):
                    for g in range(2):
                        cut = xh[:, t, g * N:(g + 1) * N]
                        ins = dve.tensor_scalar(cut, cut, rsg[:, t, g:g + 1], None, ALU.mult)
                        if g:
                            ins.then_inc(S["y_normed"], 1)
                dve.wait_ge(S["vroot_made"], 1)
                link(dve.reciprocal(lrs, lrs))
                for t in range(NT):
                    mark(dve.tensor_scalar(vs[:, t, :], vs[:, t, :], mv[:, t, 0:1], lrs[:, t:t + 1],
                                           ALU.subtract, ALU.mult))
                sync()
                for what, op in (("lng", ALU.mult), ("lnb", ALU.add)):
                    for hh in range(2):
                        b = take(dve, f"{what}{hh}")
                        for t in range(NT):
                            if what == "lnb":
                                given(dve, f"lng{hh}")
                            cut = vs[:, t, hh * N:(hh + 1) * N]
                            ins = dve.tensor_tensor(cut, b, cut, op)
                            if t == 1:
                                give(f"{what}{hh}", ins)
                            else:
                                mark(ins)
                    sync()
                given(dve, "lnb0")
                given(dve, "lnb1")
                dve.tensor_copy(small[:, 510:511], mv[:, 0, 0:1]).then_inc(S["v_normed"], 2)
                for t in range(NT):
                    for hh in range(2):
                        b = take(dve, f"yT_ssd{t}{hh}")
                        give(f"yT_ssd{t}{hh}", dve.tensor_tensor(yT[:, 4 * hh:4 * hh + 4, t * P:(t + 1) * P], by(b, h=P),
                                                                 spread(col("ssd", 4 * hh, 4), P), ALU.mult))

                def merge(br, n):
                    for t in range(NT):
                        b = take(dve, f"br_{br}{n}{t}")
                        given(dve, f"gate_{br}{n}{t}")
                        cut = merged[:, t, n * N:(n + 1) * N]
                        if br == "ssd":
                            give(f"br_{br}{n}{t}", dve.tensor_tensor(cut, b, gate[:, t, :], ALU.mult))
                            given(dve, f"br_{br}{n}{t}")
                            dve.tensor_copy(small[:, 509:510], small[:, 510:511]).then_inc(S["gated"], 1)
                        else:
                            give(f"br_{br}{n}{t}", dve.tensor_tensor(gate[:, t, :], b, gate[:, t, :], ALU.mult))
                            given(dve, f"br_{br}{n}{t}")
                            dve.tensor_tensor(cut, cut, gate[:, t, :], ALU.add).then_inc(S["gated"], 1)

                def head_norm(i):
                    src, t = (q, k)[i // 2], i % 2
                    a = by(src[:, t, :], h=QK)
                    dve.wait_ge(S["hsq_made"], i + 1)
                    link(dve.tensor_reduce(ssh, by(tmp, h=QK), AX.X, ALU.add))
                    root_mean(ssh, QK, EPS, S["hmean_made"])
                    dve.wait_ge(S["hroot_made"], i + 1)
                    link(dve.reciprocal(rsh, rsh))
                    link(dve.tensor_tensor(a, a, spread(rsh, QK), ALU.mult))
                    link(dve.tensor_tensor(a, a, repeat(gain_b[:, i // 2, :], HEADS), ALU.mult))
                    x1, x2 = a[:, :, NOPE:NOPE + HALF_ROPE], a[:, :, NOPE + HALF_ROPE:QK]
                    cs_, sn_ = repeat(cos[:, t, :], HEADS), repeat(sin[:, t, :], HEADS)
                    r = tmp[:, 0:4 * HEADS * HALF_ROPE].rearrange("p (a h c) -> p a h c", a=4, h=HEADS)
                    for j, (m, n) in enumerate(((x1, cs_), (x2, sn_), (x1, sn_), (x2, cs_))):
                        mark(dve.tensor_tensor(r[:, j], m, n, ALU.mult))
                    sync()
                    mark(dve.tensor_tensor(x1, r[:, 0], r[:, 1], ALU.subtract))
                    dve.tensor_tensor(x2, r[:, 2], r[:, 3], ALU.add).then_inc(S["hnorm_made"], 1)

                head_norm(0)
                head_norm(1)
                merge("ssd", 0)
                head_norm(2)
                head_norm(3)
                merge("ssd", 1)
                for t in range(NT):
                    for n in range(2):
                        given(dve, f"u{n}{t}")
                    for hh in range(2):
                        b = take(dve, f"mx{t}{hh}")
                        for i in range(4):
                            g = 4 * hh + i
                            cut = u[:, t, g * P:(g + 1) * P]
                            ins = dve.scalar_tensor_tensor(cut, b[:, i * P:(i + 1) * P], col("sgu_b", g), cut,
                                                           ALU.add, ALU.mult)
                            if i == 3:
                                give(f"mx{t}{hh}", ins)
                for kind, i in attention_order():
                    if kind == "close":
                        if i in (2, 4):
                            merge("sgu", i // 2 - 1)
                        continue
                    if kind == "pt":
                        continue
                    t, h0, nh = GROUPS[i]
                    keys = (t + 1) * P
                    if kind == "sc":
                        b = take(dve, f"sc{i}")
                        if i >= 2:
                            dve.wait_ge(bank_full, JOB[f"pt{i - 2}"] + 1)
                        pr = by(prob[:, i % 2, :], h=keys)
                        give(f"sc{i}", dve.tensor_tensor(pr, by(b, h=keys), repeat(mask[:, 2 * P - keys:], nh), ALU.add))
                        given(dve, f"sc{i}")
                        link(dve.tensor_reduce(mx[:, 0:nh], pr, AX.X, ALU.max))
                        if i >= 2:
                            dve.wait_ge(S["prob_made"], i - 1)
                        dve.tensor_scalar(nmx[:, i % 2, 0:nh], mx[:, 0:nh], -SCALE, None, ALU.mult
                                          ).then_inc(S["max_made"], 1)
                        dve.wait_ge(S["max_made"], i + 1)
                    else:
                        dve.wait_ge(S["prob_made"], i + 1)
                        link(dve.reciprocal(rinv[:, t, h0:h0 + nh], rsum[:, t, h0:h0 + nh]))
                        b = take(dve, f"o{i}")
                        give(f"o{i}", dve.tensor_tensor(by(o[:, t, h0 * HD:(h0 + nh) * HD], h=HD), by(b[:, 0:nh * HD], h=HD),
                                                        spread(rinv[:, t, h0:h0 + nh], HD), ALU.mult))
                        given(dve, f"o{i}")
                        dve.tensor_copy(small[:, 509:510], small[:, 510:511]).then_inc(S["o_made"], 1)
                merge("mla", 0)
                merge("mla", 1)
                dve.wait_ge(S["gated"], 12)
                dve.tensor_copy(small[:, 509:510], small[:, 510:511]).then_inc(S["merged_made"], 8)
                for n in range(2):
                    for t in range(NT):
                        b = take(dve, f"out{n}{t}")
                        cut = x[:, t, n * N:(n + 1) * N]
                        give(f"out{n}{t}", dve.tensor_tensor(cut, b, cut, ALU.add))
                dve.wait_ge(S["fsquared"], 2)
                root_mean(ss[:], D, EPS, S["fmean_made"])
                dve.wait_ge(S["frooted"], 1)
                link(dve.reciprocal(rs[:], rs[:]))
                for t in range(NT):
                    dve.tensor_scalar(fn[:, t, :], x[:, t, :], rs[:, t:t + 1], None, ALU.mult).then_inc(S["fnormed"], 1)
                for t in range(NT):
                    for hh in range(2):
                        b = take(dve, f"ft{t}{hh}")
                        give(f"ft{t}{hh}", dve.tensor_tensor(hT[:, 4 * hh:4 * hh + 4, t * P:(t + 1) * P], by(b, h=P),
                                                             spread(col("ffn", 4 * hh, 4), P), ALU.mult))
                steps = chain.n
                with dve.If(L < 1):
                    ffn(len(DENSE_UNITS), lambda i: DENSE_UNITS[i][2])
                    dve.wait_ge(S["down_done"], len(DENSE_UNITS))
                    for t in range(NT):
                        for half in range(2):
                            cut = x[:, t, half * N:(half + 1) * N]
                            dve.tensor_tensor(cut, ps[:, 4 + 2 * t + half], cut, ALU.add)
                assert chain.n == steps
                link(dve.tensor_copy(small[:, 509:510], small[:, 510:511]))
                dve.sem_inc(arrived, 1)

            chain.n = 0
            begin(dve, DEPTH + 1)

            def r(n):
                return route[:, n]

            expert2 = by(cst("expert", NT * EXPERTS), h=EXPERTS)
            dve.wait_ge(S["logits"], 1)
            link(dve.tensor_copy(r(0), by(ps[:, 0, 0:NT * EXPERTS], h=EXPERTS)))
            m1, m2, low = (r(n)[:, :, 0:1] for n in (1, 2, 5))

            def wide(a):
                return a.to_broadcast([P, NT, EXPERTS])

            def choose(logits, top, out_):
                link(dve.tensor_reduce(top, logits, AX.X, ALU.max))
                link(dve.tensor_tensor(r(6), logits, wide(top), ALU.is_equal))
                link(dve.scalar_tensor_tensor(r(7), expert2, float(EXPERTS), r(6), ALU.subtract, ALU.mult))
                link(dve.tensor_reduce(low, r(7), AX.X, ALU.min))
                link(dve.tensor_tensor(out_, r(7), wide(low), ALU.is_equal))

            choose(r(0), m1, r(8))
            link(dve.scalar_tensor_tensor(r(9), r(8), -1e30, r(0), ALU.mult, ALU.add))
            choose(r(9), m2, r(10))
            dve.tensor_tensor(r(3)[:, :, 0:1], m2, m1, ALU.subtract).then_inc(S["gap_made"], 1)
            dve.tensor_tensor(chosen, r(8), r(10), ALU.add).then_inc(S["chosen"], 1)
            e_, w1, w2 = r(4)[:, :, 0:1], r(4)[:, :, 1:2], r(4)[:, :, 2:3]
            dve.wait_ge(S["gap_exp"], 1)
            link(dve.tensor_scalar(w1, e_, 1.0, None, ALU.add))
            link(dve.reciprocal(w1, w1))
            link(dve.tensor_tensor(w2, e_, w1, ALU.mult))
            mark(dve.tensor_tensor(r(8), r(8), wide(w1), ALU.mult))
            mark(dve.tensor_tensor(r(10), r(10), wide(w2), ALU.mult))
            sync()
            link(dve.tensor_tensor(r(9), r(8), r(10), ALU.add))
            dve.wait_ge(S["ranks"], 1)
            E8 = EXPERTS
            link(dve.tensor_scalar(r(0), by(ps[:, 1, 0:NT * E8], h=E8), 1.0, None, ALU.add))
            link(dve.tensor_tensor(r(0), r(0), chosen, ALU.mult))
            link(dve.tensor_scalar(r(0), r(0), -1.0, None, ALU.add))
            big, start = r(6)[:, 0, :], r(6)[:, 1, :]
            link(dve.tensor_scalar(big, ps[:, 1, 2 * E8:3 * E8], float(P), None, ALU.is_gt))
            link(dve.tensor_copy(start, cst("expert", E8)))
            for e in range(1, E8):
                link(dve.tensor_tensor(start[:, e:E8], start[:, e:E8], big[:, e - 1:e].to_broadcast([P, E8 - e]), ALU.add))
            grid = [by(items[:, n, :], h=E8) for n in range(8)]
            number = by(cst("item", ITEM_SLOTS * E8), h=E8)
            which = by(cst("expert", ITEM_SLOTS * E8), h=E8)
            expert_of = items[:, 4, 0:ITEM_SLOTS]
            block_of = items[:, 5, 0:ITEM_SLOTS]
            mark(dve.tensor_tensor(grid[0], number, repeat(start, ITEM_SLOTS), ALU.is_ge))
            mark(dve.tensor_tensor(grid[1], number, repeat(start, ITEM_SLOTS), ALU.is_equal))
            sync()
            mark(dve.tensor_reduce(expert_of, grid[0], AX.X, ALU.add))
            mark(dve.tensor_reduce(block_of, grid[1], AX.X, ALU.add))
            sync()
            mark(dve.tensor_scalar(expert_of, expert_of, -1.0, None, ALU.add))
            mark(dve.tensor_scalar(block_of, block_of, -float(P), float(P), ALU.mult, ALU.add))
            sync()
            link(dve.tensor_tensor(grid[2], which, spread(expert_of, E8), ALU.is_equal))
            for t in range(NT):
                link(dve.tensor_tensor(grid[3], grid[2], repeat(r(0)[:, t, :], ITEM_SLOTS), ALU.mult))
                link(dve.tensor_reduce(pos_item[:, t, :], grid[3], AX.X, ALU.add))
                link(dve.tensor_tensor(pos_item[:, t, :], pos_item[:, t, :], block_of, ALU.subtract))
                link(dve.tensor_tensor(grid[3], grid[2], repeat(r(9)[:, t, :], ITEM_SLOTS), ALU.mult))
                link(dve.tensor_reduce(w_item[:, t, :], grid[3], AX.X, ALU.add))
            link(dve.tensor_reduce(items[:, 6, 0:1], big, AX.X, ALU.add))
            link(dve.tensor_scalar(items[:, 6, 0:1], items[:, 6, 0:1], float(EXPERTS), None, ALU.add))
            link(dve.tensor_copy(item_tab[0:1, 0:ITEM_SLOTS], expert_of[0:1, :]))
            dve.tensor_copy(item_tab[0:1, ITEM_SLOTS:ITEM_SLOTS + 1], items[0:1, 6, 0:1]).then_inc(routed, 1)
            dve.wait_ge(routed, 1)
            n_items = dve.value_load(item_tab[0:1, ITEM_SLOTS:ITEM_SLOTS + 1], min_val=EXPERTS, max_val=MAX_ITEMS)
            dve.sem_inc(arrived, 1)

            with dve.Fori(0, n_items) as item:
                begin(dve, item + (DEPTH + 2))
                for t in range(NT):
                    ins = dve.tensor_scalar(pick[:, t, :], slot_no, pos_item[:, t, bass.ds(item, 1)], None, ALU.is_equal)
                ins.then_inc(S["picked"], 1)
                for t in range(NT):
                    ins = dve.tensor_scalar(wpick[:, t, :], slot_no, pos_item[:, t, bass.ds(item, 1)],
                                            w_item[:, t, bass.ds(item, 1)], ALU.is_equal, ALU.mult)
                ins.then_inc(S["picked"], 1)
                for hh in range(2):
                    dve.wait_ge(S["gathered"], hh + 1)
                    dve.tensor_tensor(xg[:, 4 * hh:4 * hh + 4, :], by(ps[:, 6 + hh], h=P), spread(col("ffn", 4 * hh, 4), P),
                                      ALU.mult).then_inc(S["xg_made"], 1)
                ffn(len(MOE_PANELS), lambda i: N)
                dve.wait_ge(S["down_done"], len(MOE_PANELS))
                dve.tensor_copy(ysb[:, N:2 * N], ps[:, 5]).then_inc(S["y_copied"], 1)
                for j in range(4):
                    t, half = j // 2, j % 2
                    dve.wait_ge(S["scattered"], j + 1)
                    cut = x[:, t, half * N:(half + 1) * N]
                    ins = dve.tensor_tensor(cut, ps[:, (6, 7, 0, 1)[j]], cut, ALU.add)
                ins.then_inc(dve_steps, 1)
                dve.wait_ge(dve_steps, 1)
                dve.sem_inc(arrived, 1)


_INS = ["x", "mix_norm_g", "w_in", "conv_w", "conv_b", "dt_bias", "a_log", "d_skip", "ssd_norm_g", "sgu_ln_g",
        "sgu_ln_b", "sgu_w", "sgu_b", "q_norm_g", "w_uq", "kv_norm_g", "w_ukv", "q_head_g", "k_head_g", "w_br_ssd",
        "w_br_sgu", "w_br_mla", "w_out", "ffn_norm_g", "ffn_w_gate", "ffn_w_up", "ffn_w_down", "router_w",
        "moe_w_gate", "moe_w_up", "moe_w_down"]


def constant_table():
    import numpy as np

    c = np.zeros((P, N_CONST), np.float32)
    p, f = np.arange(P)[:, None], np.arange(P)[None, :]
    c[:, CONST["ident"]:][:, :P] = p == f
    c[:, CONST["tri"]:][:, :P] = p <= f
    c[:, CONST["before"]:][:, :P] = p < f
    c[:, CONST["slot"]:][:, :P] = f
    c[:, CONST["mask"] + P:][:, :P] = np.where(f <= p, 0.0, -1e30)
    inv = (1.0 / (np.float32(10000.0) ** (np.arange(0, 2 * HALF_ROPE, 2, dtype=np.float32) / np.float32(2 * HALF_ROPE)))
           ).astype(np.float32)
    for t in range(NT):
        ang = ((t * P + np.arange(P)).astype(np.float32)[:, None] * inv[None, :]).astype(np.float32)
        c[:, CONST["cos"] + HALF_ROPE * t:][:, :HALF_ROPE] = np.cos(ang)
        c[:, CONST["sin"] + HALF_ROPE * t:][:, :HALF_ROPE] = np.sin(ang)
    i = np.arange(ITEM_SLOTS * EXPERTS)
    c[:, CONST["item"]:][:, :i.size] = i // EXPERTS
    c[:, CONST["expert"]:][:, :i.size] = i % EXPERTS
    return c


def kernel(**inputs):
    import numpy as np
    import concourse.bacc as bacc
    from concourse.bass_utils import run_bass_kernel_spmd as run

    nc = bacc.Bacc("TRN2", target_bir_lowering=False, num_devices=1)
    arrays, aps = {}, {}
    for name in _INS + ["const"]:
        a = constant_table() if name == "const" else np.ascontiguousarray(inputs[name])
        arrays[f"in_{name}"] = a
        aps[name] = nc.dram_tensor(f"in_{name}", a.shape, mybir.dt.from_np(a.dtype), kind="ExternalInput").ap()
    out = nc.dram_tensor("out_0", (1, NT * P, D), F32, kind="ExternalOutput").ap()
    hybrid_trunk(nc, aps, out)
    return run(nc, [arrays], core_ids=[0]).results[0]["out_0"]
```

```python
from contextlib import ExitStack

import concourse.bass as bass
from concourse import mybir

ALU = mybir.AluOpType
ACT = mybir.ActivationFunctionType
F32 = mybir.dt.float32
I32 = mybir.dt.int32
F32R = mybir.dt.float32r
AX = mybir.AxisListType

P = 128
NT = 2
D = 1024
KD = D // P
DEPTH = 2
HEADS = 16
HD = 64
QK = 96
NOPE = 64
HALF_ROPE = 16
CONV_CHUNKS = 12
TAPS = 4
EPS = 1e-6
LN_EPS = 1e-5
SCALE = QK ** -0.5
N = 512
SLOT = KD * N
FFN_DENSE = 2816
FFN_EXPERT = 3584
EXPERTS = 8
MAX_ITEMS = 11
ITEM_SLOTS = 16

C_Z, C_XBC, C_DT, C_U, C_V, C_LAT, C_GATE = 0, 1024, 2560, 2576, 3600, 4624, 5040
LAT = 416

ROWS = {}
_at = 0
for _name, _n in (("mix", 8), ("ffn", 8), ("conv_b", 12), ("conv_w", 48), ("ssd", 8), ("q", 2), ("kv", 1),
                  ("sgu_b", 8), ("ln_g", 8), ("ln_b", 8)):
    ROWS[_name] = _at
    _at += _n
N_ROWS = _at

CONST = {}
_at = 0
for _name, _n in (("ident", P), ("tri", P), ("before", P), ("slot", P), ("mask", 2 * P), ("cos", 2 * HALF_ROPE),
                  ("sin", 2 * HALF_ROPE), ("item", ITEM_SLOTS * EXPERTS), ("expert", ITEM_SLOTS * EXPERTS)):
    CONST[_name] = _at
    _at += _n
N_CONST = _at


def mixer_panels():
    out = [(f"xbc{n}", "in", C_XBC + N * n, N) for n in range(3)]
    out += [("lat", "in", C_LAT, LAT)]
    out += [(f"z{n}", "in", C_Z + N * n, N) for n in range(2)]
    out += [("uq", "uq", 0, HEADS * QK), ("ukv", "ukv", 0, HEADS * 2 * HD)]
    out += [(f"u{n}", "in", C_U + N * n, N) for n in range(2)]
    out += [(f"v{n}", "in", C_V + N * n, N) for n in range(2)]
    for b, br in enumerate(("ssd", "sgu", "mla")):
        for n in range(2):
            out += [(f"gate_{br}{n}", "in", C_GATE + D * b + N * n, N), (f"br_{br}{n}", br, N * n, N)]
    out += [(f"out{n}", "out", N * n, N) for n in range(2)]
    return out


def psum_jobs():
    j = ["vec"] + [f"ht{t}{h}" for t in range(NT) for h in range(2)]
    j += [f"xbc{i}" for i in range(6)] + ["dt"] + ["lat0", "lat1"]
    j += [f"z{n}{t}" for n in range(2) for t in range(NT)]
    j += ["cs"] + [f"xt{t}{h}" for t in range(NT) for h in range(2)] + ["bt", "cb", "latT0", "latT1"]
    j += [f"q{t}{n}" for t in range(NT) for n in range(3)]
    j += [f"kv{t}{n}" for t in range(NT) for n in range(4)]
    j += [f"u{n}{t}" for n in range(2) for t in range(NT)]
    j += ["st0", "st1", "yo0", "yo1"] + [f"rb0{q}" for q in range(4)]
    j += ["v00", "v01", "yd00", "yd01"] + [f"rb1{q}" for q in range(4)]
    j += ["v10", "v11", "yd10", "yd11"] + ["wt0", "wt1", "lng0", "lng1", "lnb0", "lnb1"]
    j += closing("ssd")
    j += [f"qT{t}{i}" for t in range(NT) for i in range(4)] + [f"kT{t}{i}" for t in range(NT) for i in range(4)]
    j += [f"mx{t}{h}" for t in range(NT) for h in range(2)]
    for kind, i in attention_order():
        if kind == "close":
            j += closing_part("sgu", i)
        else:
            j += [f"{kind}{i}"]
    j += closing("mla")
    j += [f"mT{t}{h}" for t in range(NT) for h in range(2)]
    j += [f"out{n}{t}" for n in range(2) for t in range(NT)]
    j += [f"ft{t}{h}" for t in range(NT) for h in range(2)]
    return j


def closing_part(br, i):
    if i == 1:
        return [f"yT_{br}{t}{h}" for t in range(NT) for h in range(2)]
    what, n = (("gate", 0), None, ("br", 0), ("gate", 1), ("br", 1))[i]
    return [f"{what}_{br}{n}{t}" for t in range(NT)]


def closing(br):
    return [x for i in range(5) for x in closing_part(br, i)]


GROUPS = [(0, 4 * q, 4) for q in range(4)] + [(1, 2 * q, 2) for q in range(8)]


def attention_order():
    out = []
    for s in range(len(GROUPS) + 2):
        if s < len(GROUPS):
            out.append(("sc", s))
        if s in (0, 2, 4, 6, 8):
            out.append(("close", s // 2))
        if 1 <= s <= len(GROUPS):
            out.append(("pt", s - 1))
        if s >= 2:
            out.append(("o", s - 2))
    return out


PANELS = mixer_panels()
JOBS = psum_jobs()
JOB = {name: i for i, name in enumerate(JOBS)}
assert len(JOB) == len(JOBS)
RING = 4
MOE_RING = 7
DENSE_PANELS = [(c, min(N, FFN_DENSE - c)) for c in range(0, FFN_DENSE, N)]
MOE_PANELS = [(c, N) for c in range(0, FFN_EXPERT, N)]
LAYER_USES = len(PANELS) + 3 * len(DENSE_PANELS)
assert LAYER_USES % RING == 0 and 3 * len(MOE_PANELS) % MOE_RING == 0
ITEM_USES = 3 * len(MOE_PANELS) // MOE_RING
HI_SLOTS = 6
AHEAD = 4


class Split:

    def __init__(self, widths):
        n = len(widths)
        self.widths = widths
        self.order = [("gate", 0), ("up", 0)]
        for i in range(1, n):
            self.order += [("gate", i), ("up", i), ("down", i - 1)]
        self.order += [("down", n - 1)]
        self.at = {x: u for u, x in enumerate(self.order)}
        self.pieces = []
        self.first = []
        for u, (kind, i) in enumerate(self.order):
            self.first.append(len(self.pieces))
            step = D if kind == "down" else KD // 4 * widths[i]
            total = (widths[i] // P if kind == "down" else KD) * (D if kind == "down" else widths[i])
            self.pieces += [(u, o, step, o + step == total) for o in range(0, total, step)]
        self.first.append(len(self.pieces))

    def through(self, kind, i):
        return self.first[self.at[(kind, i)] + 1]


DENSE = Split([w for _, w in DENSE_PANELS])
MOE = Split([w for _, w in MOE_PANELS])
SCATTER_BANKS = (6, 7, 1, 3)


class Chain:

    def __init__(self, eng, sem):
        self.eng, self.sem, self.n = eng, sem, 0

    def mark(self, ins):
        self.n += 1
        ins.then_inc(self.sem, 1)

    def sync(self):
        self.eng.wait_ge(self.sem, self.n)

    def link(self, ins):
        self.mark(ins)
        self.sync()


def hybrid_trunk(nc, A, out):
    with ExitStack() as ctx:
        def sb(name, shape, dt=F32):
            return ctx.enter_context(nc.sbuf_tensor(name, shape, dt))

        x = sb("x", [P, NT, D])
        hT = sb("hT", [P, KD, NT * P])
        hT_base = nc.sbuf_base - 4 * KD * NT * P
        const = sb("const", [P, N_CONST])
        vec = sb("vec", [P, P])
        cols = sb("cols", [P, N_ROWS])
        w_dt = sb("w_dt", [P, KD, HEADS])
        heads_b = sb("heads_b", [P, 3, HEADS])
        gain_b = sb("gain_b", [P, 2, QK])
        small = sb("small", [P, 512])
        r_w = sb("r_w", [P, KD, EXPERTS])
        ones = sb("ones", [P, P])
        chosen = sb("chosen", [P, NT, EXPERTS])[:]
        item_tab = sb("item_tab", [1, ITEM_SLOTS + 1], I32)
        free = (nc.sbuf_bytes_remaining() if callable(nc.sbuf_bytes_remaining) else nc.sbuf_bytes_remaining) // 4 - 64
        sb("arena", [P, free])
        arena_base = nc.sbuf_base - 4 * free
        ps = ctx.enter_context(nc.psum_tensor("ps", [P, 8, N], F32))

        n_pieces = [0]

        def piece(at, *shape):
            n = 1
            for s in shape:
                n *= s
            assert at + n <= free, (at, n, free)
            n_pieces[0] += 1
            v = nc.alloc_sbuf_tensor_at(f"piece{n_pieces[0]}", [P] + list(shape), F32, offset=arena_base + 4 * at)[:]
            return v, at + -(-n // 8) * 8

        slots = [piece(s * SLOT, SLOT)[0] for s in range(MOE_RING)]
        at = RING * SLOT
        kT, _ = piece(at, HEADS, NT * P)
        xin, at = piece(at, 2, 2, NT * P + TAPS - 1)
        xc, at = piece(at, CONV_CHUNKS, NT * P)
        qT, _ = piece(at, HEADS, NT * P)
        xh, at = piece(at, NT, D)
        xs, at = piece(at, NT, D)
        z, z_end = piece(at, NT, D)
        tmp, _ = piece(at, HEADS * QK)
        at = z_end
        o, _ = piece(at, NT, D)
        q, at = piece(at, NT, HEADS * QK)
        k, at = piece(at, NT, HEADS * QK)
        v, at = piece(at, NT, HEADS, HD)
        prob, _ = piece(at, 2, N)
        probT, _ = piece(at + 2 * N, 2, N)
        lat, _ = piece(at, NT, LAT)
        sgu_wT, _ = piece(at, 8, P)
        mt, at = piece(at, 4, N)
        xn, _ = piece(at, NT, D)
        u, at = piece(at, NT, D)
        vs, at = piece(at, NT, D)
        sgu_raw, _ = piece(at, 8, P)
        cbm, _ = piece(at + 8 * P, 4, P)
        yT, at = piece(at, KD, NT * P)
        latT, _ = piece(at, 3, NT * P)
        b_tok, _ = piece(at + 3 * NT * P, 2, P)
        gate, at = piece(at, NT, N)
        prev, _ = piece(at, 2, N)
        xd, _ = piece(at + 2 * N, D)
        merged, at = piece(at, NT, D)
        at = MOE_RING * SLOT
        fn, at = piece(at, NT, D)
        sg, at = piece(at, NT, N)
        h, at = piece(at, NT, N)
        at_xg = at
        xg, at = piece(at, KD, P)
        ysb, at = piece(at, D)
        pick, at = piece(at, NT, P)
        wpick, at = piece(at, NT, P)
        wpickT, at = piece(at, NT, P)
        items, at = piece(at, 8, ITEM_SLOTS * EXPERTS)
        pos_item, at = piece(at, NT, ITEM_SLOTS)
        w_item, at = piece(at, NT, ITEM_SLOTS)
        route, at = piece(at, 12, NT, EXPERTS)

        def over(name, base, at, shape):
            return nc.alloc_sbuf_tensor_at(name, [P] + shape, F32R, offset=base + 4 * at)

        w_lo = [over(f"w_lo{s}", arena_base, s * SLOT, [SLOT]) for s in range(MOE_RING)]
        xg_lo = over("xg_lo", arena_base, at_xg, [KD, P])
        hT_lo = over("hT_lo", hT_base, 0, [KD, NT * P])
        hT_hi = over("hT_hi", arena_base, RING * SLOT, [KD, NT * P])
        hid_hi = over("hid_hi", arena_base, at, [NT, N])
        hid_lo = over("hid_lo", arena_base, at + NT * N, [NT, N])
        at += 2 * NT * N
        xg_hi = over("xg_hi", arena_base, at, [KD, P])
        at += KD * P
        w_hi = over("w_hi", arena_base, at, [HI_SLOTS, D])
        assert at + HI_SLOTS * D <= free

        s_at = [0]

        def tiny(n):
            s_at[0] += n
            assert s_at[0] <= 512
            return small[:, s_at[0] - n:s_at[0]]

        def by(ap, **kw):
            (n1, s1), = [(a, b) for a, b in kw.items()]
            return ap.rearrange(f"p (a {n1}) -> p a {n1}", **{n1: s1})

        ss = tiny(2)
        rs = tiny(2)
        dtr = by(tiny(32), h=HEADS)
        dte = by(tiny(32), h=HEADS)
        dtv = by(tiny(32), h=HEADS)
        adt = by(tiny(32), h=HEADS)
        aexp = tiny(16)
        csv = by(tiny(64), h=HEADS)
        expcs = tiny(16)
        decay = tiny(16)
        ssg = by(tiny(4), h=2)
        rsg = by(tiny(4), h=2)
        ssl = by(tiny(4), h=2)
        rsl = by(tiny(4), h=2)
        ssh = tiny(16)
        rsh = tiny(16)
        mx = tiny(4)
        nmx = by(tiny(8), h=4)
        rsum = by(tiny(32), h=HEADS)
        rinv = by(tiny(32), h=HEADS)
        bn = tiny(24).rearrange("p (a b c) -> p a b c", a=NT, b=2)
        mv = by(tiny(4), h=2)
        lrs = tiny(2)
        lss = tiny(2)

        def cst(name, n):
            return const[:, CONST[name]:CONST[name] + n]

        ident = cst("ident", P)
        tri = cst("tri", P)
        before = cst("before", P)
        slot_no = cst("slot", P)
        mask = cst("mask", 2 * P)
        cos = by(cst("cos", 2 * HALF_ROPE), h=HALF_ROPE)
        sin = by(cst("sin", 2 * HALF_ROPE), h=HALF_ROPE)

        def col(name, i, n=1):
            return cols[:, ROWS[name] + i:ROWS[name] + i + n]

        def spread(ap, n):
            return ap.unsqueeze(2).to_broadcast([ap.shape[0], ap.shape[1], n])

        def repeat(ap, n):
            return ap.unsqueeze(1).to_broadcast([ap.shape[0], n, ap.shape[1]])

        def sem(name):
            return ctx.enter_context(nc.semaphore(name))

        const_in = sem("const_in")
        setup_done = sem("setup_done")
        ring_full = [sem(f"ring_full{s}") for s in range(MOE_RING)]
        ring_used = [sem(f"ring_used{s}") for s in range(MOE_RING)]
        go = sem("go")
        begun = sem("begun")
        stored = sem("stored")
        fills_begun = sem("fills_begun")
        routed = sem("routed")
        finished = sem("finished")

        first_cleared = sem("arrived")
        arrived = first_cleared
        numbers = [arrived.num]

        def local(name):
            s = sem(name)
            numbers.append(s.num)
            return s

        bank_full = local("bank_full")
        bank_free = [local(f"bank_free{b}") for b in range(8)]
        act_steps = local("act_steps")
        dve_steps = local("dve_steps")
        vec_in = local("vec_in")
        small_in = local("small_in")
        S = {name: local(name) for name in (
            "squared", "mean_made", "rooted", "normed", "conv_made", "silu_made", "dt_neg", "dt_log", "a_exp",
            "adt_made", "tail_made", "cs_exp", "xs_made", "xd_made", "decay_made", "mt_made", "y_made", "ysq_made",
            "ymean_made", "yroot_made", "y_normed", "latsq_made", "latmean_made", "latroot_made", "lat_normed",
            "kpe_made", "kv_copied", "gated", "hsq_made", "hmean_made", "hroot_made", "hnorm_made", "max_made",
            "prob_made", "o_made", "var_made", "vroot_made", "v_normed", "merged_made", "fsquared", "fmean_made",
            "frooted", "fnormed", "sg_made", "h_made", "t_full", "hid_hi_made", "hid_made",
            "hi_made", "lo_made", "piece_used", "panel_done", "hT_hi_made", "hT_lo_made",
            "picked", "gathered", "xg_made", "xg_hi_made", "xg_lo_made", "wpickT_full", "wpickT_made", "y_copied", "scattered", "added", "zeroed",
            "logits", "chosen", "ranks", "gap_made", "gap_exp",
            "zeros_made")}
        assert numbers == list(range(numbers[0], numbers[0] + len(numbers)))
        cleared = range(numbers[0], numbers[-1] + 1)

        bank_uses = [len(JOBS[b::8]) for b in range(8)]

        def take(eng, name):
            eng.wait_ge(bank_full, JOB[name] + 1)
            return ps[:, JOB[name] % 8]

        def give(name, ins):
            ins.then_inc(bank_free[JOB[name] % 8], 1)

        def given(eng, name):
            eng.wait_ge(bank_free[JOB[name] % 8], JOB[name] // 8 + 1)

        def wait_panel(eng, split, kind, i):
            eng.wait_ge(S["panel_done"], split.at[(kind, i)] + 1)

        def split_pieces(eng, split, done_, upto, slot_of, one_piece, wait_full):
            while done_[0] < min(upto, len(split.pieces)):
                c = done_[0]
                u, at_, n, last = split.pieces[c]
                wait_full(c, u, at_ == 0)
                one_piece(w_hi[:, c % HI_SLOTS, 0:n], slot_of(u), at_, n)
                done_[0] += 1

        def hidden_in(i, tiles):
            return slice(0, 2) if tiles == 2 else slice(i % 2, i % 2 + 1)

        def hidden_free(eng, split, i, tiles):
            if i > 2 - tiles:
                wait_panel(eng, split, "down", i - (1 if tiles == 2 else 2))

        def turned_before(split, i, tiles):
            if i == 0 or (tiles == 1 and i == len(split.widths) - 1):
                return split.through("up", i)
            return split.through("down", i - 1)

        def hi_free(eng, split, c):
            if c >= HI_SLOTS:
                u, _, _, last = split.pieces[c - HI_SLOTS]
                if last:
                    eng.wait_ge(S["panel_done"], u + 1)
                else:
                    eng.wait_ge(S["piece_used"], c - HI_SLOTS + 1 - u)

        def begin(eng, turn):
            eng.wait_ge(go, turn)
            eng.sem_inc(begun, 1)

        def rows(w):
            return w.rearrange("l (k p) n -> l p k n", p=P)

        W = {"in": rows(A["w_in"]), "uq": rows(A["w_uq"]), "ukv": rows(A["w_ukv"]), "ssd": rows(A["w_br_ssd"]),
             "sgu": rows(A["w_br_sgu"]), "mla": rows(A["w_br_mla"]), "out": rows(A["w_out"])}
        chunks_of = {"uq": 2, "ukv": 1}

        def slot_view(s, kchunks, width):
            return slots[s][:, 0:kchunks * width].rearrange("p (k n) -> p k n", k=kchunks)

        uses0 = [LAYER_USES // RING + len(range(s, len(PANELS), RING)) for s in range(RING)] + [0] * (MOE_RING - RING)

        def dense_slot(u):
            return (len(PANELS) + u) % RING

        def moe_slot(u):
            return u % MOE_RING

        block = ctx.enter_context(nc.Block())

        @block.sync
        def _(sp):
            sp.dma_start(const[:], A["const"]).then_inc(const_in, 16)
            sp.dma_start(r_w[:], A["router_w"][0].rearrange("(k p) e -> p k e", p=P)).then_inc(const_in, 16)
            sp.dma_start(x[:], A["x"][0].rearrange("(t p) d -> p t d", p=P)).then_inc(const_in, 16)

            with sp.Fori(0, DEPTH) as L:
                one = bass.ds(L, 1)

                def panel(use):
                    name, src, c, width = PANELS[use]
                    s, n = use % RING, use // RING
                    kc = chunks_of.get(src, KD)
                    sp.wait_ge(ring_used[s], L * (LAYER_USES // RING) + n + 1)
                    if c == 0:
                        sp.sem_inc(fills_begun, 1)
                    sp.dma_start(slot_view(s, kc, width),
                                 W[src][one, :, :, c:c + width].rearrange("a p k n -> p (a k) n")
                                 ).then_inc(ring_full[s], 16)

                for use in range(RING):
                    panel(use)
                sp.wait_ge(go, L + 1)
                for name, src, n in (("mix", "mix_norm_g", 8), ("ffn", "ffn_norm_g", 8), ("conv_b", "conv_b", 12),
                                     ("ssd", "ssd_norm_g", 8), ("q", "q_norm_g", 2), ("kv", "kv_norm_g", 1),
                                     ("ln_g", "sgu_ln_g", 8), ("ln_b", "sgu_ln_b", 8)):
                    sp.dma_start(vec[ROWS[name]:ROWS[name] + n, :],
                                 A[src][one, :].rearrange("a (r c) -> (a r) c", c=P)).then_inc(vec_in, 16)
                sp.dma_start(vec[ROWS["conv_w"]:ROWS["conv_w"] + 48, :],
                             A["conv_w"][one].rearrange("a k (r c) -> (a k r) c", c=P)).then_inc(vec_in, 16)
                sp.dma_start(vec[ROWS["sgu_b"]:ROWS["sgu_b"] + 8, :],
                             A["sgu_b"][one].rearrange("a r c -> (a r) c")).then_inc(vec_in, 16)
                for i, src in enumerate(("dt_bias", "a_log", "d_skip")):
                    sp.dma_start(heads_b[:, i, :], A[src][one, :].to_broadcast([P, HEADS])).then_inc(small_in, 16)
                for i, src in enumerate(("q_head_g", "k_head_g")):
                    sp.dma_start(gain_b[:, i, :], A[src][one, :].to_broadcast([P, QK])).then_inc(small_in, 16)
                with nc.allow_non_contiguous_dma(reason="sixteen columns of each row"):
                    sp.dma_start(w_dt[:], W["in"][one, :, :, C_DT:C_DT + HEADS].rearrange("a p k n -> p (a k) n")
                                 ).then_inc(small_in, 16)
                sp.dma_start(sgu_raw, A["sgu_w"][one].rearrange("a g t s -> t (a g) s")).then_inc(small_in, 16)
                for use in range(RING, len(PANELS)):
                    panel(use)
                with sp.If(L < 1):
                    for u, (kind, i) in enumerate(DENSE.order):
                        c, width = DENSE_PANELS[i]
                        use = len(PANELS) + u
                        s, n = use % RING, use // RING
                        sp.wait_ge(ring_used[s], n + 1)
                        if kind == "down":
                            dst = slots[s][:, 0:width // P * D].rearrange("p (k n) -> p k n", n=D)
                            w = A["ffn_w_down"][0, c:c + width, :].rearrange("(k p) n -> p k n", p=P)
                        else:
                            dst = slot_view(s, KD, width)
                            w = A[f"ffn_w_{kind}"][0].rearrange("(k p) n -> p k n", p=P)[:, :, c:c + width]
                        sp.dma_start(dst, w).then_inc(ring_full[s], 16)

            moe_w = {kind: A[f"moe_w_{kind}"][0].rearrange("e (k p) n -> e p k n", p=P) for kind in ("gate", "up", "down")}

            def moe_panel(item, u, expert):
                kind, p = MOE.order[u]
                c, width = MOE_PANELS[p]
                s, n = u % MOE_RING, u // MOE_RING
                sp.wait_ge(ring_used[s], item * ITEM_USES + (uses0[s] + n + 1))
                if kind == "down":
                    dst = slots[s].rearrange("p (k n) -> p k n", n=D)
                    w = moe_w[kind][expert, :, c // P:c // P + 4, :]
                else:
                    dst = slot_view(s, KD, width)
                    w = moe_w[kind][expert, :, :, c:c + width]
                sp.dma_start(dst, w.rearrange("a p k n -> p (a k) n")).then_inc(ring_full[s], 16)

            for u in range(RING):
                moe_panel(0, u, slice(0, 1))
            sp.wait_ge(go, DEPTH + 1)
            for u in range(RING, MOE_RING):
                moe_panel(0, u, slice(0, 1))
            sp.wait_ge(routed, 1)
            n_items = sp.value_load(item_tab[0:1, ITEM_SLOTS:ITEM_SLOTS + 1], min_val=EXPERTS, max_val=MAX_ITEMS)
            with sp.Fori(0, n_items) as i:
                e = sp.value_load(item_tab[0:1, bass.ds(i, 1)], min_val=0, max_val=EXPERTS - 1)
                for u in range(MOE_RING, len(MOE.order)):
                    moe_panel(i, u, bass.ds(e, 1))
                with sp.If(i < n_items - 1):
                    e2 = sp.value_load(item_tab[0:1, bass.ds(i + 1, 1)], min_val=0, max_val=EXPERTS - 1)
                    for u in range(MOE_RING):
                        moe_panel(i + 1, u, bass.ds(e2, 1))
            for t in range(NT):
                sp.wait_ge(finished, t + 1)
                sp.dma_start(out[0, t * P:(t + 1) * P, :], x[:, t, :]).then_inc(stored, 16)
            sp.wait_ge(stored, 32)

        @block.gpsimd
        def _(pool):
            pool.memset(vec[:], 0.0).then_inc(setup_done, 1)
            pool.memset(xin[:, :, :, 0:TAPS - 1], 0.0).then_inc(setup_done, 1)
            pool.memset(ones[:], 1.0).then_inc(setup_done, 1)
            pool.memset(small[:], 0.0).then_inc(setup_done, 1)
            pool.wait_ge(setup_done, 4)
            for s in range(MOE_RING):
                pool.sem_inc(ring_used[s], 1)
            pool.sem_inc(go, 1)
            with pool.Fori(0, DEPTH):
                pool.wait_ge(arrived, 3)
                pool.memset(xin[:, :, :, 0:TAPS - 1], 0.0).then_inc(S["zeros_made"], 1)
                pool.wait_ge(S["zeros_made"], 1)
                pool.sem_clear(cleared)
                pool.sem_inc(go, 1)
            pool.wait_ge(arrived, 3)
            n_items = pool.value_load(item_tab[0:1, ITEM_SLOTS:ITEM_SLOTS + 1], min_val=EXPERTS, max_val=MAX_ITEMS)
            pool.sem_clear(cleared)
            pool.sem_inc(go, 1)
            with pool.Fori(0, n_items):
                pool.wait_ge(arrived, 3)
                pool.sem_clear(cleared)
                pool.sem_inc(go, 1)

        @block.tensor
        def _(pe):
            turn = [0]
            unreleased = []

            def bank(name):
                i = turn[0]
                assert JOBS[i] == name, (JOBS[i], name)
                turn[0] += 1
                if i >= 8:
                    pe.wait_ge(bank_free[i % 8], i // 8)
                return ps[:, i % 8]

            def done(ins):
                ins.then_inc(bank_full, 1)

            def release():
                while unreleased:
                    s, signal, n = unreleased.pop(0)
                    pe.wait_ge(signal, n)
                    pe.sem_inc(ring_used[s], 1)

            def turn_over(name, parts):
                b = bank(name)
                at = 0
                for a in parts:
                    n, m = a.shape[0], a.shape[1]
                    last = pe.transpose(b[0:m, at:at + n], a, ident[0:n, 0:n])
                    at += n
                done(last)

            def htile(kk, t):
                return hT[:, kk, t * P:(t + 1) * P]

            def ytile(kk, t):
                return yT[:, kk, t * P:(t + 1) * P]

            def ffn(split, tiles, slot_of, lhs, acc, before_turn=None, before_down=None):
                n_panels = len(split.widths)

                def turn_hidden(i):
                    pe.wait_ge(S["h_made"], i + 1)
                    for t in range(tiles):
                        for j in range(split.widths[i] // P):
                            last = pe.transpose(ps[:, 2 + t, j * P:(j + 1) * P], h[:, t, j * P:(j + 1) * P], ident)
                    last.then_inc(S["t_full"], 1)

                for c, (u, at_, n, ends) in enumerate(split.pieces):
                    kind, i = split.order[u]
                    s, width = slot_of(u), split.widths[i]
                    if kind == "up" and i and at_ == 0:
                        pe.wait_ge(S["hid_made"], i)
                    if kind == "down" and at_ == 0:
                        pe.wait_ge(S["hid_made"], i + 1)
                    pe.wait_ge(S["lo_made"], c + 1)
                    hi, lo = w_hi[:, c % HI_SLOTS, 0:n], w_lo[s][:, at_:at_ + n]
                    for t in range(tiles):
                        if kind == "down":
                            j = at_ // D
                            a_hi, a_lo = (a[:, hidden_in(i, tiles), :][:, t, j * P:(j + 1) * P] for a in (hid_hi, hid_lo))
                            for half in range(2):
                                cs_ = slice(half * N, (half + 1) * N)
                                start, stop = i == 0 and j == 0, i == n_panels - 1 and ends
                                pe.matmul(acc(t, half), a_hi, hi[:, cs_], start=start, stop=False)
                                pe.matmul(acc(t, half), a_hi, lo[:, cs_], start=False, stop=False)
                                last = pe.matmul(acc(t, half), a_lo, hi[:, cs_], start=False, stop=stop)
                        else:
                            b = ps[:, (0 if kind == "gate" else 2) + t, 0:width]
                            for j in range(n // width):
                                kk = at_ // width + j
                                a_hi, a_lo = lhs(kk, t)
                                cs_ = slice(j * width, (j + 1) * width)
                                pe.matmul(b, a_hi, hi[:, cs_], start=(kk == 0), stop=False)
                                pe.matmul(b, a_hi, lo[:, cs_], start=False, stop=False)
                                last = pe.matmul(b, a_lo, hi[:, cs_], start=False, stop=(kk == KD - 1))
                    last.then_inc(S["panel_done" if ends else "piece_used"], 1)
                    if at_ == 0:
                        release()
                    if ends:
                        unreleased.append((s, S["panel_done"], u + 1))
                        if kind == "up" and i == 0:
                            if before_turn:
                                before_turn()
                            turn_hidden(0)
                        if kind == "up" and i == n_panels - 1 and before_down:
                            before_down()
                            turn_hidden(i)
                        if kind == "down" and i + 1 < n_panels - (1 if before_down else 0):
                            turn_hidden(i + 1)
                release()

            pe.wait_ge(const_in, 48)
            pe.wait_ge(setup_done, 4)

            with pe.Fori(0, DEPTH) as L:
                turn[0] = 0
                use = [0]

                def panel(name):
                    assert PANELS[use[0]][0] == name, (PANELS[use[0]], name)
                    s, n = use[0] % RING, use[0] // RING
                    src, width = PANELS[use[0]][1], PANELS[use[0]][3]
                    use[0] += 1
                    pe.wait_ge(ring_full[s], L * (16 * (LAYER_USES // RING)) + 16 * (n + 1))
                    return s, slot_view(s, chunks_of.get(src, KD), width), width

                def project(name, lhs):
                    s, w, width = panel(name)
                    for t in range(NT):
                        b = bank(f"{name}{t}")
                        for kk in range(KD):
                            last = pe.matmul(b[:, 0:width], lhs(kk, t), w[:, kk, :], start=(kk == 0), stop=(kk == KD - 1))
                        done(last)
                        if t == 0:
                            release()
                    unreleased.append((s, bank_full, turn[0]))

                def close_part(br, i, y, ready):
                    if i == 1:
                        for t in range(NT):
                            ready(t)
                            for hh in range(2):
                                turn_over(f"yT_{br}{t}{hh}",
                                          [y[:, t, c * P:(c + 1) * P] for c in range(4 * hh, 4 * hh + 4)])
                        return
                    what, n = (("gate", 0), None, ("br", 0), ("gate", 1), ("br", 1))[i]
                    if i == 2:
                        for t in range(NT):
                            for hh in range(2):
                                given(pe, f"yT_{br}{t}{hh}")
                    project(f"{what}_{br}{n}", htile if what == "gate" else ytile)

                begin(pe, L + 1)
                pe.wait_ge(vec_in, 160)
                done(pe.transpose(bank("vec")[:, 0:P], vec[:, :], ident))
                for t in range(NT):
                    pe.wait_ge(S["normed"], t + 1)
                    for hh in range(2):
                        turn_over(f"ht{t}{hh}", [xn[:, t, c * P:(c + 1) * P] for c in range(4 * hh, 4 * hh + 4)])
                for t in range(NT):
                    for hh in range(2):
                        given(pe, f"ht{t}{hh}")
                for n in range(3):
                    s, w, _ = panel(f"xbc{n}")
                    for i in range(2):
                        b = bank(f"xbc{2 * n + i}")
                        for j in range(2):
                            c = (2 * i + j) * P
                            for kk in range(KD):
                                last = pe.matmul(b[:, j * NT * P:(j + 1) * NT * P], w[:, kk, c:c + P], hT[:, kk, :],
                                                 start=(kk == 0), stop=(kk == KD - 1))
                        done(last)
                        release()
                    unreleased.append((s, bank_full, turn[0]))
                pe.wait_ge(small_in, 112)
                b = bank("dt")
                for t in range(NT):
                    for kk in range(KD):
                        last = pe.matmul(b[:, t * HEADS:(t + 1) * HEADS], htile(kk, t), w_dt[:, kk, :],
                                         start=(kk == 0), stop=(kk == KD - 1))
                done(last)
                project("lat", htile)
                project("z0", htile)
                project("z1", htile)
                pe.wait_ge(S["adt_made"], 1)
                b = bank("cs")
                for c in range(NT):
                    pe.matmul(b[:, c * HEADS:(c + 1) * HEADS], tri, adt[:, c, :], start=True, stop=True)
                for c in range(NT):
                    last = pe.matmul(b[:, (2 + c) * HEADS:(3 + c) * HEADS], ones[:], adt[:, c, :],
                                     start=True, stop=True)
                done(last)
                pe.wait_ge(S["silu_made"], 6)
                for t in range(NT):
                    for hh in range(2):
                        turn_over(f"xt{t}{hh}", [xc[:, c, t * P:(t + 1) * P] for c in range(4 * hh, 4 * hh + 4)])
                turn_over("bt", [xc[:, 8 + g, 0:P] for g in range(2)])
                b = bank("cb")
                for c in range(NT):
                    for g in range(2):
                        at = (2 * c + g) * P
                        last = pe.matmul(b[:, at:at + P], xc[:, 8 + g, c * P:(c + 1) * P],
                                         xc[:, 10 + g, c * P:(c + 1) * P], start=True, stop=True)
                done(last)
                for t in range(NT):
                    pe.wait_ge(S["lat_normed"], t + 1)
                    turn_over(f"latT{t}", [lat[:, t, c * P:(c + 1) * P] for c in range(3)])
                s, w, _ = panel("uq")
                for t in range(NT):
                    given(pe, f"latT{t}")
                    for n in range(3):
                        b = bank(f"q{t}{n}")
                        for kk in range(2):
                            last = pe.matmul(b[:], latT[:, kk, t * P:(t + 1) * P], w[:, kk, n * N:(n + 1) * N],
                                             start=(kk == 0), stop=(kk == 1))
                        done(last)
                        release()
                unreleased.append((s, bank_full, turn[0]))
                s, w, _ = panel("ukv")
                for t in range(NT):
                    for n in range(4):
                        b = bank(f"kv{t}{n}")
                        done(pe.matmul(b[:], latT[:, 2, t * P:(t + 1) * P], w[:, 0, n * N:(n + 1) * N],
                                       start=True, stop=True))
                        release()
                unreleased.append((s, bank_full, turn[0]))
                project("u0", htile)
                project("u1", htile)
                pe.wait_ge(S["xd_made"], 1)
                given(pe, "bt")
                for g in range(2):
                    done(pe.matmul(bank(f"st{g}")[:], b_tok[:, g, :], xd[:, g * N:(g + 1) * N], start=True, stop=True))
                for g in range(2):
                    given(pe, f"st{g}")
                    done(pe.matmul(bank(f"yo{g}")[:], xc[:, 10 + g, P:2 * P], prev[:, g, :], start=True, stop=True))
                for c in range(NT):
                    for qd in range(4):
                        b = bank(f"rb{c}{qd}")
                        for i in range(4):
                            hh = 4 * qd + i
                            last = pe.matmul(b[:, i * P:(i + 1) * P], adt[:, c, hh:hh + 1].to_broadcast([P, P]), tri,
                                             start=True, stop=True)
                        done(last)
                    project(f"v{c}", htile)
                    pe.wait_ge(S["xs_made"], c + 1)
                    for g in range(2):
                        pe.wait_ge(S["mt_made"], 4 * c + 2 * g + 2)
                        b = bank(f"yd{c}{g}")
                        for i in range(8):
                            hh = 8 * g + i
                            last = pe.matmul(b[:, i * HD:(i + 1) * HD], mt[:, hh // 4, (hh % 4) * P:(hh % 4 + 1) * P],
                                             xs[:, c, hh * HD:(hh + 1) * HD], start=True, stop=True)
                        done(last)
                for i in range(2):
                    turn_over(f"wt{i}", [sgu_raw[:, g, :] for g in range(4 * i, 4 * i + 4)])
                for what, row in (("lng", "ln_g"), ("lnb", "ln_b")):
                    for hh in range(2):
                        b = bank(f"{what}{hh}")
                        for i in range(4):
                            r = ROWS[row] + 4 * hh + i
                            last = pe.matmul(b[:, i * P:(i + 1) * P], ident[:, r:r + 1].to_broadcast([P, P]), vec[:, :],
                                             start=True, stop=True)
                        done(last)
                for i in range(5):
                    close_part("ssd", i, xh, lambda t: pe.wait_ge(S["y_normed"], t + 1))
                for w_no, (name, src) in enumerate((("qT", q), ("kT", k))):
                    for t in range(NT):
                        pe.wait_ge(S["hnorm_made"], 2 * w_no + t + 1)
                        for i in range(4):
                            turn_over(f"{name}{t}{i}",
                                      [src[:, t, hh * QK:(hh + 1) * QK] for hh in range(4 * i, 4 * i + 4)])
                given(pe, "wt0")
                given(pe, "wt1")
                for t in range(NT):
                    pe.wait_ge(S["v_normed"], t + 1)
                    for hh in range(2):
                        b = bank(f"mx{t}{hh}")
                        for i in range(4):
                            g = 4 * hh + i
                            last = pe.matmul(b[:, i * P:(i + 1) * P], sgu_wT[:, g, :], vs[:, t, g * P:(g + 1) * P],
                                             start=True, stop=True)
                        done(last)
                for name in [f"{w}T{t}{i}" for w in "qk" for t in range(NT) for i in range(4)]:
                    given(pe, name)
                for kind, i in attention_order():
                    if kind == "close":
                        close_part("sgu", i, u, lambda t: (given(pe, f"mx{t}0"), given(pe, f"mx{t}1")))
                        continue
                    t, h0, nh = GROUPS[i]
                    blocks = t + 1
                    b = bank(f"{kind}{i}")
                    if kind == "sc":
                        keys = blocks * P
                        for j in range(nh):
                            last = pe.matmul(b[:, j * keys:(j + 1) * keys], qT[0:QK, h0 + j, t * P:(t + 1) * P],
                                             kT[0:QK, h0 + j, 0:keys], start=True, stop=True)
                    elif kind == "pt":
                        pe.wait_ge(S["prob_made"], i + 1)
                        for j in range(4):
                            last = pe.transpose(b[:, j * P:(j + 1) * P], prob[:, i % 2, j * P:(j + 1) * P], ident)
                    else:
                        given(pe, f"pt{i}")
                        for j in range(nh):
                            for kb in range(blocks):
                                at = (j * blocks + kb) * P
                                last = pe.matmul(b[:, j * HD:(j + 1) * HD], probT[:, i % 2, at:at + P],
                                                 v[:, kb, h0 + j, :], start=(kb == 0), stop=(kb == blocks - 1))
                    done(last)
                for i in range(5):
                    close_part("mla", i, o, lambda t: pe.wait_ge(S["o_made"], (4, 12)[t]))
                pe.wait_ge(S["merged_made"], 8)
                for t in range(NT):
                    for hh in range(2):
                        turn_over(f"mT{t}{hh}", [merged[:, t, c * P:(c + 1) * P] for c in range(4 * hh, 4 * hh + 4)])
                for t in range(NT):
                    for hh in range(2):
                        given(pe, f"mT{t}{hh}")
                project("out0", ytile)
                project("out1", ytile)
                release()
                for t in range(NT):
                    pe.wait_ge(S["fnormed"], t + 1)
                    for hh in range(2):
                        turn_over(f"ft{t}{hh}", [fn[:, t, c * P:(c + 1) * P] for c in range(4 * hh, 4 * hh + 4)])
                for b in range(8):
                    pe.wait_ge(bank_free[b], bank_uses[b])
                with pe.If(L < 1):
                    pe.wait_ge(S["hT_lo_made"], 1)
                    ffn(DENSE, NT, dense_slot, lambda kk, t: tuple(a[:, kk, t * P:(t + 1) * P] for a in (hT_hi, hT_lo)),
                        lambda t, half: ps[:, 4 + 2 * t + half])
                pe.wait_ge(bank_full, len(JOBS))
                pe.sem_inc(arrived, 1)

            begin(pe, DEPTH + 1)
            for t in range(NT):
                for kk in range(KD):
                    last = pe.matmul(ps[:, 0, t * EXPERTS:(t + 1) * EXPERTS], htile(kk, t), r_w[:, kk, :],
                                     start=(kk == 0), stop=(kk == KD - 1))
            last.then_inc(S["logits"], 1)
            pe.wait_ge(S["chosen"], 1)
            E8 = EXPERTS
            pe.matmul(ps[:, 1, 0:E8], before, chosen[:, 0, :], start=True, stop=True)
            pe.matmul(ps[:, 1, E8:2 * E8], before, chosen[:, 1, :], start=True, stop=False)
            pe.matmul(ps[:, 1, E8:2 * E8], ones[:], chosen[:, 0, :], start=False, stop=True)
            pe.matmul(ps[:, 1, 2 * E8:3 * E8], ones[:], chosen[:, 0, :], start=True, stop=False)
            pe.matmul(ps[:, 1, 2 * E8:3 * E8], ones[:], chosen[:, 1, :], start=False, stop=True
                      ).then_inc(S["ranks"], 1)

            def gather(picks):
                pe.wait_ge(S["picked"], picks)
                for c in range(KD):
                    for t in range(NT):
                        last = pe.matmul(ps[:, 6 + c // 4, c % 4 * P:(c % 4 + 1) * P], fn[:, t, c * P:(c + 1) * P],
                                         pick[:, t, :], start=(t == 0), stop=(t == NT - 1))
                    if c % 4 == 3:
                        last.then_inc(S["gathered"], 1)

            def scatter():
                for j in range(4):
                    t, half = j // 2, j % 2
                    pe.matmul(ps[:, SCATTER_BANKS[j]], wpickT[:, t, :], ysb[:, half * N:(half + 1) * N],
                              start=True, stop=True).then_inc(S["scattered"], 1)

            def gather_next():
                pe.wait_ge(S["added"], 2)
                gather(1)
                pe.wait_ge(S["picked"], 2)
                for t in range(NT):
                    last = pe.transpose(ps[:, 3, t * P:(t + 1) * P], wpick[:, t, :], ident)
                last.then_inc(S["wpickT_full"], 1)

            gather(1)
            pe.wait_ge(S["gathered"], 2)
            pe.sem_inc(arrived, 1)

            pe.wait_ge(routed, 1)
            n_items = pe.value_load(item_tab[0:1, ITEM_SLOTS:ITEM_SLOTS + 1], min_val=EXPERTS, max_val=MAX_ITEMS)
            with pe.Fori(0, n_items) as item:
                begin(pe, item + (DEPTH + 2))
                ffn(MOE, 1, moe_slot, lambda kk, t: (xg_hi[:, kk, :], xg_lo[:, kk, :]), lambda t, half: ps[:, 4 + half],
                    scatter, gather_next)
                pe.sem_inc(arrived, 1)
            begin(pe, n_items + (DEPTH + 2))
            scatter()

        @block.scalar
        def _(act):
            def copy_out(name, out_ap, in_ap):
                give(name, act.activation(out_ap, in_ap, ACT.Copy))

            def ffn(split, tiles, slot_of, wait_full, at_end=None):
                made = [0]

                def lead(hi, s, at_, n):
                    act.activation(hi, slots[s][:, at_:at_ + n], ACT.Copy).then_inc(S["hi_made"], 1)

                def ready(c, u, first):
                    if first:
                        wait_full(u)
                    hi_free(act, split, c)

                def ahead(upto):
                    split_pieces(act, split, made, upto, slot_of, lead, ready)

                for i, width in enumerate(split.widths):
                    ahead(split.through("gate", i) + AHEAD)
                    wait_panel(act, split, "gate", i)
                    if i:
                        act.wait_ge(S["h_made"], i)
                    act.activation(sg[:, 0:tiles, 0:width], ps[:, 0:tiles, 0:width], ACT.Silu).then_inc(S["sg_made"], 1)
                    ahead(turned_before(split, i, tiles) + AHEAD)
                    act.wait_ge(S["t_full"], i + 1)
                    hidden_free(act, split, i, tiles)
                    act.activation(hid_hi[:, hidden_in(i, tiles), 0:width], ps[:, 2:2 + tiles, 0:width], ACT.Copy
                                   ).then_inc(S["hid_hi_made"], 1)
                ahead(len(split.pieces))
                if at_end:
                    at_end()

            act.wait_ge(const_in, 48)
            act.wait_ge(setup_done, 4)
            with act.Fori(0, DEPTH) as L:
                begin(act, L + 1)
                for t in range(NT):
                    act.activation(vs[:, t, :], x[:, t, :], ACT.Square, accum_out=ss[:, t:t + 1]).then_inc(S["squared"], 1)
                act.wait_ge(S["mean_made"], 1)
                act.activation(rs[:], ss[:], ACT.Sqrt).then_inc(S["rooted"], 1)
                for i in range(7):
                    if i < 6:
                        b = take(act, f"xbc{i}")
                        if i >= 2:
                            act.wait_ge(S["conv_made"], i - 1)
                        copy_out(f"xbc{i}", xin[:, i % 2, :, TAPS - 1:], by(b, h=NT * P))
                    if i:
                        act.wait_ge(S["conv_made"], i)
                        piece_ = xc[:, 2 * i - 2:2 * i, :]
                        act.activation(piece_, piece_, ACT.Silu).then_inc(S["silu_made"], 1)
                act.wait_ge(small_in, 112)
                act.activation(aexp, heads_b[:, 1, :], ACT.Exp).then_inc(S["a_exp"], 1)
                act.wait_ge(S["dt_neg"], 1)
                act.activation(dte, dtv, ACT.Exp).then_inc(act_steps, 1)
                act.wait_ge(act_steps, 1)
                act.activation(dte, dte, ACT.Ln, bias=1.0).then_inc(S["dt_log"], 1)
                for t in range(NT):
                    b = take(act, f"lat{t}")
                    copy_out(f"lat{t}", lat[:, t, :], b[:, 0:LAT])
                for t in range(NT):
                    given(act, f"lat{t}")
                    act.activation(vs[:, t, 0:256], lat[:, t, 0:256], ACT.Square, accum_out=ssl[:, t, 0:1])
                    act.activation(vs[:, t, 256:384], lat[:, t, 256:384], ACT.Square, accum_out=ssl[:, t, 1:2]
                                   ).then_inc(S["latsq_made"], 1)
                act.wait_ge(S["latmean_made"], 1)
                act.activation(rsl, ssl, ACT.Sqrt).then_inc(S["latroot_made"], 1)
                for n in range(2):
                    for t in range(NT):
                        b = take(act, f"z{n}{t}")
                        give(f"z{n}{t}", act.activation(z[:, t, n * N:(n + 1) * N], b, ACT.Silu))
                given(act, "z11")
                act.wait_ge(bank_free[JOB["cs"] % 8], JOB["cs"] // 8 + 1)
                act.activation(expcs, csv[:, 1, :], ACT.Exp).then_inc(S["cs_exp"], 1)
                act.wait_ge(S["tail_made"], 1)
                act.activation(decay, decay, ACT.Exp).then_inc(S["cs_exp"], 1)
                for t in range(NT):
                    for hh in range(2):
                        b = take(act, f"xt{t}{hh}")
                        copy_out(f"xt{t}{hh}", xh[:, t, hh * N:(hh + 1) * N], b)
                for t in range(NT):
                    for n in range(3):
                        b = take(act, f"q{t}{n}")
                        copy_out(f"q{t}{n}", q[:, t, n * N:(n + 1) * N], b)
                for t in range(NT):
                    for n in range(4):
                        b = by(take(act, f"kv{t}{n}"), h=2 * HD)
                        act.activation(by(k[:, t, :], h=QK)[:, 4 * n:4 * n + 4, 0:NOPE], b[:, :, 0:NOPE], ACT.Copy
                                       ).then_inc(S["kv_copied"], 1)
                        copy_out(f"kv{t}{n}", v[:, t, 4 * n:4 * n + 4, :], b[:, :, NOPE:])
                for n in range(2):
                    for t in range(NT):
                        b = take(act, f"u{n}{t}")
                        give(f"u{n}{t}", act.activation(u[:, t, n * N:(n + 1) * N], b, ACT.Gelu))
                for g in range(2):
                    b = take(act, f"st{g}")
                    copy_out(f"st{g}", prev[:, g, :], b)
                for c in range(NT):
                    for qd in range(4):
                        given(act, f"rb{c}{qd}")
                        act.activation(mt[:, qd, :], mt[:, qd, :], ACT.Exp).then_inc(S["decay_made"], 1)
                    for t in range(NT):
                        b = take(act, f"v{c}{t}")
                        give(f"v{c}{t}", act.activation(vs[:, t, c * N:(c + 1) * N], b, ACT.Gelu))
                for t in range(NT):
                    act.wait_ge(S["y_made"], 2 * t + 2)
                    for g in range(2):
                        act.activation(xs[:, t, g * N:(g + 1) * N], xh[:, t, g * N:(g + 1) * N], ACT.Square,
                                       accum_out=ssg[:, t, g:g + 1]).then_inc(S["ysq_made"], 1)
                act.wait_ge(S["ymean_made"], 1)
                act.activation(rsg, ssg, ACT.Sqrt).then_inc(S["yroot_made"], 1)
                act.wait_ge(S["var_made"], 1)
                act.activation(lrs, lss, ACT.Sqrt).then_inc(S["vroot_made"], 1)

                gates = [0]

                def gate_panel(br, n):
                    if gates[0]:
                        act.wait_ge(S["gated"], 2 * gates[0])
                    gates[0] += 1
                    for t in range(NT):
                        b = take(act, f"gate_{br}{n}{t}")
                        give(f"gate_{br}{n}{t}", act.activation(gate[:, t, :], b, ACT.Sigmoid))

                def head_squares(i):
                    src, t = (q, k)[i // 2], i % 2
                    if i == 0:
                        for tt in range(NT):
                            given(act, f"q{tt}2")
                    if i == 2:
                        act.wait_ge(S["kv_copied"], 8)
                        act.wait_ge(S["kpe_made"], 2)
                    if i:
                        act.wait_ge(S["hnorm_made"], i)
                    act.activation(tmp, src[:, t, :], ACT.Square).then_inc(S["hsq_made"], 1)
                    act.wait_ge(S["hmean_made"], i + 1)
                    act.activation(rsh, ssh, ACT.Sqrt).then_inc(S["hroot_made"], 1)

                gate_panel("ssd", 0)
                head_squares(0)
                head_squares(1)
                gate_panel("ssd", 1)
                head_squares(2)
                head_squares(3)
                for name, dst in (("qT", qT), ("kT", kT)):
                    for t in range(NT):
                        for i in range(4):
                            b = take(act, f"{name}{t}{i}")
                            copy_out(f"{name}{t}{i}", dst[0:QK, 4 * i:4 * i + 4, t * P:(t + 1) * P], by(b[0:QK, :], h=P))

                def turned(br):
                    for t in range(NT):
                        for hh in range(2):
                            b = take(act, f"yT_{br}{t}{hh}")
                            copy_out(f"yT_{br}{t}{hh}", yT[:, 4 * hh:4 * hh + 4, t * P:(t + 1) * P], by(b, h=P))

                for kind, i in attention_order():
                    if kind == "sc":
                        t, h0, nh = GROUPS[i]
                        keys = (t + 1) * P
                        act.wait_ge(S["max_made"], i + 1)
                        for j in range(nh):
                            p_ = prob[:, i % 2, j * keys:(j + 1) * keys]
                            e_ = act.activation(p_, p_, ACT.Exp, bias=nmx[:, i % 2, j:j + 1], scale=SCALE,
                                                accum_out=rsum[:, t, h0 + j:h0 + j + 1])
                        e_.then_inc(S["prob_made"], 1)
                    elif kind == "pt":
                        b = take(act, f"pt{i}")
                        if i >= 2:
                            act.wait_ge(bank_full, JOB[f"o{i - 2}"] + 1)
                        copy_out(f"pt{i}", probT[:, i % 2, :], b)
                    elif kind == "close":
                        if i == 1:
                            turned("sgu")
                        elif i in (0, 3):
                            gate_panel("sgu", i // 3)
                gate_panel("mla", 0)
                turned("mla")
                gate_panel("mla", 1)
                for t in range(NT):
                    for hh in range(2):
                        b = take(act, f"mT{t}{hh}")
                        copy_out(f"mT{t}{hh}", yT[:, 4 * hh:4 * hh + 4, t * P:(t + 1) * P], by(b, h=P))
                for t in range(NT):
                    given(act, f"out0{t}")
                    given(act, f"out1{t}")
                    act.activation(fn[:, t, :], x[:, t, :], ACT.Square, accum_out=ss[:, t:t + 1]
                                   ).then_inc(S["fsquared"], 1)
                act.wait_ge(S["fmean_made"], 1)
                act.activation(rs[:], ss[:], ACT.Sqrt).then_inc(S["frooted"], 1)
                with act.If(L < 1):
                    def dense_full(u):
                        act.wait_ge(ring_full[dense_slot(u)], 16 * ((len(PANELS) + u) // RING + 1))

                    for t in range(NT):
                        for hh in range(2):
                            given(act, f"ft{t}{hh}")
                    act.activation(hT_hi[:], hT[:], ACT.Copy).then_inc(S["hT_hi_made"], 1)
                    ffn(DENSE, NT, dense_slot, dense_full)
                act.activation(small[:, 511:512], small[:, 511:512], ACT.Copy).then_inc(act_steps, 1)
                act.wait_ge(act_steps, 2)
                act.sem_inc(arrived, 1)

            begin(act, DEPTH + 1)
            act.wait_ge(S["gap_made"], 1)
            act.activation(route[:, 4, :, 0:1], route[:, 3, :, 0:1], ACT.Exp).then_inc(S["gap_exp"], 1)
            act.wait_ge(S["gap_exp"], 1)

            def lead_tokens():
                act.wait_ge(S["xg_made"], 2)
                act.activation(xg_hi[:], xg, ACT.Copy).then_inc(S["xg_hi_made"], 1)

            def lead_next():
                lead_tokens()
                act.wait_ge(S["wpickT_full"], 1)
                act.wait_ge(S["scattered"], 4)
                act.activation(wpickT, by(ps[:, 3, 0:NT * P], h=P), ACT.Copy).then_inc(S["wpickT_made"], 1)

            lead_tokens()
            act.wait_ge(S["xg_hi_made"], 1)
            act.sem_inc(arrived, 1)
            act.wait_ge(routed, 1)
            n_items = act.value_load(item_tab[0:1, ITEM_SLOTS:ITEM_SLOTS + 1], min_val=EXPERTS, max_val=MAX_ITEMS)
            with act.Fori(0, n_items) as item:
                begin(act, item + (DEPTH + 2))

                def moe_full(u):
                    s = moe_slot(u)
                    act.wait_ge(ring_full[s], item * (16 * ITEM_USES) + 16 * (uses0[s] + u // MOE_RING + 1))

                ffn(MOE, 1, moe_slot, moe_full, lead_next)
                act.wait_ge(S["wpickT_made"], 1)
                act.wait_ge(S["panel_done"], len(MOE.order))
                act.activation(ysb[:, 0:N], ps[:, 4], ACT.Copy).then_inc(S["y_copied"], 1)
                act.wait_ge(S["y_copied"], 2)
                act.sem_inc(arrived, 1)

        @block.vector
        def _(dve):
            chain = Chain(dve, dve_steps)
            mark, link, sync = chain.mark, chain.link, chain.sync

            def ffn(split, tiles, slot_of, after=None, tokens=None):
                made = [0]

                def rest(hi, s, at_, n):
                    dve.tensor_tensor(w_lo[s][:, at_:at_ + n], slots[s][:, at_:at_ + n], hi.bitcast(F32), ALU.subtract
                                      ).then_inc(S["lo_made"], 1)

                def ready(c, u, first):
                    dve.wait_ge(S["hi_made"], c + 1)

                def ahead(upto):
                    split_pieces(dve, split, made, upto, slot_of, rest, ready)

                for i, width in enumerate(split.widths):
                    ahead(split.through("up", i) + AHEAD)
                    dve.wait_ge(S["sg_made"], i + 1)
                    wait_panel(dve, split, "up", i)
                    if i:
                        dve.wait_ge(S["t_full"], i)
                    dve.tensor_tensor(h[:, 0:tiles, 0:width], ps[:, 2:2 + tiles, 0:width], sg[:, 0:tiles, 0:width],
                                      ALU.mult).then_inc(S["h_made"], 1)
                    if tokens and i == len(split.widths) - 1:
                        tokens()
                    ahead(turned_before(split, i, tiles) + AHEAD)
                    hidden_free(dve, split, i, tiles)
                    dve.wait_ge(S["hid_hi_made"], i + 1)
                    dve.tensor_tensor(hid_lo[:, hidden_in(i, tiles), 0:width], ps[:, 2:2 + tiles, 0:width],
                                      hid_hi[:, hidden_in(i, tiles), 0:width].bitcast(F32), ALU.subtract).then_inc(S["hid_made"], 1)
                    if i == len(split.widths) - 1:
                        ahead(len(split.pieces))
                    if after:
                        after(i)

            def root_mean(sums, n, eps, signal):
                dve.tensor_scalar(sums, sums, 1.0 / n, eps, ALU.mult, ALU.add).then_inc(signal, 1)

            dve.wait_ge(const_in, 48)
            dve.wait_ge(setup_done, 4)
            with dve.Fori(0, DEPTH) as L:
                chain.n = 0
                begin(dve, L + 1)
                b = take(dve, "vec")
                give("vec", dve.tensor_copy(cols[:], b[:, 0:N_ROWS]))
                dve.wait_ge(S["squared"], 2)
                root_mean(ss[:], D, EPS, S["mean_made"])
                dve.wait_ge(S["rooted"], 1)
                link(dve.reciprocal(rs[:], rs[:]))
                for t in range(NT):
                    dve.tensor_scalar(xn[:, t, :], x[:, t, :], rs[:, t:t + 1], None, ALU.mult).then_inc(S["normed"], 1)
                given(dve, "vec")
                for t in range(NT):
                    for hh in range(2):
                        b = take(dve, f"ht{t}{hh}")
                        give(f"ht{t}{hh}", dve.tensor_tensor(hT[:, 4 * hh:4 * hh + 4, t * P:(t + 1) * P], by(b, h=P),
                                                             spread(col("mix", 4 * hh, 4), P), ALU.mult))
                for i in range(6):
                    given(dve, f"xbc{i}")
                    for tap in range(TAPS):
                        for j in range(2):
                            c = 2 * i + j
                            src = xin[:, i % 2, j, tap:tap + NT * P]
                            w = col("conv_w", tap * CONV_CHUNKS + c)
                            if tap == 0:
                                mark(dve.tensor_scalar(xc[:, c, :], src, w, col("conv_b", c), ALU.mult, ALU.add))
                            else:
                                ins = dve.scalar_tensor_tensor(xc[:, c, :], src, w, xc[:, c, :], ALU.mult, ALU.add)
                                if tap == TAPS - 1 and j == 1:
                                    ins.then_inc(S["conv_made"], 1)
                                else:
                                    mark(ins)
                        if tap < TAPS - 1:
                            sync()
                dve.wait_ge(small_in, 112)
                b = take(dve, "dt")
                give("dt", dve.tensor_tensor(dtr, by(b[:, 0:NT * HEADS], h=HEADS), repeat(heads_b[:, 0, :], NT), ALU.add))
                given(dve, "dt")
                dve.scalar_tensor_tensor(dtv, dtr, -1.0, dtr, ALU.mult, ALU.min).then_inc(S["dt_neg"], 1)
                dve.wait_ge(S["dt_neg"], 1)
                dve.wait_ge(S["dt_log"], 1)
                link(dve.scalar_tensor_tensor(dtr, dtr, 0.0, dte, ALU.max, ALU.add))
                dve.wait_ge(S["a_exp"], 1)
                dve.scalar_tensor_tensor(adt, dtr, -1.0, repeat(aexp, NT), ALU.mult, ALU.mult).then_inc(S["adt_made"], 1)
                dve.wait_ge(S["latsq_made"], 2)
                link(dve.tensor_scalar(ssl[:, :, 0:1], ssl[:, :, 0:1], 1.0 / 256, EPS, ALU.mult, ALU.add))
                root_mean(ssl[:, :, 1:2], P, EPS, S["latmean_made"])
                dve.wait_ge(S["latroot_made"], 1)
                link(dve.reciprocal(rsl, rsl))
                for t in range(NT):
                    mark(dve.tensor_scalar(lat[:, t, 0:256], lat[:, t, 0:256], rsl[:, t, 0:1], None, ALU.mult))
                    dve.tensor_scalar(lat[:, t, 256:384], lat[:, t, 256:384], rsl[:, t, 1:2], None, ALU.mult
                                      ).then_inc(S["lat_normed"], 1)
                    dve.tensor_copy(by(k[:, t, :], h=QK)[:, :, NOPE:], repeat(lat[:, t, 384:LAT], HEADS)
                                    ).then_inc(S["kpe_made"], 1)
                b = take(dve, "cs")
                give("cs", dve.tensor_copy(csv, by(b[:, 0:4 * HEADS], h=HEADS)))
                given(dve, "cs")
                dve.tensor_tensor(decay, csv[:, 2, :], csv[:, 0, :], ALU.subtract).then_inc(S["tail_made"], 1)
                for t in range(NT):
                    given(dve, f"xt{t}0")
                    given(dve, f"xt{t}1")
                    dve.tensor_tensor(by(xs[:, t, :], h=HD), by(xh[:, t, :], h=HD), spread(dtr[:, t, :], HD), ALU.mult
                                      ).then_inc(S["xs_made"], 1)
                b = take(dve, "bt")
                give("bt", dve.tensor_copy(b_tok, by(b[:, 0:2 * P], h=P)))
                b = take(dve, "cb")
                give("cb", dve.tensor_tensor(cbm, by(b, h=P), repeat(tri, 4), ALU.mult))
                for t in range(NT):
                    b = take(dve, f"latT{t}")
                    give(f"latT{t}", dve.tensor_tensor(latT[:, :, t * P:(t + 1) * P], by(b[:, 0:3 * P], h=P),
                                                       spread(col("q", 0, 3), P), ALU.mult))
                dve.wait_ge(S["cs_exp"], 2)
                dve.wait_ge(S["xs_made"], 2)
                dve.tensor_tensor(by(xd, h=HD), by(xs[:, 0, :], h=HD), spread(decay, HD), ALU.mult
                                  ).then_inc(S["xd_made"], 1)
                for t in range(NT):
                    mark(dve.tensor_tensor(by(xh[:, t, :], h=HD), by(xh[:, t, :], h=HD), spread(heads_b[:, 2, :], HD),
                                           ALU.mult))
                sync()
                for g in range(2):
                    b = take(dve, f"yo{g}")
                    give(f"yo{g}", dve.tensor_tensor(by(xd[:, g * N:(g + 1) * N], h=HD), by(b, h=HD),
                                                     spread(expcs[:, 8 * g:8 * g + 8], HD), ALU.mult))
                for g in range(2):
                    given(dve, f"yo{g}")
                    cut = xh[:, 1, g * N:(g + 1) * N]
                    mark(dve.tensor_tensor(cut, cut, xd[:, g * N:(g + 1) * N], ALU.add))
                given(dve, "cb")
                for c in range(NT):
                    for qd in range(5):
                        if qd < 4:
                            b = take(dve, f"rb{c}{qd}")
                            if c:
                                dve.wait_ge(bank_full, JOB[f"yd0{qd // 2}"] + 1)
                            for i in range(4):
                                hh = 4 * qd + i
                                ins = dve.tensor_scalar(mt[:, qd, i * P:(i + 1) * P], b[:, i * P:(i + 1) * P],
                                                        csv[:, c, hh:hh + 1], 0.0, ALU.subtract, ALU.min)
                                if i == 3:
                                    give(f"rb{c}{qd}", ins)
                        if qd:
                            dve.wait_ge(S["decay_made"], 4 * c + qd)
                            m = by(mt[:, qd - 1, :], h=P)
                            dve.tensor_tensor(m, m, repeat(cbm[:, 2 * c + (qd - 1) // 2, :], 4), ALU.mult
                                              ).then_inc(S["mt_made"], 1)
                    if c == 0:
                        pass
                    sync()
                    for g in range(2):
                        cut = xh[:, c, g * N:(g + 1) * N]
                        b = take(dve, f"yd{c}{g}")
                        give(f"yd{c}{g}", dve.tensor_tensor(cut, b, cut, ALU.add))
                        given(dve, f"yd{c}{g}")
                        for n in range(2):
                            given(dve, f"z{n}{c}")
                        dve.tensor_tensor(cut, cut, z[:, c, g * N:(g + 1) * N], ALU.mult).then_inc(S["y_made"], 1)
                for i in range(2):
                    b = take(dve, f"wt{i}")
                    give(f"wt{i}", dve.tensor_tensor(sgu_wT[:, 4 * i:4 * i + 4, :], by(b, h=P), repeat(tri, 4), ALU.mult))
                dve.wait_ge(S["ysq_made"], 4)
                root_mean(ssg, N, EPS, S["ymean_made"])
                for t in range(NT):
                    for n in range(2):
                        given(dve, f"v{n}{t}")
                        mark(dve.bn_stats(bn[:, t, n, :], vs[:, t, n * N:(n + 1) * N]))
                sync()
                for t in range(NT):
                    mark(dve.bn_aggr(mv[:, t, :], bn[:, t, :, :].rearrange("p a b -> p (a b)")))
                sync()
                dve.tensor_scalar(by(lss, h=1), mv[:, :, 1:2], LN_EPS, None, ALU.add).then_inc(S["var_made"], 1)
                dve.wait_ge(S["yroot_made"], 1)
                link(dve.reciprocal(rsg, rsg))
                for t in range(NT):
                    for g in range(2):
                        cut = xh[:, t, g * N:(g + 1) * N]
                        ins = dve.tensor_scalar(cut, cut, rsg[:, t, g:g + 1], None, ALU.mult)
                        if g:
                            ins.then_inc(S["y_normed"], 1)
                dve.wait_ge(S["vroot_made"], 1)
                link(dve.reciprocal(lrs, lrs))
                for t in range(NT):
                    mark(dve.tensor_scalar(vs[:, t, :], vs[:, t, :], mv[:, t, 0:1], lrs[:, t:t + 1],
                                           ALU.subtract, ALU.mult))
                sync()
                for what, op in (("lng", ALU.mult), ("lnb", ALU.add)):
                    for hh in range(2):
                        b = take(dve, f"{what}{hh}")
                        for t in range(NT):
                            if what == "lnb":
                                given(dve, f"lng{hh}")
                            cut = vs[:, t, hh * N:(hh + 1) * N]
                            ins = dve.tensor_tensor(cut, b, cut, op)
                            if t == 1:
                                give(f"{what}{hh}", ins)
                            else:
                                mark(ins)
                    sync()
                given(dve, "lnb0")
                given(dve, "lnb1")
                dve.tensor_copy(small[:, 510:511], mv[:, 0, 0:1]).then_inc(S["v_normed"], 2)
                for t in range(NT):
                    for hh in range(2):
                        b = take(dve, f"yT_ssd{t}{hh}")
                        give(f"yT_ssd{t}{hh}", dve.tensor_tensor(yT[:, 4 * hh:4 * hh + 4, t * P:(t + 1) * P], by(b, h=P),
                                                                 spread(col("ssd", 4 * hh, 4), P), ALU.mult))

                def merge(br, n):
                    for t in range(NT):
                        b = take(dve, f"br_{br}{n}{t}")
                        given(dve, f"gate_{br}{n}{t}")
                        cut = merged[:, t, n * N:(n + 1) * N]
                        if br == "ssd":
                            give(f"br_{br}{n}{t}", dve.tensor_tensor(cut, b, gate[:, t, :], ALU.mult))
                            given(dve, f"br_{br}{n}{t}")
                            dve.tensor_copy(small[:, 509:510], small[:, 510:511]).then_inc(S["gated"], 1)
                        else:
                            give(f"br_{br}{n}{t}", dve.tensor_tensor(gate[:, t, :], b, gate[:, t, :], ALU.mult))
                            given(dve, f"br_{br}{n}{t}")
                            dve.tensor_tensor(cut, cut, gate[:, t, :], ALU.add).then_inc(S["gated"], 1)

                def head_norm(i):
                    src, t = (q, k)[i // 2], i % 2
                    a = by(src[:, t, :], h=QK)
                    dve.wait_ge(S["hsq_made"], i + 1)
                    link(dve.tensor_reduce(ssh, by(tmp, h=QK), AX.X, ALU.add))
                    root_mean(ssh, QK, EPS, S["hmean_made"])
                    dve.wait_ge(S["hroot_made"], i + 1)
                    link(dve.reciprocal(rsh, rsh))
                    link(dve.tensor_tensor(a, a, spread(rsh, QK), ALU.mult))
                    link(dve.tensor_tensor(a, a, repeat(gain_b[:, i // 2, :], HEADS), ALU.mult))
                    x1, x2 = a[:, :, NOPE:NOPE + HALF_ROPE], a[:, :, NOPE + HALF_ROPE:QK]
                    cs_, sn_ = repeat(cos[:, t, :], HEADS), repeat(sin[:, t, :], HEADS)
                    r = tmp[:, 0:4 * HEADS * HALF_ROPE].rearrange("p (a h c) -> p a h c", a=4, h=HEADS)
                    for j, (m, n) in enumerate(((x1, cs_), (x2, sn_), (x1, sn_), (x2, cs_))):
                        mark(dve.tensor_tensor(r[:, j], m, n, ALU.mult))
                    sync()
                    mark(dve.tensor_tensor(x1, r[:, 0], r[:, 1], ALU.subtract))
                    dve.tensor_tensor(x2, r[:, 2], r[:, 3], ALU.add).then_inc(S["hnorm_made"], 1)

                head_norm(0)
                head_norm(1)
                merge("ssd", 0)
                head_norm(2)
                head_norm(3)
                merge("ssd", 1)
                for t in range(NT):
                    for n in range(2):
                        given(dve, f"u{n}{t}")
                    for hh in range(2):
                        b = take(dve, f"mx{t}{hh}")
                        for i in range(4):
                            g = 4 * hh + i
                            cut = u[:, t, g * P:(g + 1) * P]
                            ins = dve.scalar_tensor_tensor(cut, b[:, i * P:(i + 1) * P], col("sgu_b", g), cut,
                                                           ALU.add, ALU.mult)
                            if i == 3:
                                give(f"mx{t}{hh}", ins)
                for kind, i in attention_order():
                    if kind == "close":
                        if i in (2, 4):
                            merge("sgu", i // 2 - 1)
                        continue
                    if kind == "pt":
                        continue
                    t, h0, nh = GROUPS[i]
                    keys = (t + 1) * P
                    if kind == "sc":
                        b = take(dve, f"sc{i}")
                        if i >= 2:
                            dve.wait_ge(bank_full, JOB[f"pt{i - 2}"] + 1)
                        pr = by(prob[:, i % 2, :], h=keys)
                        give(f"sc{i}", dve.tensor_tensor(pr, by(b, h=keys), repeat(mask[:, 2 * P - keys:], nh), ALU.add))
                        given(dve, f"sc{i}")
                        link(dve.tensor_reduce(mx[:, 0:nh], pr, AX.X, ALU.max))
                        if i >= 2:
                            dve.wait_ge(S["prob_made"], i - 1)
                        dve.tensor_scalar(nmx[:, i % 2, 0:nh], mx[:, 0:nh], -SCALE, None, ALU.mult
                                          ).then_inc(S["max_made"], 1)
                        dve.wait_ge(S["max_made"], i + 1)
                    else:
                        dve.wait_ge(S["prob_made"], i + 1)
                        link(dve.reciprocal(rinv[:, t, h0:h0 + nh], rsum[:, t, h0:h0 + nh]))
                        b = take(dve, f"o{i}")
                        give(f"o{i}", dve.tensor_tensor(by(o[:, t, h0 * HD:(h0 + nh) * HD], h=HD), by(b[:, 0:nh * HD], h=HD),
                                                        spread(rinv[:, t, h0:h0 + nh], HD), ALU.mult))
                        given(dve, f"o{i}")
                        dve.tensor_copy(small[:, 509:510], small[:, 510:511]).then_inc(S["o_made"], 1)
                merge("mla", 0)
                merge("mla", 1)
                dve.wait_ge(S["gated"], 12)
                dve.tensor_copy(small[:, 509:510], small[:, 510:511]).then_inc(S["merged_made"], 8)
                for n in range(2):
                    for t in range(NT):
                        b = take(dve, f"out{n}{t}")
                        cut = x[:, t, n * N:(n + 1) * N]
                        give(f"out{n}{t}", dve.tensor_tensor(cut, b, cut, ALU.add))
                dve.wait_ge(S["fsquared"], 2)
                root_mean(ss[:], D, EPS, S["fmean_made"])
                dve.wait_ge(S["frooted"], 1)
                link(dve.reciprocal(rs[:], rs[:]))
                for t in range(NT):
                    dve.tensor_scalar(fn[:, t, :], x[:, t, :], rs[:, t:t + 1], None, ALU.mult).then_inc(S["fnormed"], 1)
                for t in range(NT):
                    for hh in range(2):
                        b = take(dve, f"ft{t}{hh}")
                        give(f"ft{t}{hh}", dve.tensor_tensor(hT[:, 4 * hh:4 * hh + 4, t * P:(t + 1) * P], by(b, h=P),
                                                             spread(col("ffn", 4 * hh, 4), P), ALU.mult))
                steps = chain.n
                with dve.If(L < 1):
                    dve.wait_ge(S["hT_hi_made"], 1)
                    dve.tensor_tensor(hT_lo[:], hT[:], hT_hi[:].bitcast(F32), ALU.subtract).then_inc(S["hT_lo_made"], 1)
                    ffn(DENSE, NT, dense_slot)
                    dve.wait_ge(S["panel_done"], len(DENSE.order))
                    for t in range(NT):
                        for half in range(2):
                            cut = x[:, t, half * N:(half + 1) * N]
                            dve.tensor_tensor(cut, ps[:, 4 + 2 * t + half], cut, ALU.add)
                assert chain.n == steps
                link(dve.tensor_copy(small[:, 509:510], small[:, 510:511]))
                dve.sem_inc(arrived, 1)

            chain.n = 0
            begin(dve, DEPTH + 1)

            def r(n):
                return route[:, n]

            expert2 = by(cst("expert", NT * EXPERTS), h=EXPERTS)
            dve.wait_ge(S["logits"], 1)
            link(dve.tensor_copy(r(0), by(ps[:, 0, 0:NT * EXPERTS], h=EXPERTS)))
            m1, m2, low = (r(n)[:, :, 0:1] for n in (1, 2, 5))

            def wide(a):
                return a.to_broadcast([P, NT, EXPERTS])

            def choose(logits, top, out_):
                link(dve.tensor_reduce(top, logits, AX.X, ALU.max))
                link(dve.tensor_tensor(r(6), logits, wide(top), ALU.is_equal))
                link(dve.scalar_tensor_tensor(r(7), expert2, float(EXPERTS), r(6), ALU.subtract, ALU.mult))
                link(dve.tensor_reduce(low, r(7), AX.X, ALU.min))
                link(dve.tensor_tensor(out_, r(7), wide(low), ALU.is_equal))

            choose(r(0), m1, r(8))
            link(dve.scalar_tensor_tensor(r(9), r(8), -1e30, r(0), ALU.mult, ALU.add))
            choose(r(9), m2, r(10))
            dve.tensor_tensor(r(3)[:, :, 0:1], m2, m1, ALU.subtract).then_inc(S["gap_made"], 1)
            dve.tensor_tensor(chosen, r(8), r(10), ALU.add).then_inc(S["chosen"], 1)
            e_, w1, w2 = r(4)[:, :, 0:1], r(4)[:, :, 1:2], r(4)[:, :, 2:3]
            dve.wait_ge(S["gap_exp"], 1)
            link(dve.tensor_scalar(w1, e_, 1.0, None, ALU.add))
            link(dve.reciprocal(w1, w1))
            link(dve.tensor_tensor(w2, e_, w1, ALU.mult))
            mark(dve.tensor_tensor(r(8), r(8), wide(w1), ALU.mult))
            mark(dve.tensor_tensor(r(10), r(10), wide(w2), ALU.mult))
            sync()
            link(dve.tensor_tensor(r(9), r(8), r(10), ALU.add))
            dve.wait_ge(S["ranks"], 1)
            E8 = EXPERTS
            link(dve.tensor_scalar(r(0), by(ps[:, 1, 0:NT * E8], h=E8), 1.0, None, ALU.add))
            link(dve.tensor_tensor(r(0), r(0), chosen, ALU.mult))
            link(dve.tensor_scalar(r(0), r(0), -1.0, None, ALU.add))
            big, start = r(6)[:, 0, :], r(6)[:, 1, :]
            link(dve.tensor_scalar(big, ps[:, 1, 2 * E8:3 * E8], float(P), None, ALU.is_gt))
            link(dve.tensor_copy(start, cst("expert", E8)))
            for e in range(1, E8):
                link(dve.tensor_tensor(start[:, e:E8], start[:, e:E8], big[:, e - 1:e].to_broadcast([P, E8 - e]), ALU.add))
            grid = [by(items[:, n, :], h=E8) for n in range(8)]
            number = by(cst("item", ITEM_SLOTS * E8), h=E8)
            which = by(cst("expert", ITEM_SLOTS * E8), h=E8)
            expert_of = items[:, 4, 0:ITEM_SLOTS]
            block_of = items[:, 5, 0:ITEM_SLOTS]
            mark(dve.tensor_tensor(grid[0], number, repeat(start, ITEM_SLOTS), ALU.is_ge))
            mark(dve.tensor_tensor(grid[1], number, repeat(start, ITEM_SLOTS), ALU.is_equal))
            sync()
            mark(dve.tensor_reduce(expert_of, grid[0], AX.X, ALU.add))
            mark(dve.tensor_reduce(block_of, grid[1], AX.X, ALU.add))
            sync()
            mark(dve.tensor_scalar(expert_of, expert_of, -1.0, None, ALU.add))
            mark(dve.tensor_scalar(block_of, block_of, -float(P), float(P), ALU.mult, ALU.add))
            sync()
            link(dve.tensor_tensor(grid[2], which, spread(expert_of, E8), ALU.is_equal))
            for t in range(NT):
                link(dve.tensor_tensor(grid[3], grid[2], repeat(r(0)[:, t, :], ITEM_SLOTS), ALU.mult))
                link(dve.tensor_reduce(pos_item[:, t, :], grid[3], AX.X, ALU.add))
                link(dve.tensor_tensor(pos_item[:, t, :], pos_item[:, t, :], block_of, ALU.subtract))
                link(dve.tensor_tensor(grid[3], grid[2], repeat(r(9)[:, t, :], ITEM_SLOTS), ALU.mult))
                link(dve.tensor_reduce(w_item[:, t, :], grid[3], AX.X, ALU.add))
            link(dve.tensor_reduce(items[:, 6, 0:1], big, AX.X, ALU.add))
            link(dve.tensor_scalar(items[:, 6, 0:1], items[:, 6, 0:1], float(EXPERTS), None, ALU.add))
            link(dve.tensor_copy(item_tab[0:1, 0:ITEM_SLOTS], expert_of[0:1, :]))
            dve.tensor_copy(item_tab[0:1, ITEM_SLOTS:ITEM_SLOTS + 1], items[0:1, 6, 0:1]).then_inc(routed, 1)

            def pick_tokens(i):
                for t in range(NT):
                    ins = dve.tensor_scalar(pick[:, t, :], slot_no, pos_item[:, t, i], None, ALU.is_equal)
                ins.then_inc(S["picked"], 1)

            def take_tokens():
                for hh in range(2):
                    dve.wait_ge(S["gathered"], hh + 1)
                    dve.tensor_tensor(xg[:, 4 * hh:4 * hh + 4, :], by(ps[:, 6 + hh], h=P), spread(col("ffn", 4 * hh, 4), P),
                                      ALU.mult).then_inc(S["xg_made"], 1)

            def rest_of_tokens():
                dve.wait_ge(S["xg_hi_made"], 1)
                dve.tensor_tensor(xg_lo[:], xg, xg_hi[:].bitcast(F32), ALU.subtract).then_inc(S["xg_lo_made"], 1)

            def add_outputs(signal):
                for j in range(4):
                    t, half = j // 2, j % 2
                    dve.wait_ge(S["scattered"], j + 1)
                    cut = x[:, t, half * N:(half + 1) * N]
                    ins = dve.tensor_tensor(cut, ps[:, SCATTER_BANKS[j]], cut, ALU.add)
                    if half:
                        ins.then_inc(signal, 1)

            pick_tokens(slice(0, 1))
            dve.memset(ysb, 0.0)
            dve.memset(wpickT, 0.0).then_inc(S["zeroed"], 1)
            take_tokens()
            rest_of_tokens()
            dve.wait_ge(S["zeroed"], 1)
            dve.wait_ge(S["xg_lo_made"], 1)
            dve.wait_ge(routed, 1)
            n_items = dve.value_load(item_tab[0:1, ITEM_SLOTS:ITEM_SLOTS + 1], min_val=EXPERTS, max_val=MAX_ITEMS)
            dve.sem_inc(arrived, 1)

            with dve.Fori(0, n_items) as item:
                begin(dve, item + (DEPTH + 2))

                def after(i):
                    if i == 0:
                        add_outputs(S["added"])
                    if i == len(MOE_PANELS) - 3:
                        pick_tokens(bass.ds(item + 1, 1))
                        for t in range(NT):
                            ins = dve.tensor_scalar(wpick[:, t, :], slot_no, pos_item[:, t, bass.ds(item, 1)],
                                                    w_item[:, t, bass.ds(item, 1)], ALU.is_equal, ALU.mult)
                        ins.then_inc(S["picked"], 1)
                    if i == len(MOE_PANELS) - 1:
                        rest_of_tokens()

                ffn(MOE, 1, moe_slot, after, take_tokens)
                dve.wait_ge(S["xg_lo_made"], 1)
                dve.wait_ge(S["panel_done"], len(MOE.order))
                dve.tensor_copy(ysb[:, N:2 * N], ps[:, 5]).then_inc(S["y_copied"], 1)
                dve.wait_ge(S["y_copied"], 2)
                dve.sem_inc(arrived, 1)
            begin(dve, n_items + (DEPTH + 2))
            add_outputs(finished)


_INS = ["x", "mix_norm_g", "w_in", "conv_w", "conv_b", "dt_bias", "a_log", "d_skip", "ssd_norm_g", "sgu_ln_g",
        "sgu_ln_b", "sgu_w", "sgu_b", "q_norm_g", "w_uq", "kv_norm_g", "w_ukv", "q_head_g", "k_head_g", "w_br_ssd",
        "w_br_sgu", "w_br_mla", "w_out", "ffn_norm_g", "ffn_w_gate", "ffn_w_up", "ffn_w_down", "router_w",
        "moe_w_gate", "moe_w_up", "moe_w_down"]


def constant_table():
    import numpy as np

    c = np.zeros((P, N_CONST), np.float32)
    p, f = np.arange(P)[:, None], np.arange(P)[None, :]
    c[:, CONST["ident"]:][:, :P] = p == f
    c[:, CONST["tri"]:][:, :P] = p <= f
    c[:, CONST["before"]:][:, :P] = p < f
    c[:, CONST["slot"]:][:, :P] = f
    c[:, CONST["mask"] + P:][:, :P] = np.where(f <= p, 0.0, -1e30)
    inv = (1.0 / (np.float32(10000.0) ** (np.arange(0, 2 * HALF_ROPE, 2, dtype=np.float32) / np.float32(2 * HALF_ROPE)))
           ).astype(np.float32)
    for t in range(NT):
        ang = ((t * P + np.arange(P)).astype(np.float32)[:, None] * inv[None, :]).astype(np.float32)
        c[:, CONST["cos"] + HALF_ROPE * t:][:, :HALF_ROPE] = np.cos(ang)
        c[:, CONST["sin"] + HALF_ROPE * t:][:, :HALF_ROPE] = np.sin(ang)
    i = np.arange(ITEM_SLOTS * EXPERTS)
    c[:, CONST["item"]:][:, :i.size] = i // EXPERTS
    c[:, CONST["expert"]:][:, :i.size] = i % EXPERTS
    return c


def kernel(**inputs):
    import numpy as np
    import concourse.bacc as bacc
    from concourse.bass_utils import run_bass_kernel_spmd as run

    nc = bacc.Bacc("TRN2", target_bir_lowering=False, num_devices=1)
    arrays, aps = {}, {}
    for name in _INS + ["const"]:
        a = constant_table() if name == "const" else np.ascontiguousarray(inputs[name])
        arrays[f"in_{name}"] = a
        aps[name] = nc.dram_tensor(f"in_{name}", a.shape, mybir.dt.from_np(a.dtype), kind="ExternalInput").ap()
    out = nc.dram_tensor("out_0", (1, NT * P, D), F32, kind="ExternalOutput").ap()
    hybrid_trunk(nc, aps, out)
    return run(nc, [arrays], core_ids=[0]).results[0]["out_0"]
```

```python
from contextlib import ExitStack

import concourse.bass as bass
from concourse import mybir

ALU = mybir.AluOpType
ACT = mybir.ActivationFunctionType
F32 = mybir.dt.float32
I32 = mybir.dt.int32
F32R = mybir.dt.float32r
AX = mybir.AxisListType

P = 128
NT = 2
D = 1024
KD = D // P
DEPTH = 2
HEADS = 16
HD = 64
QK = 96
NOPE = 64
HALF_ROPE = 16
CONV_CHUNKS = 12
TAPS = 4
EPS = 1e-6
LN_EPS = 1e-5
SCALE = QK ** -0.5
N = 512
SLOT = KD * N
FFN_DENSE = 2816
FFN_EXPERT = 3584
EXPERTS = 8
MAX_ITEMS = 11
ITEM_SLOTS = 16

C_Z, C_XBC, C_DT, C_U, C_V, C_LAT, C_GATE = 0, 1024, 2560, 2576, 3600, 4624, 5040
LAT = 416

ROWS = {}
_at = 0
for _name, _n in (("mix", 8), ("ffn", 8), ("conv_b", 12), ("conv_w", 48), ("ssd", 8), ("q", 2), ("kv", 1),
                  ("sgu_b", 8), ("ln_g", 8), ("ln_b", 8)):
    ROWS[_name] = _at
    _at += _n
N_ROWS = _at

CONST = {}
_at = 0
for _name, _n in (("ident", P), ("tri", P), ("before", P), ("slot", P), ("mask", 2 * P), ("cos", 2 * HALF_ROPE),
                  ("sin", 2 * HALF_ROPE), ("item", ITEM_SLOTS * EXPERTS), ("expert", ITEM_SLOTS * EXPERTS)):
    CONST[_name] = _at
    _at += _n
N_CONST = _at


def mixer_panels():
    out = [(f"xbc{n}", "in", C_XBC + N * n, N) for n in range(3)]
    out += [("lat", "in", C_LAT, LAT)]
    out += [("u0", "in", C_U, N)]
    out += [("uq", "uq", 0, HEADS * QK), ("ukv", "ukv", 0, HEADS * 2 * HD)]
    out += [("u1", "in", C_U + N, N)]
    out += [(f"v{n}", "in", C_V + N * n, N) for n in range(2)]
    out += [(f"z{n}", "in", C_Z + N * n, N) for n in range(2)]
    for b, br in enumerate(("ssd", "sgu", "mla")):
        for n in range(2):
            out += [(f"gate_{br}{n}", "in", C_GATE + D * b + N * n, N), (f"br_{br}{n}", br, N * n, N)]
    out += [(f"out{n}", "out", N * n, N) for n in range(2)]
    return out


def psum_jobs():
    j = ["vec"] + [f"ht{t}{h}" for t in range(NT) for h in range(2)]
    j += [f"xbc{i}" for i in range(6)] + ["dt"] + ["lat0", "lat1"]
    j += ["u00", "u01"]
    j += ["cs"] + [f"xt{t}{h}" for t in range(NT) for h in range(2)] + ["bt", "cb", "latT0", "latT1"]
    j += [f"q{t}{n}" for t in range(NT) for n in range(3)]
    j += [f"kv{t}{n}" for t in range(NT) for n in range(4)]
    j += ["u10", "u11"]
    j += ["st0", "st1", "yo0", "yo1"] + [f"rb0{q}" for q in range(4)]
    j += ["v00", "v01", "yd00", "yd01"] + [f"rb1{q}" for q in range(4)]
    j += ["v10", "v11", "yd10", "yd11"] + [f"z{n}{t}" for n in range(2) for t in range(NT)]
    j += ["wt0", "wt1", "lng0", "lng1", "lnb0", "lnb1"]
    j += closing("ssd")
    j += [f"qT{t}{i}" for t in range(NT) for i in range(4)]
    j += [f"mx{t}{h}" for t in range(NT) for h in range(2)] + closing_part("sgu", 0)
    j += [f"kT{t}{i}" for t in range(NT) for i in range(4)]
    for kind, i in attention_order():
        if kind == "close":
            j += closing_part("sgu", i)
        else:
            j += [f"{kind}{i}"]
    j += closing("mla")
    j += [f"mT{t}{h}" for h in range(2) for t in range(NT)]
    j += [f"out{n}{t}" for n in range(2) for t in range(NT)]
    j += [f"ft{t}{h}" for t in range(NT) for h in range(2)]
    return j


def closing_part(br, i):
    if i == 1:
        return [f"yT_{br}{t}{h}" for t in range(NT) for h in range(2)]
    what, n = (("gate", 0), None, ("br", 0), ("gate", 1), ("br", 1))[i]
    return [f"{what}_{br}{n}{t}" for t in range(NT)]


def closing(br):
    return [x for i in range(5) for x in closing_part(br, i)]


GROUPS = [(0, 4 * q, 4) for q in range(4)] + [(1, 2 * q, 2) for q in range(8)]


def attention_order():
    out = []
    for s in range(len(GROUPS) + 2):
        if s < len(GROUPS):
            out.append(("sc", s))
        if s in (1, 3, 5, 7):
            out.append(("close", (s + 1) // 2))
        if 1 <= s <= len(GROUPS):
            out.append(("pt", s - 1))
        if s >= 2:
            out.append(("o", s - 2))
    return out


PANELS = mixer_panels()
JOBS = psum_jobs()
JOB = {name: i for i, name in enumerate(JOBS)}
assert len(JOB) == len(JOBS)
RING = 3
MOE_RING = 7
DENSE_PANELS = [(c, min(N, FFN_DENSE - c)) for c in range(0, FFN_DENSE, N)]
MOE_PANELS = [(c, N) for c in range(0, FFN_EXPERT, N)]
LAYER_USES = len(PANELS) + 3 * len(DENSE_PANELS)
LAYER_FILLS = [len(range(s, LAYER_USES, RING)) for s in range(RING)]
assert 3 * len(MOE_PANELS) % MOE_RING == 0
ITEM_USES = 3 * len(MOE_PANELS) // MOE_RING
MIXER_HI_SLOTS = 4
MIXER_AHEAD = 3
HI_SLOTS = 6
AHEAD = 4

WHOLE = ("uq", "ukv")
MIXER_PIECES = [(use, r) for use, panel in enumerate(PANELS) if panel[0] not in WHOLE for r in range(4)]


def pieces_needed():
    needed, used, so_far = {}, {}, 0
    names = [p[0] for p in PANELS if p[0] not in WHOLE]
    counted = 0
    for job in JOBS:
        if names and names[0].startswith("xbc"):
            n = int(names[0][3:])
            if job in (f"xbc{2 * n}", f"xbc{2 * n + 1}"):
                counted += 1
                used[so_far] = ("piece", counted)
                used[so_far + 1] = ("job", job)
                so_far += 2
                if job == f"xbc{2 * n + 1}":
                    names.pop(0)
        elif names and job == names[0] + "0":
            for r in range(3):
                counted += 1
                used[so_far + r] = ("piece", counted)
            used[so_far + 3] = ("job", names[0] + "1")
            so_far += 4
            names.pop(0)
        needed[job] = so_far
    assert so_far == len(MIXER_PIECES) and not names
    return needed, used


NEEDED, USED = pieces_needed()


class Split:

    def __init__(self, widths):
        n = len(widths)
        self.widths = widths
        self.order = [("gate", 0), ("up", 0)]
        for i in range(1, n):
            self.order += [("gate", i), ("up", i), ("down", i - 1)]
        self.order += [("down", n - 1)]
        self.at = {x: u for u, x in enumerate(self.order)}
        self.pieces = []
        self.first = []
        for u, (kind, i) in enumerate(self.order):
            self.first.append(len(self.pieces))
            step = D if kind == "down" else KD // 4 * widths[i]
            total = (widths[i] // P if kind == "down" else KD) * (D if kind == "down" else widths[i])
            self.pieces += [(u, o, step, o + step == total) for o in range(0, total, step)]
        self.first.append(len(self.pieces))

    def through(self, kind, i):
        return self.first[self.at[(kind, i)] + 1]


DENSE = Split([w for _, w in DENSE_PANELS])
MOE = Split([w for _, w in MOE_PANELS])
EARLY = 4
assert len(MOE.pieces) % HI_SLOTS == 0 and EARLY <= MOE.first[1]
SCATTER_BANKS = (6, 7, 1, 3)


class Chain:

    def __init__(self, eng, sem):
        self.eng, self.sem, self.n = eng, sem, 0

    def mark(self, ins):
        self.n += 1
        ins.then_inc(self.sem, 1)

    def sync(self):
        self.eng.wait_ge(self.sem, self.n)

    def link(self, ins):
        self.mark(ins)
        self.sync()


def hybrid_trunk(nc, A, out):
    with ExitStack() as ctx:
        def sb(name, shape, dt=F32):
            return ctx.enter_context(nc.sbuf_tensor(name, shape, dt))

        x = sb("x", [P, NT, D])
        hT = sb("hT", [P, KD, NT * P])
        hT_base = nc.sbuf_base - 4 * KD * NT * P
        const = sb("const", [P, N_CONST])
        vec = sb("vec", [P, P])
        cols = sb("cols", [P, N_ROWS])
        w_dt = sb("w_dt", [P, KD, HEADS])
        w_dt_base = nc.sbuf_base - 4 * KD * HEADS
        w_dt_hi = sb("w_dt_hi", [P, KD, HEADS], F32R)[:]
        heads_b = sb("heads_b", [P, 3, HEADS])
        gain_b = sb("gain_b", [P, 2, QK])
        small = sb("small", [P, 512])
        r_w = sb("r_w", [P, KD, EXPERTS])
        ones = sb("ones", [P, P])
        chosen = sb("chosen", [P, NT, EXPERTS])[:]
        item_tab = sb("item_tab", [1, ITEM_SLOTS + 1], I32)
        free = (nc.sbuf_bytes_remaining() if callable(nc.sbuf_bytes_remaining) else nc.sbuf_bytes_remaining) // 4 - 64
        sb("arena", [P, free])
        arena_base = nc.sbuf_base - 4 * free
        ps = ctx.enter_context(nc.psum_tensor("ps", [P, 8, N], F32))

        n_pieces = [0]

        def piece(at, *shape):
            n = 1
            for s in shape:
                n *= s
            assert at + n <= free, (at, n, free)
            n_pieces[0] += 1
            v = nc.alloc_sbuf_tensor_at(f"piece{n_pieces[0]}", [P] + list(shape), F32, offset=arena_base + 4 * at)[:]
            return v, at + -(-n // 8) * 8

        slots = [piece(s * SLOT, SLOT)[0] for s in range(MOE_RING)]
        at = RING * SLOT
        at_hT_hi = at
        at += KD * NT * P
        at_conv = at
        kT, _ = piece(at, HEADS, NT * P)
        xin, at = piece(at, 2, 2, NT * P + TAPS - 1)
        xc, at = piece(at, CONV_CHUNKS, NT * P)
        qT, _ = piece(at, HEADS, NT * P)
        xh, at = piece(at, NT, D)
        tmp, _ = piece(at_conv + KD * NT * P, HEADS * QK)
        xs, at = piece(at, NT, D)
        o, _ = piece(at, NT, D)
        q, at = piece(at, NT, HEADS * QK)
        at_k = at
        k, at = piece(at, NT, HEADS * QK)
        v, at = piece(at, NT, HEADS, HD)
        prob, _ = piece(at, 2, N)
        probT, _ = piece(at + 2 * N, 2, N)
        lat, _ = piece(at, NT, LAT)
        sgu_wT, _ = piece(at, 8, P)
        mt, at = piece(at, 4, N)
        xn, _ = piece(at, NT, D)
        u, at = piece(at, NT, D)
        vs, at = piece(at, NT, D)
        sgu_raw, _ = piece(at, 8, P)
        cbm, _ = piece(at + 8 * P, 4, P)
        at_yT = at
        yT, at = piece(at, KD, NT * P)
        latT, _ = piece(at, 3, NT * P)
        b_tok, _ = piece(at + 3 * NT * P, 2, P)
        gate, at = piece(at, NT, N)
        prev, _ = piece(at, 2, N)
        xd, _ = piece(at + 2 * N, D)
        merged, at = piece(at, NT, D)
        at_mixer_hi = at
        assert at + MIXER_HI_SLOTS * D <= free
        at = MOE_RING * SLOT
        fn, at = piece(at, NT, D)
        sg, at = piece(at, NT, N)
        h, at = piece(at, NT, N)
        at_xg = at
        xg, at = piece(at, KD, P)
        ysb, at = piece(at, D)
        pick, at = piece(at, NT, P)
        wpick, at = piece(at, NT, P)
        wpickT, at = piece(at, NT, P)
        items, at = piece(at, 8, ITEM_SLOTS * EXPERTS)
        pos_item, at = piece(at, NT, ITEM_SLOTS)
        w_item, at = piece(at, NT, ITEM_SLOTS)
        route, at = piece(at, 12, NT, EXPERTS)

        def over(name, base, at, shape):
            return nc.alloc_sbuf_tensor_at(name, [P] + shape, F32R, offset=base + 4 * at)

        w_lo = [over(f"w_lo{s}", arena_base, s * SLOT, [SLOT]) for s in range(MOE_RING)]
        xg_lo = over("xg_lo", arena_base, at_xg, [KD, P])
        hT_lo = over("hT_lo", hT_base, 0, [KD, NT * P])
        hT_hi = over("hT_hi", arena_base, at_hT_hi, [KD, NT * P])
        mixer_hi = over("mixer_hi", arena_base, at_mixer_hi, [MIXER_HI_SLOTS, D])
        yT_lo = over("yT_lo", arena_base, at_yT, [KD, NT * P])
        ssd_hi = over("ssd_hi", arena_base, at_conv, [KD, NT * P])
        yT_hi = over("yT_hi", arena_base, at_k, [KD, NT * P])
        w_dt_lo = over("w_dt_lo", w_dt_base, 0, [KD, HEADS])
        hid_hi = over("hid_hi", arena_base, at, [NT, N])
        hid_lo = over("hid_lo", arena_base, at + NT * N, [NT, N])
        at += 2 * NT * N
        xg_hi = over("xg_hi", arena_base, at, [KD, P])
        at += KD * P
        w_hi = over("w_hi", arena_base, at, [HI_SLOTS, D])
        assert at + HI_SLOTS * D <= free

        s_at = [0]

        def tiny(n):
            s_at[0] += n
            assert s_at[0] <= 512
            return small[:, s_at[0] - n:s_at[0]]

        def by(ap, **kw):
            (n1, s1), = [(a, b) for a, b in kw.items()]
            return ap.rearrange(f"p (a {n1}) -> p a {n1}", **{n1: s1})

        ss = tiny(2)
        rs = tiny(2)
        dtr = by(tiny(32), h=HEADS)
        dte = by(tiny(32), h=HEADS)
        dtv = by(tiny(32), h=HEADS)
        adt = by(tiny(32), h=HEADS)
        aexp = tiny(16)
        csv = by(tiny(64), h=HEADS)
        expcs = tiny(16)
        decay = tiny(16)
        ssg = by(tiny(4), h=2)
        rsg = by(tiny(4), h=2)
        ssl = by(tiny(4), h=2)
        rsl = by(tiny(4), h=2)
        ssh = tiny(16)
        rsh = tiny(16)
        mx = tiny(4)
        nmx = by(tiny(8), h=4)
        rsum = by(tiny(32), h=HEADS)
        rinv = by(tiny(32), h=HEADS)
        bn = tiny(24).rearrange("p (a b c) -> p a b c", a=NT, b=2)
        mv = by(tiny(4), h=2)
        lrs = tiny(2)
        lss = tiny(2)

        def cst(name, n):
            return const[:, CONST[name]:CONST[name] + n]

        ident = cst("ident", P)
        tri = cst("tri", P)
        before = cst("before", P)
        slot_no = cst("slot", P)
        mask = cst("mask", 2 * P)
        cos = by(cst("cos", 2 * HALF_ROPE), h=HALF_ROPE)
        sin = by(cst("sin", 2 * HALF_ROPE), h=HALF_ROPE)

        def col(name, i, n=1):
            return cols[:, ROWS[name] + i:ROWS[name] + i + n]

        def spread(ap, n):
            return ap.unsqueeze(2).to_broadcast([ap.shape[0], ap.shape[1], n])

        def repeat(ap, n):
            return ap.unsqueeze(1).to_broadcast([ap.shape[0], n, ap.shape[1]])

        def sem(name):
            return ctx.enter_context(nc.semaphore(name))

        const_in = sem("const_in")
        setup_done = sem("setup_done")
        ring_full = [sem(f"ring_full{s}") for s in range(MOE_RING)]
        ring_used = [sem(f"ring_used{s}") for s in range(MOE_RING)]
        go = sem("go")
        begun = sem("begun")
        stored = sem("stored")
        vec_in = sem("vec_in")
        vec_used = sem("vec_used")
        fills_begun = sem("fills_begun")
        routed = sem("routed")
        finished = sem("finished")

        arrived = sem("arrived")
        numbers = [arrived.num]

        def local(name):
            s = sem(name)
            numbers.append(s.num)
            return s

        bank_full = local("bank_full")
        bank_free = [local(f"bank_free{b}") for b in range(8)]
        act_steps = local("act_steps")
        dve_steps = local("dve_steps")
        small_in = local("small_in")
        S = {name: local(name) for name in (
            "squared", "mean_made", "rooted", "normed", "conv_made", "silu_made", "dt_neg", "dt_log", "a_exp",
            "adt_made", "tail_made", "cs_exp", "xs_made", "xd_made", "decay_made", "mt_made", "y_made", "ysq_made",
            "ymean_made", "yroot_made", "y_normed", "y_scale_made",
            "latsq_made", "latmean_made", "latroot_made", "lat_normed",
            "kpe_made", "kv_copied", "gated", "hsq_made", "hmean_made", "hroot_made", "hnorm_made", "max_made",
            "prob_made", "o_made", "var_made", "vroot_made", "v_normed", "fsquared", "fmean_made",
            "frooted", "fnormed", "sg_made", "h_made", "t_full", "hid_hi_made", "hid_made",
            "mixer_hi_made", "mixer_lo_made", "mixer_piece_used", "h_hi_made", "h_lo_made", "dt_hi_made", "dt_lo_made",
            "yT_hi_made", "yT_lo_made", "hi_made", "lo_made", "piece_used", "panel_done", "hT_hi_made", "hT_lo_made",
            "picked", "gathered", "xg_made", "xg_hi_made", "xg_lo_made", "wpickT_full", "wpickT_made",
            "y_copied", "scattered", "added", "zeroed",
            "logits", "chosen", "ranks", "gap_made", "gap_exp",
            "zeros_made")}
        assert numbers == list(range(numbers[0], numbers[0] + len(numbers)))
        cleared = range(numbers[0], numbers[-1] + 1)

        bank_uses = [len(JOBS[b::8]) for b in range(8)]

        splitters = {}

        def keep_ahead(eng, name):
            if id(eng) in splitters and JOB[name] >= JOB["xbc0"]:
                splitters[id(eng)](NEEDED[name] + (MIXER_AHEAD if NEEDED[name] != NEEDED["q00"] or JOB[name] > JOB["q00"]
                                                   else 0))

        def norm_pieces(i, step):
            return min(NEEDED["yT_ssd11"] + 4 * i + step + 4, NEEDED["br_ssd11"] + MIXER_AHEAD)

        def piece_free(eng, c):
            if c >= MIXER_HI_SLOTS:
                what, n = USED[c - MIXER_HI_SLOTS]
                if what == "job":
                    eng.wait_ge(bank_full, JOB[n] + 1)
                else:
                    eng.wait_ge(S["mixer_piece_used"], n)

        def mixer_piece(c):
            use, r = MIXER_PIECES[c]
            name, src, _, width = PANELS[use]
            sl = use % RING

            def cut(ap):
                ap = ap[:, 0:KD * width].rearrange("p (k n) -> p k n", k=KD)
                return ap[:, :, r * P:(r + 1) * P] if name.startswith("xbc") else ap[:, 2 * r:2 * r + 2, :]

            kc, n = (KD, P) if name.startswith("xbc") else (2, width)
            hi = mixer_hi[:, c % MIXER_HI_SLOTS, 0:kc * n].rearrange("p (k n) -> p k n", k=kc)
            return sl, cut(slots[sl]), hi, cut(w_lo[sl])

        def take(eng, name):
            keep_ahead(eng, name)
            eng.wait_ge(bank_full, JOB[name] + 1)
            return ps[:, JOB[name] % 8]

        def give(name, ins):
            ins.then_inc(bank_free[JOB[name] % 8], 1)

        def given(eng, name):
            keep_ahead(eng, name)
            eng.wait_ge(bank_free[JOB[name] % 8], JOB[name] // 8 + 1)

        def wait_panel(eng, split, kind, i):
            eng.wait_ge(S["panel_done"], split.at[(kind, i)] + 1)

        def split_pieces(eng, split, done_, upto, slot_of, one_piece, wait_full):
            while done_[0] < min(upto, len(split.pieces)):
                c = done_[0]
                u, at_, n, last = split.pieces[c]
                wait_full(c, u, at_ == 0)
                one_piece(w_hi[:, c % HI_SLOTS, 0:n], slot_of(u), at_, n)
                done_[0] += 1

        def hidden_in(i, tiles):
            return slice(0, 2) if tiles == 2 else slice(i % 2, i % 2 + 1)

        def hidden_free(eng, split, i, tiles):
            if i > 2 - tiles:
                wait_panel(eng, split, "down", i - (1 if tiles == 2 else 2))

        def turned_before(split, i, tiles):
            if i == 0 or (tiles == 1 and i == len(split.widths) - 1):
                return split.through("up", i)
            return split.through("down", i - 1)

        def hi_free(eng, split, c):
            if c >= HI_SLOTS:
                u, _, _, last = split.pieces[c - HI_SLOTS]
                if last:
                    eng.wait_ge(S["panel_done"], u + 1)
                else:
                    eng.wait_ge(S["piece_used"], c - HI_SLOTS + 1 - u)

        def halves(name):
            return sorted(((t, hh) for t in range(NT) for hh in range(2)), key=lambda x: JOB[f"{name}{x[0]}{x[1]}"])

        def begin(eng, turn):
            eng.wait_ge(go, turn)
            eng.sem_inc(begun, 1)

        def rows(w):
            return w.rearrange("l (k p) n -> l p k n", p=P)

        W = {"in": rows(A["w_in"]), "uq": rows(A["w_uq"]), "ukv": rows(A["w_ukv"]), "ssd": rows(A["w_br_ssd"]),
             "sgu": rows(A["w_br_sgu"]), "mla": rows(A["w_br_mla"]), "out": rows(A["w_out"])}
        chunks_of = {"uq": 2, "ukv": 1}

        def slot_view(s, kchunks, width):
            return slots[s][:, 0:kchunks * width].rearrange("p (k n) -> p k n", k=kchunks)

        uses0 = [LAYER_FILLS[s] + len(range(s, len(PANELS), RING)) for s in range(RING)] + [0] * (MOE_RING - RING)

        def dense_slot(u):
            return (len(PANELS) + u) % RING

        def moe_slot(u):
            return u % MOE_RING

        block = ctx.enter_context(nc.Block())

        @block.sync
        def _(sp):
            sp.dma_start(x[:], A["x"][0].rearrange("(t p) d -> p t d", p=P)).then_inc(const_in, 16)
            sp.dma_start(const[:], A["const"]).then_inc(const_in, 16)
            sp.dma_start(r_w[:], A["router_w"][0].rearrange("(k p) e -> p k e", p=P)).then_inc(const_in, 16)

            with sp.Fori(0, DEPTH) as L:
                one = bass.ds(L, 1)

                def panel(use):
                    name, src, c, width = PANELS[use]
                    s, n = use % RING, use // RING
                    kc = chunks_of.get(src, KD)
                    sp.wait_ge(ring_used[s], L * LAYER_FILLS[s] + n + 1)
                    if c == 0:
                        sp.sem_inc(fills_begun, 1)
                    sp.dma_start(slot_view(s, kc, width),
                                 W[src][one, :, :, c:c + width].rearrange("a p k n -> p (a k) n")
                                 ).then_inc(ring_full[s], 16)

                sp.wait_ge(vec_used, L + 1)
                sp.sem_inc(fills_begun, 1)
                for name, src, n in (("mix", "mix_norm_g", 8), ("ffn", "ffn_norm_g", 8), ("conv_b", "conv_b", 12),
                                     ("ssd", "ssd_norm_g", 8), ("q", "q_norm_g", 2), ("kv", "kv_norm_g", 1),
                                     ("ln_g", "sgu_ln_g", 8), ("ln_b", "sgu_ln_b", 8)):
                    sp.dma_start(vec[ROWS[name]:ROWS[name] + n, :],
                                 A[src][one, :].rearrange("a (r c) -> (a r) c", c=P)).then_inc(vec_in, 16)
                sp.dma_start(vec[ROWS["conv_w"]:ROWS["conv_w"] + 48, :],
                             A["conv_w"][one].rearrange("a k (r c) -> (a k r) c", c=P)).then_inc(vec_in, 16)
                sp.dma_start(vec[ROWS["sgu_b"]:ROWS["sgu_b"] + 8, :],
                             A["sgu_b"][one].rearrange("a r c -> (a r) c")).then_inc(vec_in, 16)
                for use in range(RING):
                    panel(use)
                sp.wait_ge(go, L + 1)
                for i, src in enumerate(("dt_bias", "a_log", "d_skip")):
                    sp.dma_start(heads_b[:, i, :], A[src][one, :].to_broadcast([P, HEADS])).then_inc(small_in, 16)
                for i, src in enumerate(("q_head_g", "k_head_g")):
                    sp.dma_start(gain_b[:, i, :], A[src][one, :].to_broadcast([P, QK])).then_inc(small_in, 16)
                with nc.allow_non_contiguous_dma(reason="sixteen columns of each row"):
                    sp.dma_start(w_dt[:], W["in"][one, :, :, C_DT:C_DT + HEADS].rearrange("a p k n -> p (a k) n")
                                 ).then_inc(small_in, 16)
                sp.dma_start(sgu_raw, A["sgu_w"][one].rearrange("a g t s -> t (a g) s")).then_inc(small_in, 16)
                for use in range(RING, len(PANELS)):
                    panel(use)
                with sp.If(L < 1):
                    for u, (kind, i) in enumerate(DENSE.order):
                        c, width = DENSE_PANELS[i]
                        use = len(PANELS) + u
                        s, n = use % RING, use // RING
                        sp.wait_ge(ring_used[s], n + 1)
                        if kind == "down":
                            dst = slots[s][:, 0:width // P * D].rearrange("p (k n) -> p k n", n=D)
                            w = A["ffn_w_down"][0, c:c + width, :].rearrange("(k p) n -> p k n", p=P)
                        else:
                            dst = slot_view(s, KD, width)
                            w = A[f"ffn_w_{kind}"][0].rearrange("(k p) n -> p k n", p=P)[:, :, c:c + width]
                        sp.dma_start(dst, w).then_inc(ring_full[s], 16)

            moe_w = {kind: A[f"moe_w_{kind}"][0].rearrange("e (k p) n -> e p k n", p=P) for kind in ("gate", "up", "down")}

            def moe_panel(item, u, expert):
                kind, p = MOE.order[u]
                c, width = MOE_PANELS[p]
                s, n = u % MOE_RING, u // MOE_RING
                sp.wait_ge(ring_used[s], item * ITEM_USES + (uses0[s] + n + 1))
                if kind == "down":
                    dst = slots[s].rearrange("p (k n) -> p k n", n=D)
                    w = moe_w[kind][expert, :, c // P:c // P + 4, :]
                else:
                    dst = slot_view(s, KD, width)
                    w = moe_w[kind][expert, :, :, c:c + width]
                sp.dma_start(dst, w.rearrange("a p k n -> p (a k) n")).then_inc(ring_full[s], 16)

            for u in range(RING):
                moe_panel(0, u, slice(0, 1))
            sp.wait_ge(go, DEPTH + 1)
            for u in range(RING, MOE_RING):
                moe_panel(0, u, slice(0, 1))
            sp.wait_ge(routed, 1)
            n_items = sp.value_load(item_tab[0:1, ITEM_SLOTS:ITEM_SLOTS + 1], min_val=EXPERTS, max_val=MAX_ITEMS)
            with sp.Fori(0, n_items) as i:
                e = sp.value_load(item_tab[0:1, bass.ds(i, 1)], min_val=0, max_val=EXPERTS - 1)
                for u in range(MOE_RING, len(MOE.order)):
                    moe_panel(i, u, bass.ds(e, 1))
                with sp.If(i < n_items - 1):
                    e2 = sp.value_load(item_tab[0:1, bass.ds(i + 1, 1)], min_val=0, max_val=EXPERTS - 1)
                    for u in range(MOE_RING):
                        moe_panel(i + 1, u, bass.ds(e2, 1))
            for t in range(NT):
                sp.wait_ge(finished, t + 1)
                sp.dma_start(out[0, t * P:(t + 1) * P, :], x[:, t, :]).then_inc(stored, 16)
            sp.wait_ge(stored, 32)

        @block.gpsimd
        def _(pool):
            pool.memset(vec[:], 0.0).then_inc(setup_done, 1)
            pool.memset(xin[:, :, :, 0:TAPS - 1], 0.0).then_inc(setup_done, 1)
            pool.memset(ones[:], 1.0).then_inc(setup_done, 1)
            pool.memset(small[:], 0.0).then_inc(setup_done, 1)
            pool.wait_ge(setup_done, 4)
            for s in range(MOE_RING):
                pool.sem_inc(ring_used[s], 1)
            pool.sem_inc(vec_used, 1)
            pool.sem_inc(go, 1)
            with pool.Fori(0, DEPTH):
                pool.wait_ge(arrived, 3)
                pool.memset(xin[:, :, :, 0:TAPS - 1], 0.0).then_inc(S["zeros_made"], 1)
                pool.wait_ge(S["zeros_made"], 1)
                pool.sem_clear(cleared)
                pool.sem_inc(go, 1)
            pool.wait_ge(arrived, 3)
            n_items = pool.value_load(item_tab[0:1, ITEM_SLOTS:ITEM_SLOTS + 1], min_val=EXPERTS, max_val=MAX_ITEMS)
            pool.sem_clear(cleared)
            pool.sem_inc(go, 1)
            with pool.Fori(0, n_items):
                pool.wait_ge(arrived, 3)
                pool.sem_clear(cleared)
                pool.sem_inc(go, 1)

        @block.tensor
        def _(pe):
            turn = [0]
            unreleased = []

            def bank(name):
                i = turn[0]
                assert JOBS[i] == name, (JOBS[i], name)
                turn[0] += 1
                if i >= 8:
                    pe.wait_ge(bank_free[i % 8], i // 8)
                return ps[:, i % 8]

            def done(ins):
                ins.then_inc(bank_full, 1)

            def release():
                while unreleased:
                    s, signal, n = unreleased.pop(0)
                    pe.wait_ge(signal, n)
                    pe.sem_inc(ring_used[s], 1)

            def turn_over(name, parts):
                b = bank(name)
                at = 0
                for a in parts:
                    n, m = a.shape[0], a.shape[1]
                    last = pe.transpose(b[0:m, at:at + n], a, ident[0:n, 0:n])
                    at += n
                done(last)

            def htile(kk, t):
                return hT[:, kk, t * P:(t + 1) * P]

            def both(a_hi, a_lo):
                return lambda kk, t: (a_hi[:, kk, t * P:(t + 1) * P], a_lo[:, kk, t * P:(t + 1) * P])

            hsplit, ssplit, ysplit = both(hT_hi, hT_lo), both(ssd_hi, yT_lo), both(yT_hi, yT_lo)

            def ffn(split, tiles, slot_of, lhs, acc, before_turn=None, before_down=None, early=0):
                n_panels = len(split.widths)

                def turn_hidden(i):
                    pe.wait_ge(S["h_made"], i + 1)
                    for t in range(tiles):
                        for j in range(split.widths[i] // P):
                            last = pe.transpose(ps[:, 2 + t, j * P:(j + 1) * P], h[:, t, j * P:(j + 1) * P], ident)
                    last.then_inc(S["t_full"], 1)

                for c, (u, at_, n, ends) in enumerate(split.pieces):
                    kind, i = split.order[u]
                    s, width = slot_of(u), split.widths[i]
                    if kind == "up" and i and at_ == 0:
                        pe.wait_ge(S["hid_made"], i)
                    if kind == "down" and at_ == 0:
                        pe.wait_ge(S["hid_made"], i + 1)
                    if c >= early:
                        pe.wait_ge(S["lo_made"], c + 1 - early)
                    hi, lo = w_hi[:, c % HI_SLOTS, 0:n], w_lo[s][:, at_:at_ + n]
                    for t in range(tiles):
                        if kind == "down":
                            j = at_ // D
                            a_hi, a_lo = (a[:, hidden_in(i, tiles), :][:, t, j * P:(j + 1) * P] for a in (hid_hi, hid_lo))
                            for half in range(2):
                                cs_ = slice(half * N, (half + 1) * N)
                                start, stop = i == 0 and j == 0, i == n_panels - 1 and ends
                                pe.matmul(acc(t, half), a_hi, hi[:, cs_], start=start, stop=False)
                                pe.matmul(acc(t, half), a_hi, lo[:, cs_], start=False, stop=False)
                                last = pe.matmul(acc(t, half), a_lo, hi[:, cs_], start=False, stop=stop)
                        else:
                            b = ps[:, (0 if kind == "gate" else 2) + t, 0:width]
                            for j in range(n // width):
                                kk = at_ // width + j
                                a_hi, a_lo = lhs(kk, t)
                                cs_ = slice(j * width, (j + 1) * width)
                                pe.matmul(b, a_hi, hi[:, cs_], start=(kk == 0), stop=False)
                                pe.matmul(b, a_hi, lo[:, cs_], start=False, stop=False)
                                last = pe.matmul(b, a_lo, hi[:, cs_], start=False, stop=(kk == KD - 1))
                    last.then_inc(S["panel_done" if ends else "piece_used"], 1)
                    if at_ == 0:
                        release()
                    if ends:
                        unreleased.append((s, S["panel_done"], u + 1))
                        if kind == "up" and i == 0:
                            if before_turn:
                                before_turn()
                            turn_hidden(0)
                        if kind == "up" and i == n_panels - 1 and before_down:
                            before_down()
                            turn_hidden(i)
                        if kind == "down" and i + 1 < n_panels - (1 if before_down else 0):
                            turn_hidden(i + 1)
                release()

            pe.wait_ge(const_in, 48)
            pe.wait_ge(setup_done, 4)

            with pe.Fori(0, DEPTH) as L:
                turn[0] = 0
                use = [0]

                def panel(name):
                    assert PANELS[use[0]][0] == name, (PANELS[use[0]], name)
                    s, n = use[0] % RING, use[0] // RING
                    src, width = PANELS[use[0]][1], PANELS[use[0]][3]
                    use[0] += 1
                    if name in WHOLE:
                        pe.wait_ge(ring_full[s], L * (16 * LAYER_FILLS[s]) + 16 * (n + 1))
                    return s, slot_view(s, chunks_of.get(src, KD), width), width

                piece_no = [0]

                def split_piece():
                    c = piece_no[0]
                    piece_no[0] += 1
                    pe.wait_ge(S["mixer_lo_made"], c + 1)
                    return mixer_piece(c)[2:]

                def project(name, lhs):
                    s, _, width = panel(name)
                    banks = [bank(f"{name}{t}") for t in range(NT)]
                    for r in range(4):
                        hi, lo = split_piece()
                        for t in range(NT):
                            b = banks[t][:, 0:width]
                            for j in range(2):
                                kk = 2 * r + j
                                a_hi, a_lo = lhs(kk, t)
                                pe.matmul(b, a_hi, hi[:, j, :], start=(kk == 0), stop=False)
                                pe.matmul(b, a_hi, lo[:, j, :], start=False, stop=False)
                                last = pe.matmul(b, a_lo, hi[:, j, :], start=False, stop=(kk == KD - 1))
                            if r == 3:
                                done(last)
                        if r < 3:
                            last.then_inc(S["mixer_piece_used"], 1)
                        if r == 0:
                            release()
                    unreleased.append((s, bank_full, turn[0]))

                def close_part(br, i, y, ready):
                    if i == 1:
                        for t in range(NT):
                            ready(t)
                            for hh in range(2):
                                turn_over(f"yT_{br}{t}{hh}",
                                          [y[:, t, c * P:(c + 1) * P] for c in range(4 * hh, 4 * hh + 4)])
                        return
                    what, n = (("gate", 0), None, ("br", 0), ("gate", 1), ("br", 1))[i]
                    if i == 2:
                        pe.wait_ge(S["yT_lo_made"], 4 * ("ssd", "sgu", "mla").index(br) + 4)
                    project(f"{what}_{br}{n}", hsplit if what == "gate" else ssplit if br == "ssd" else ysplit)

                begin(pe, L + 1)
                pe.wait_ge(vec_in, L * 160 + 160)
                done(pe.transpose(bank("vec")[:, 0:P], vec[:, :], ident))
                for t in range(NT):
                    pe.wait_ge(S["normed"], t + 1)
                    for hh in range(2):
                        turn_over(f"ht{t}{hh}", [xn[:, t, c * P:(c + 1) * P] for c in range(4 * hh, 4 * hh + 4)])
                pe.wait_ge(S["h_lo_made"], 4)
                for n in range(3):
                    s, _, _ = panel(f"xbc{n}")
                    for i in range(2):
                        b = bank(f"xbc{2 * n + i}")
                        for j in range(2):
                            hi, lo = split_piece()
                            o_ = b[:, j * NT * P:(j + 1) * NT * P]
                            for kk in range(KD):
                                pe.matmul(o_, hi[:, kk, :], hT_hi[:, kk, :], start=(kk == 0), stop=False)
                                pe.matmul(o_, lo[:, kk, :], hT_hi[:, kk, :], start=False, stop=False)
                                last = pe.matmul(o_, hi[:, kk, :], hT_lo[:, kk, :], start=False, stop=(kk == KD - 1))
                            if j == 0:
                                last.then_inc(S["mixer_piece_used"], 1)
                                release()
                        done(last)
                    unreleased.append((s, bank_full, turn[0]))
                pe.wait_ge(S["dt_lo_made"], 1)
                b = bank("dt")
                for t in range(NT):
                    o_ = b[:, t * HEADS:(t + 1) * HEADS]
                    for kk in range(KD):
                        a_hi, a_lo = hsplit(kk, t)
                        pe.matmul(o_, a_hi, w_dt_hi[:, kk, :], start=(kk == 0), stop=False)
                        pe.matmul(o_, a_hi, w_dt_lo[:, kk, :], start=False, stop=False)
                        last = pe.matmul(o_, a_lo, w_dt_hi[:, kk, :], start=False, stop=(kk == KD - 1))
                done(last)
                project("lat", hsplit)
                project("u0", hsplit)
                release()
                pe.wait_ge(S["adt_made"], 1)
                b = bank("cs")
                for c in range(NT):
                    pe.matmul(b[:, c * HEADS:(c + 1) * HEADS], tri, adt[:, c, :], start=True, stop=True)
                for c in range(NT):
                    last = pe.matmul(b[:, (2 + c) * HEADS:(3 + c) * HEADS], ones[:], adt[:, c, :],
                                     start=True, stop=True)
                done(last)
                pe.wait_ge(S["silu_made"], 6)
                for t in range(NT):
                    for hh in range(2):
                        turn_over(f"xt{t}{hh}", [xc[:, c, t * P:(t + 1) * P] for c in range(4 * hh, 4 * hh + 4)])
                turn_over("bt", [xc[:, 8 + g, 0:P] for g in range(2)])
                b = bank("cb")
                for c in range(NT):
                    for g in range(2):
                        at = (2 * c + g) * P
                        last = pe.matmul(b[:, at:at + P], xc[:, 8 + g, c * P:(c + 1) * P],
                                         xc[:, 10 + g, c * P:(c + 1) * P], start=True, stop=True)
                done(last)
                for t in range(NT):
                    pe.wait_ge(S["lat_normed"], t + 1)
                    turn_over(f"latT{t}", [lat[:, t, c * P:(c + 1) * P] for c in range(3)])
                s, w, _ = panel("uq")
                for t in range(NT):
                    given(pe, f"latT{t}")
                    for n in range(3):
                        b = bank(f"q{t}{n}")
                        for kk in range(2):
                            last = pe.matmul(b[:], latT[:, kk, t * P:(t + 1) * P], w[:, kk, n * N:(n + 1) * N],
                                             start=(kk == 0), stop=(kk == 1))
                        done(last)
                        release()
                unreleased.append((s, bank_full, turn[0]))
                s, w, _ = panel("ukv")
                for t in range(NT):
                    for n in range(4):
                        b = bank(f"kv{t}{n}")
                        done(pe.matmul(b[:], latT[:, 2, t * P:(t + 1) * P], w[:, 0, n * N:(n + 1) * N],
                                       start=True, stop=True))
                        release()
                unreleased.append((s, bank_full, turn[0]))
                project("u1", hsplit)
                pe.wait_ge(S["xd_made"], 1)
                given(pe, "bt")
                for g in range(2):
                    done(pe.matmul(bank(f"st{g}")[:], b_tok[:, g, :], xd[:, g * N:(g + 1) * N], start=True, stop=True))
                for g in range(2):
                    given(pe, f"st{g}")
                    done(pe.matmul(bank(f"yo{g}")[:], xc[:, 10 + g, P:2 * P], prev[:, g, :], start=True, stop=True))
                for c in range(NT):
                    for qd in range(4):
                        b = bank(f"rb{c}{qd}")
                        for i in range(4):
                            hh = 4 * qd + i
                            last = pe.matmul(b[:, i * P:(i + 1) * P], adt[:, c, hh:hh + 1].to_broadcast([P, P]), tri,
                                             start=True, stop=True)
                        done(last)
                    project(f"v{c}", hsplit)
                    pe.wait_ge(S["xs_made"], c + 1)
                    for g in range(2):
                        pe.wait_ge(S["mt_made"], 4 * c + 2 * g + 2)
                        b = bank(f"yd{c}{g}")
                        for i in range(8):
                            hh = 8 * g + i
                            last = pe.matmul(b[:, i * HD:(i + 1) * HD], mt[:, hh // 4, (hh % 4) * P:(hh % 4 + 1) * P],
                                             xs[:, c, hh * HD:(hh + 1) * HD], start=True, stop=True)
                        done(last)
                project("z0", hsplit)
                project("z1", hsplit)
                for i in range(2):
                    turn_over(f"wt{i}", [sgu_raw[:, g, :] for g in range(4 * i, 4 * i + 4)])
                for what, row in (("lng", "ln_g"), ("lnb", "ln_b")):
                    for hh in range(2):
                        b = bank(f"{what}{hh}")
                        for i in range(4):
                            r = ROWS[row] + 4 * hh + i
                            last = pe.matmul(b[:, i * P:(i + 1) * P], ident[:, r:r + 1].to_broadcast([P, P]), vec[:, :],
                                             start=True, stop=True)
                        done(last)
                pe.wait_ge(bank_full, turn[0])
                pe.sem_inc(vec_used, 1)
                for i in range(5):
                    close_part("ssd", i, xh, lambda t: pe.wait_ge(S["y_normed"], t + 1))
                def turn_heads(w_no, name, src):
                    for t in range(NT):
                        pe.wait_ge(S["hnorm_made"], 2 * w_no + t + 1)
                        for i in range(4):
                            turn_over(f"{name}{t}{i}",
                                      [src[:, t, hh * QK:(hh + 1) * QK] for hh in range(4 * i, 4 * i + 4)])

                def u_ready(t):
                    given(pe, f"mx{t}0")
                    given(pe, f"mx{t}1")

                turn_heads(0, "qT", q)
                given(pe, "wt0")
                given(pe, "wt1")
                for t in range(NT):
                    pe.wait_ge(S["v_normed"], t + 1)
                    for hh in range(2):
                        b = bank(f"mx{t}{hh}")
                        for i in range(4):
                            g = 4 * hh + i
                            last = pe.matmul(b[:, i * P:(i + 1) * P], sgu_wT[:, g, :], vs[:, t, g * P:(g + 1) * P],
                                             start=True, stop=True)
                        done(last)
                close_part("sgu", 0, u, u_ready)
                turn_heads(1, "kT", k)
                for name in [f"{w}T{t}{i}" for w in "qk" for t in range(NT) for i in range(4)]:
                    given(pe, name)
                for kind, i in attention_order():
                    if kind == "close":
                        close_part("sgu", i, u, u_ready)
                        continue
                    t, h0, nh = GROUPS[i]
                    blocks = t + 1
                    b = bank(f"{kind}{i}")
                    if kind == "sc":
                        keys = blocks * P
                        for j in range(nh):
                            last = pe.matmul(b[:, j * keys:(j + 1) * keys], qT[0:QK, h0 + j, t * P:(t + 1) * P],
                                             kT[0:QK, h0 + j, 0:keys], start=True, stop=True)
                    elif kind == "pt":
                        pe.wait_ge(S["prob_made"], i + 1)
                        for j in range(4):
                            last = pe.transpose(b[:, j * P:(j + 1) * P], prob[:, i % 2, j * P:(j + 1) * P], ident)
                    else:
                        given(pe, f"pt{i}")
                        for j in range(nh):
                            for kb in range(blocks):
                                at = (j * blocks + kb) * P
                                last = pe.matmul(b[:, j * HD:(j + 1) * HD], probT[:, i % 2, at:at + P],
                                                 v[:, kb, h0 + j, :], start=(kb == 0), stop=(kb == blocks - 1))
                    done(last)
                for i in range(5):
                    close_part("mla", i, o, lambda t: pe.wait_ge(S["o_made"], (4, 12)[t]))
                for hh in range(2):
                    pe.wait_ge(S["gated"], 10 + 2 * hh)
                    for t in range(NT):
                        turn_over(f"mT{t}{hh}", [merged[:, t, c * P:(c + 1) * P] for c in range(4 * hh, 4 * hh + 4)])
                pe.wait_ge(S["yT_lo_made"], 16)
                project("out0", ysplit)
                project("out1", ysplit)
                release()
                for t in range(NT):
                    pe.wait_ge(S["fnormed"], t + 1)
                    for hh in range(2):
                        turn_over(f"ft{t}{hh}", [fn[:, t, c * P:(c + 1) * P] for c in range(4 * hh, 4 * hh + 4)])
                for b in range(8):
                    pe.wait_ge(bank_free[b], bank_uses[b])
                with pe.If(L < 1):
                    pe.wait_ge(S["hT_lo_made"], 2)
                    ffn(DENSE, NT, dense_slot, hsplit, lambda t, half: ps[:, 4 + 2 * t + half])
                pe.wait_ge(bank_full, len(JOBS))
                pe.sem_inc(arrived, 1)

            begin(pe, DEPTH + 1)
            for t in range(NT):
                for kk in range(KD):
                    last = pe.matmul(ps[:, 0, t * EXPERTS:(t + 1) * EXPERTS], htile(kk, t), r_w[:, kk, :],
                                     start=(kk == 0), stop=(kk == KD - 1))
            last.then_inc(S["logits"], 1)
            pe.wait_ge(S["chosen"], 1)
            E8 = EXPERTS
            pe.matmul(ps[:, 1, 0:E8], before, chosen[:, 0, :], start=True, stop=True)
            pe.matmul(ps[:, 1, E8:2 * E8], before, chosen[:, 1, :], start=True, stop=False)
            pe.matmul(ps[:, 1, E8:2 * E8], ones[:], chosen[:, 0, :], start=False, stop=True)
            pe.matmul(ps[:, 1, 2 * E8:3 * E8], ones[:], chosen[:, 0, :], start=True, stop=False)
            pe.matmul(ps[:, 1, 2 * E8:3 * E8], ones[:], chosen[:, 1, :], start=False, stop=True
                      ).then_inc(S["ranks"], 1)

            def gather(picks):
                pe.wait_ge(S["picked"], picks)
                for c in range(KD):
                    for t in range(NT):
                        last = pe.matmul(ps[:, 6 + c // 4, c % 4 * P:(c % 4 + 1) * P], fn[:, t, c * P:(c + 1) * P],
                                         pick[:, t, :], start=(t == 0), stop=(t == NT - 1))
                    if c % 4 == 3:
                        last.then_inc(S["gathered"], 1)

            def scatter():
                pe.wait_ge(S["y_copied"], 2)
                for j in range(4):
                    t, half = j // 2, j % 2
                    pe.matmul(ps[:, SCATTER_BANKS[j]], wpickT[:, t, :], ysb[:, half * N:(half + 1) * N],
                              start=True, stop=True).then_inc(S["scattered"], 1)

            def gather_next():
                pe.wait_ge(S["added"], 2)
                gather(1)
                pe.wait_ge(S["picked"], 2)
                for t in range(NT):
                    last = pe.transpose(ps[:, 3, t * P:(t + 1) * P], wpick[:, t, :], ident)
                last.then_inc(S["wpickT_full"], 1)

            gather(1)
            pe.wait_ge(S["gathered"], 2)
            pe.sem_inc(arrived, 1)

            pe.wait_ge(routed, 1)
            n_items = pe.value_load(item_tab[0:1, ITEM_SLOTS:ITEM_SLOTS + 1], min_val=EXPERTS, max_val=MAX_ITEMS)
            with pe.Fori(0, n_items) as item:
                begin(pe, item + (DEPTH + 2))
                ffn(MOE, 1, moe_slot, lambda kk, t: (xg_hi[:, kk, :], xg_lo[:, kk, :]), lambda t, half: ps[:, 4 + half],
                    scatter, gather_next, EARLY)
                pe.sem_inc(arrived, 1)
            begin(pe, n_items + (DEPTH + 2))
            scatter()

        @block.scalar
        def _(act):
            def copy_out(name, out_ap, in_ap):
                give(name, act.activation(out_ap, in_ap, ACT.Copy))

            def lead(hi, s, at_, n):
                act.activation(hi, slots[s][:, at_:at_ + n], ACT.Copy).then_inc(S["hi_made"], 1)

            def ffn(split, tiles, slot_of, wait_full, at_end=None, early=0):
                made = [early]

                def ready(c, u, first):
                    if first:
                        wait_full(u)
                    hi_free(act, split, c)

                def ahead(upto):
                    split_pieces(act, split, made, upto, slot_of, lead, ready)

                for i, width in enumerate(split.widths):
                    ahead(split.through("gate", i) + AHEAD)
                    wait_panel(act, split, "gate", i)
                    if i:
                        act.wait_ge(S["h_made"], i)
                    act.activation(sg[:, 0:tiles, 0:width], ps[:, 0:tiles, 0:width], ACT.Silu).then_inc(S["sg_made"], 1)
                    ahead(turned_before(split, i, tiles) + AHEAD)
                    act.wait_ge(S["t_full"], i + 1)
                    hidden_free(act, split, i, tiles)
                    act.activation(hid_hi[:, hidden_in(i, tiles), 0:width], ps[:, 2:2 + tiles, 0:width], ACT.Copy
                                   ).then_inc(S["hid_hi_made"], 1)
                ahead(len(split.pieces))
                if at_end:
                    at_end()

            act.wait_ge(const_in, 48)
            act.wait_ge(setup_done, 4)
            with act.Fori(0, DEPTH) as L:
                begin(act, L + 1)
                leads = [0]

                def lead_mixer(upto):
                    while leads[0] < min(upto, len(MIXER_PIECES)):
                        c = leads[0]
                        leads[0] += 1
                        s, value, hi, _ = mixer_piece(c)
                        use, r = MIXER_PIECES[c]
                        if r == 0:
                            act.wait_ge(ring_full[s], L * (16 * LAYER_FILLS[s]) + 16 * (use // RING + 1))
                        piece_free(act, c)
                        act.activation(hi, value, ACT.Copy).then_inc(S["mixer_hi_made"], 1)

                splitters[id(act)] = lead_mixer
                for t in range(NT):
                    act.activation(vs[:, t, :], x[:, t, :], ACT.Square, accum_out=ss[:, t:t + 1]).then_inc(S["squared"], 1)
                act.wait_ge(S["mean_made"], 1)
                act.activation(rs[:], ss[:], ACT.Sqrt).then_inc(S["rooted"], 1)
                for t in range(NT):
                    for hh in range(2):
                        given(act, f"ht{t}{hh}")
                        cut = (slice(None), slice(4 * hh, 4 * hh + 4), slice(t * P, (t + 1) * P))
                        act.activation(hT_hi[cut], hT[cut], ACT.Copy).then_inc(S["h_hi_made"], 1)
                for i in range(7):
                    if i == 3:
                        act.wait_ge(small_in, 112)
                        act.activation(w_dt_hi, w_dt[:], ACT.Copy).then_inc(S["dt_hi_made"], 1)
                    if i < 6:
                        b = take(act, f"xbc{i}")
                        if i >= 2:
                            act.wait_ge(S["conv_made"], i - 1)
                        copy_out(f"xbc{i}", xin[:, i % 2, :, TAPS - 1:], by(b, h=NT * P))
                    if i:
                        act.wait_ge(S["conv_made"], i)
                        piece_ = xc[:, 2 * i - 2:2 * i, :]
                        act.activation(piece_, piece_, ACT.Silu).then_inc(S["silu_made"], 1)
                act.wait_ge(small_in, 112)
                act.activation(aexp, heads_b[:, 1, :], ACT.Exp).then_inc(S["a_exp"], 1)
                act.wait_ge(S["dt_neg"], 1)
                act.activation(dte, dtv, ACT.Exp).then_inc(act_steps, 1)
                act.wait_ge(act_steps, 1)
                act.activation(dte, dte, ACT.Ln, bias=1.0).then_inc(S["dt_log"], 1)
                for t in range(NT):
                    b = take(act, f"lat{t}")
                    copy_out(f"lat{t}", lat[:, t, :], b[:, 0:LAT])
                for t in range(NT):
                    given(act, f"lat{t}")
                    act.activation(vs[:, t, 0:256], lat[:, t, 0:256], ACT.Square, accum_out=ssl[:, t, 0:1])
                    act.activation(vs[:, t, 256:384], lat[:, t, 256:384], ACT.Square, accum_out=ssl[:, t, 1:2]
                                   ).then_inc(S["latsq_made"], 1)
                act.wait_ge(S["latmean_made"], 1)
                act.activation(rsl, ssl, ACT.Sqrt).then_inc(S["latroot_made"], 1)

                def gelu_u(n):
                    for t in range(NT):
                        b = take(act, f"u{n}{t}")
                        give(f"u{n}{t}", act.activation(u[:, t, n * N:(n + 1) * N], b, ACT.Gelu))

                gelu_u(0)
                given(act, "cs")
                act.activation(expcs, csv[:, 1, :], ACT.Exp).then_inc(S["cs_exp"], 1)
                act.wait_ge(S["tail_made"], 1)
                act.activation(decay, decay, ACT.Exp).then_inc(S["cs_exp"], 1)
                for t in range(NT):
                    for hh in range(2):
                        b = take(act, f"xt{t}{hh}")
                        copy_out(f"xt{t}{hh}", xh[:, t, hh * N:(hh + 1) * N], b)
                for t in range(NT):
                    for n in range(3):
                        b = take(act, f"q{t}{n}")
                        copy_out(f"q{t}{n}", q[:, t, n * N:(n + 1) * N], b)
                for t in range(NT):
                    for n in range(4):
                        b = by(take(act, f"kv{t}{n}"), h=2 * HD)
                        act.activation(by(k[:, t, :], h=QK)[:, 4 * n:4 * n + 4, 0:NOPE], b[:, :, 0:NOPE], ACT.Copy
                                       ).then_inc(S["kv_copied"], 1)
                        copy_out(f"kv{t}{n}", v[:, t, 4 * n:4 * n + 4, :], b[:, :, NOPE:])
                gelu_u(1)
                for g in range(2):
                    b = take(act, f"st{g}")
                    copy_out(f"st{g}", prev[:, g, :], b)
                for c in range(NT):
                    for qd in range(4):
                        given(act, f"rb{c}{qd}")
                        act.activation(mt[:, qd, :], mt[:, qd, :], ACT.Exp).then_inc(S["decay_made"], 1)
                    for t in range(NT):
                        b = take(act, f"v{c}{t}")
                        give(f"v{c}{t}", act.activation(vs[:, t, c * N:(c + 1) * N], b, ACT.Gelu))
                for n in range(2):
                    for t in range(NT):
                        b = take(act, f"z{n}{t}")
                        if n:
                            act.wait_ge(S["y_made"], t + 1)
                        give(f"z{n}{t}", act.activation(gate[:, t, :], b, ACT.Silu))
                for g in range(2):
                    for t in range(NT):
                        act.wait_ge(S["y_made"], 2 * g + t + 1)
                        act.activation(xs[:, t, g * N:(g + 1) * N], xh[:, t, g * N:(g + 1) * N], ACT.Square,
                                       accum_out=ssg[:, t, g:g + 1]).then_inc(S["ysq_made"], 1)
                act.wait_ge(S["ymean_made"], 1)
                act.activation(rsg, ssg, ACT.Sqrt).then_inc(S["yroot_made"], 1)
                act.wait_ge(S["var_made"], 1)
                act.activation(lrs, lss, ACT.Sqrt).then_inc(S["vroot_made"], 1)
                act.wait_ge(S["y_scale_made"], 1)
                for t in range(NT):
                    for g in range(2):
                        cut = xh[:, t, g * N:(g + 1) * N]
                        ins = act.activation(cut, cut, ACT.Copy, scale=rsg[:, t, g:g + 1])
                        if g:
                            ins.then_inc(S["y_normed"], 1)

                gates = []

                def gate_panel(br, n):
                    if gates:
                        keep_ahead(act, f"br_{gates[-1]}1")
                        act.wait_ge(S["gated"], 2 * len(gates))
                    gates.append(f"{br}{n}")
                    for t in range(NT):
                        b = take(act, f"gate_{br}{n}{t}")
                        give(f"gate_{br}{n}{t}", act.activation(gate[:, t, :], b, ACT.Sigmoid))

                def head_squares(i):
                    src, t = (q, k)[i // 2], i % 2
                    if i == 0:
                        for tt in range(NT):
                            given(act, f"q{tt}2")
                    if i == 2:
                        act.wait_ge(S["kv_copied"], 8)
                        act.wait_ge(S["kpe_made"], 2)
                    if i:
                        act.wait_ge(S["hnorm_made"], i)
                    act.activation(tmp, src[:, t, :], ACT.Square).then_inc(S["hsq_made"], 1)
                    lead_mixer(norm_pieces(i, 0))
                    act.wait_ge(S["hmean_made"], i + 1)
                    act.activation(rsh, ssh, ACT.Sqrt).then_inc(S["hroot_made"], 1)
                    lead_mixer(norm_pieces(i, 3))

                gate_panel("ssd", 0)
                for t in range(NT):
                    for hh in range(2):
                        given(act, f"yT_ssd{t}{hh}")
                        cut = (slice(None), slice(4 * hh, 4 * hh + 4), slice(t * P, (t + 1) * P))
                        act.activation(ssd_hi[cut], yT[cut], ACT.Copy).then_inc(S["yT_hi_made"], 1)
                head_squares(0)
                head_squares(1)
                gate_panel("ssd", 1)
                head_squares(2)
                head_squares(3)
                for name, dst in (("qT", qT), ("kT", kT)):
                    if dst is kT:
                        gate_panel("sgu", 0)
                    for t in range(NT):
                        for i in range(4):
                            b = take(act, f"{name}{t}{i}")
                            if dst is kT and t == 0 and i == 0:
                                act.wait_ge(S["hnorm_made"], 4)
                            copy_out(f"{name}{t}{i}", dst[0:QK, 4 * i:4 * i + 4, t * P:(t + 1) * P], by(b[0:QK, :], h=P))

                def turned(name):
                    for t, hh in halves(name):
                        b = take(act, f"{name}{t}{hh}")
                        act.activation(yT_hi[:, 4 * hh:4 * hh + 4, t * P:(t + 1) * P], by(b, h=P), ACT.Copy
                                       ).then_inc(S["yT_hi_made"], 1)

                for kind, i in attention_order():
                    if kind == "sc":
                        t, h0, nh = GROUPS[i]
                        keys = (t + 1) * P
                        keep_ahead(act, f"sc{i}")
                        act.wait_ge(S["max_made"], i + 1)
                        for j in range(nh):
                            p_ = prob[:, i % 2, j * keys:(j + 1) * keys]
                            e_ = act.activation(p_, p_, ACT.Exp, bias=nmx[:, i % 2, j:j + 1], scale=SCALE,
                                                accum_out=rsum[:, t, h0 + j:h0 + j + 1])
                        e_.then_inc(S["prob_made"], 1)
                    elif kind == "pt":
                        b = take(act, f"pt{i}")
                        if i >= 2:
                            act.wait_ge(bank_full, JOB[f"o{i - 2}"] + 1)
                        copy_out(f"pt{i}", probT[:, i % 2, :], b)
                    elif kind == "close":
                        if i == 1:
                            turned("yT_sgu")
                        elif i == 3:
                            gate_panel("sgu", 1)
                gate_panel("mla", 0)
                turned("yT_mla")
                gate_panel("mla", 1)
                turned("mT")
                for t in range(NT):
                    given(act, f"out0{t}")
                    given(act, f"out1{t}")
                    act.activation(fn[:, t, :], x[:, t, :], ACT.Square, accum_out=ss[:, t:t + 1]
                                   ).then_inc(S["fsquared"], 1)
                act.wait_ge(S["fmean_made"], 1)
                act.activation(rs[:], ss[:], ACT.Sqrt).then_inc(S["frooted"], 1)
                with act.If(L < 1):
                    def dense_full(u):
                        act.wait_ge(ring_full[dense_slot(u)], 16 * ((len(PANELS) + u) // RING + 1))

                    for t in range(NT):
                        for hh in range(2):
                            given(act, f"ft{t}{hh}")
                    for half in range(2):
                        cut = (slice(None), slice(4 * half, 4 * half + 4))
                        act.activation(hT_hi[cut], hT[cut], ACT.Copy).then_inc(S["hT_hi_made"], 1)
                    ffn(DENSE, NT, dense_slot, dense_full)
                act.activation(small[:, 511:512], small[:, 511:512], ACT.Copy).then_inc(act_steps, 1)
                act.wait_ge(act_steps, 2)
                act.sem_inc(arrived, 1)

            begin(act, DEPTH + 1)

            def lead_early(wait):
                for c in range(EARLY):
                    panel, at_, n, _ = MOE.pieces[c]
                    if wait:
                        hi_free(act, MOE, len(MOE.pieces) + c)
                    lead(w_hi[:, c, 0:n], moe_slot(panel), at_, n)

            act.wait_ge(ring_full[0], 16 * (uses0[0] + 1))
            lead_early(False)
            act.wait_ge(S["gap_made"], 1)
            act.activation(route[:, 4, :, 0:1], route[:, 3, :, 0:1], ACT.Exp).then_inc(S["gap_exp"], 1)
            act.wait_ge(S["gap_exp"], 1)

            def lead_tokens():
                act.wait_ge(S["xg_made"], 2)
                act.activation(xg_hi[:], xg, ACT.Copy).then_inc(S["xg_hi_made"], 1)

            def lead_next():
                lead_tokens()
                act.wait_ge(S["wpickT_full"], 1)
                act.wait_ge(S["scattered"], 4)
                act.activation(wpickT, by(ps[:, 3, 0:NT * P], h=P), ACT.Copy).then_inc(S["wpickT_made"], 1)

            lead_tokens()
            act.wait_ge(S["xg_hi_made"], 1)
            act.sem_inc(arrived, 1)
            act.wait_ge(routed, 1)
            n_items = act.value_load(item_tab[0:1, ITEM_SLOTS:ITEM_SLOTS + 1], min_val=EXPERTS, max_val=MAX_ITEMS)
            with act.Fori(0, n_items) as item:
                begin(act, item + (DEPTH + 2))
                act.activation(ysb[:, 0:N], ps[:, 4], ACT.Copy).then_inc(S["y_copied"], 1)

                def moe_full(u):
                    s = moe_slot(u)
                    act.wait_ge(ring_full[s], item * (16 * ITEM_USES) + 16 * (uses0[s] + u // MOE_RING + 1))

                ffn(MOE, 1, moe_slot, moe_full, lead_next, EARLY)
                with act.If(item < n_items - 1):
                    act.wait_ge(ring_full[0], item * (16 * ITEM_USES) + 16 * (uses0[0] + 1 + ITEM_USES))
                    lead_early(True)
                act.wait_ge(S["wpickT_made"], 1)
                act.wait_ge(S["panel_done"], len(MOE.order))
                act.sem_inc(arrived, 1)
            begin(act, n_items + (DEPTH + 2))
            act.activation(ysb[:, 0:N], ps[:, 4], ACT.Copy).then_inc(S["y_copied"], 1)

        @block.vector
        def _(dve):
            chain = Chain(dve, dve_steps)
            mark, link, sync = chain.mark, chain.link, chain.sync

            def rest(hi, s, at_, n):
                dve.tensor_tensor(w_lo[s][:, at_:at_ + n], slots[s][:, at_:at_ + n], hi.bitcast(F32), ALU.subtract
                                  ).then_inc(S["lo_made"], 1)

            def rest_early(made_before):
                for c in range(EARLY):
                    u, at_, n, _ = MOE.pieces[c]
                    dve.wait_ge(S["hi_made"], made_before + c + 1)
                    rest(w_hi[:, c, 0:n], moe_slot(u), at_, n)
                dve.wait_ge(S["lo_made"], made_before + EARLY)

            def ffn(split, tiles, slot_of, after=None, tokens=None, early=0):
                made = [early]

                def ready(c, u, first):
                    dve.wait_ge(S["hi_made"], c + 1 - early)

                def ahead(upto):
                    split_pieces(dve, split, made, upto, slot_of, rest, ready)

                for i, width in enumerate(split.widths):
                    ahead(split.through("up", i) + AHEAD)
                    dve.wait_ge(S["sg_made"], i + 1)
                    wait_panel(dve, split, "up", i)
                    if i:
                        dve.wait_ge(S["t_full"], i)
                    dve.tensor_tensor(h[:, 0:tiles, 0:width], ps[:, 2:2 + tiles, 0:width], sg[:, 0:tiles, 0:width],
                                      ALU.mult).then_inc(S["h_made"], 1)
                    if tokens and i == len(split.widths) - 1:
                        tokens()
                    ahead(turned_before(split, i, tiles) + AHEAD)
                    hidden_free(dve, split, i, tiles)
                    dve.wait_ge(S["hid_hi_made"], i + 1)
                    dve.tensor_tensor(hid_lo[:, hidden_in(i, tiles), 0:width], ps[:, 2:2 + tiles, 0:width],
                                      hid_hi[:, hidden_in(i, tiles), 0:width].bitcast(F32), ALU.subtract).then_inc(S["hid_made"], 1)
                    if i == len(split.widths) - 1:
                        ahead(len(split.pieces))
                    if after:
                        after(i)

            def root_mean(sums, n, eps, signal):
                dve.tensor_scalar(sums, sums, 1.0 / n, eps, ALU.mult, ALU.add).then_inc(signal, 1)

            dve.wait_ge(const_in, 48)
            dve.wait_ge(setup_done, 4)
            with dve.Fori(0, DEPTH) as L:
                chain.n = 0
                begin(dve, L + 1)
                rests = [0]

                def rest_mixer(upto):
                    while rests[0] < min(upto, len(MIXER_PIECES)):
                        c = rests[0]
                        rests[0] += 1
                        _, value, hi, lo = mixer_piece(c)
                        dve.wait_ge(S["mixer_hi_made"], c + 1)
                        dve.tensor_tensor(lo, value, hi.bitcast(F32), ALU.subtract).then_inc(S["mixer_lo_made"], 1)

                splitters[id(dve)] = rest_mixer
                b = take(dve, "vec")
                give("vec", dve.tensor_copy(cols[:], b[:, 0:N_ROWS]))
                dve.wait_ge(S["squared"], 2)
                root_mean(ss[:], D, EPS, S["mean_made"])
                dve.wait_ge(S["rooted"], 1)
                link(dve.reciprocal(rs[:], rs[:]))
                for t in range(NT):
                    dve.tensor_scalar(xn[:, t, :], x[:, t, :], rs[:, t:t + 1], None, ALU.mult).then_inc(S["normed"], 1)
                given(dve, "vec")
                for t in range(NT):
                    for hh in range(2):
                        b = take(dve, f"ht{t}{hh}")
                        give(f"ht{t}{hh}", dve.tensor_tensor(hT[:, 4 * hh:4 * hh + 4, t * P:(t + 1) * P], by(b, h=P),
                                                             spread(col("mix", 4 * hh, 4), P), ALU.mult))
                for t in range(NT):
                    for hh in range(2):
                        cut = (slice(None), slice(4 * hh, 4 * hh + 4), slice(t * P, (t + 1) * P))
                        dve.wait_ge(S["h_hi_made"], 2 * t + hh + 1)
                        dve.tensor_tensor(hT_lo[cut], hT[cut], hT_hi[cut].bitcast(F32), ALU.subtract
                                          ).then_inc(S["h_lo_made"], 1)
                for i in range(6):
                    if i == 4:
                        dve.wait_ge(S["dt_hi_made"], 1)
                        dve.tensor_tensor(w_dt_lo[:], w_dt[:], w_dt_hi.bitcast(F32), ALU.subtract
                                          ).then_inc(S["dt_lo_made"], 1)
                    given(dve, f"xbc{i}")
                    for tap in range(TAPS):
                        for j in range(2):
                            c = 2 * i + j
                            src = xin[:, i % 2, j, tap:tap + NT * P]
                            w = col("conv_w", tap * CONV_CHUNKS + c)
                            if tap == 0:
                                mark(dve.tensor_scalar(xc[:, c, :], src, w, col("conv_b", c), ALU.mult, ALU.add))
                            else:
                                ins = dve.scalar_tensor_tensor(xc[:, c, :], src, w, xc[:, c, :], ALU.mult, ALU.add)
                                if tap == TAPS - 1 and j == 1:
                                    ins.then_inc(S["conv_made"], 1)
                                else:
                                    mark(ins)
                        if tap < TAPS - 1:
                            sync()
                dve.wait_ge(small_in, 112)
                b = take(dve, "dt")
                give("dt", dve.tensor_tensor(dtr, by(b[:, 0:NT * HEADS], h=HEADS), repeat(heads_b[:, 0, :], NT), ALU.add))
                given(dve, "dt")
                dve.scalar_tensor_tensor(dtv, dtr, -1.0, dtr, ALU.mult, ALU.min).then_inc(S["dt_neg"], 1)
                dve.wait_ge(S["dt_neg"], 1)
                dve.wait_ge(S["dt_log"], 1)
                link(dve.scalar_tensor_tensor(dtr, dtr, 0.0, dte, ALU.max, ALU.add))
                dve.wait_ge(S["a_exp"], 1)
                dve.scalar_tensor_tensor(adt, dtr, -1.0, repeat(aexp, NT), ALU.mult, ALU.mult).then_inc(S["adt_made"], 1)
                keep_ahead(dve, "lat1")
                dve.wait_ge(S["latsq_made"], 2)
                link(dve.tensor_scalar(ssl[:, :, 0:1], ssl[:, :, 0:1], 1.0 / 256, EPS, ALU.mult, ALU.add))
                root_mean(ssl[:, :, 1:2], P, EPS, S["latmean_made"])
                dve.wait_ge(S["latroot_made"], 1)
                link(dve.reciprocal(rsl, rsl))
                for t in range(NT):
                    mark(dve.tensor_scalar(lat[:, t, 0:256], lat[:, t, 0:256], rsl[:, t, 0:1], None, ALU.mult))
                    dve.tensor_scalar(lat[:, t, 256:384], lat[:, t, 256:384], rsl[:, t, 1:2], None, ALU.mult
                                      ).then_inc(S["lat_normed"], 1)
                    dve.tensor_copy(by(k[:, t, :], h=QK)[:, :, NOPE:], repeat(lat[:, t, 384:LAT], HEADS)
                                    ).then_inc(S["kpe_made"], 1)
                b = take(dve, "cs")
                give("cs", dve.tensor_copy(csv, by(b[:, 0:4 * HEADS], h=HEADS)))
                given(dve, "cs")
                dve.tensor_tensor(decay, csv[:, 2, :], csv[:, 0, :], ALU.subtract).then_inc(S["tail_made"], 1)
                for t in range(NT):
                    given(dve, f"xt{t}0")
                    given(dve, f"xt{t}1")
                    dve.tensor_tensor(by(xs[:, t, :], h=HD), by(xh[:, t, :], h=HD), spread(dtr[:, t, :], HD), ALU.mult
                                      ).then_inc(S["xs_made"], 1)
                b = take(dve, "bt")
                give("bt", dve.tensor_copy(b_tok, by(b[:, 0:2 * P], h=P)))
                b = take(dve, "cb")
                give("cb", dve.tensor_tensor(cbm, by(b, h=P), repeat(tri, 4), ALU.mult))
                for t in range(NT):
                    b = take(dve, f"latT{t}")
                    give(f"latT{t}", dve.tensor_tensor(latT[:, :, t * P:(t + 1) * P], by(b[:, 0:3 * P], h=P),
                                                       spread(col("q", 0, 3), P), ALU.mult))
                dve.wait_ge(S["cs_exp"], 2)
                dve.wait_ge(S["xs_made"], 2)
                dve.tensor_tensor(by(xd, h=HD), by(xs[:, 0, :], h=HD), spread(decay, HD), ALU.mult
                                  ).then_inc(S["xd_made"], 1)
                for t in range(NT):
                    mark(dve.tensor_tensor(by(xh[:, t, :], h=HD), by(xh[:, t, :], h=HD), spread(heads_b[:, 2, :], HD),
                                           ALU.mult))
                sync()
                for g in range(2):
                    b = take(dve, f"yo{g}")
                    give(f"yo{g}", dve.tensor_tensor(by(xd[:, g * N:(g + 1) * N], h=HD), by(b, h=HD),
                                                     spread(expcs[:, 8 * g:8 * g + 8], HD), ALU.mult))
                for g in range(2):
                    given(dve, f"yo{g}")
                    cut = xh[:, 1, g * N:(g + 1) * N]
                    mark(dve.tensor_tensor(cut, cut, xd[:, g * N:(g + 1) * N], ALU.add))
                given(dve, "cb")
                for c in range(NT):
                    for qd in range(5):
                        if qd < 4:
                            b = take(dve, f"rb{c}{qd}")
                            if c:
                                dve.wait_ge(bank_full, JOB[f"yd0{qd // 2}"] + 1)
                            for i in range(4):
                                hh = 4 * qd + i
                                ins = dve.tensor_scalar(mt[:, qd, i * P:(i + 1) * P], b[:, i * P:(i + 1) * P],
                                                        csv[:, c, hh:hh + 1], 0.0, ALU.subtract, ALU.min)
                                if i == 3:
                                    give(f"rb{c}{qd}", ins)
                        if qd:
                            dve.wait_ge(S["decay_made"], 4 * c + qd)
                            m = by(mt[:, qd - 1, :], h=P)
                            dve.tensor_tensor(m, m, repeat(cbm[:, 2 * c + (qd - 1) // 2, :], 4), ALU.mult
                                              ).then_inc(S["mt_made"], 1)
                    sync()
                    for g in range(2):
                        cut = xh[:, c, g * N:(g + 1) * N]
                        b = take(dve, f"yd{c}{g}")
                        give(f"yd{c}{g}", dve.tensor_tensor(cut, b, cut, ALU.add))
                for n in range(2):
                    for t in range(NT):
                        cut = xh[:, t, n * N:(n + 1) * N]
                        given(dve, f"yd{t}{n}")
                        given(dve, f"z{n}{t}")
                        dve.tensor_tensor(cut, cut, gate[:, t, :], ALU.mult).then_inc(S["y_made"], 1)
                for i in range(2):
                    b = take(dve, f"wt{i}")
                    give(f"wt{i}", dve.tensor_tensor(sgu_wT[:, 4 * i:4 * i + 4, :], by(b, h=P), repeat(tri, 4), ALU.mult))
                dve.wait_ge(S["ysq_made"], 4)
                root_mean(ssg, N, EPS, S["ymean_made"])
                for t in range(NT):
                    for n in range(2):
                        given(dve, f"v{n}{t}")
                        mark(dve.bn_stats(bn[:, t, n, :], vs[:, t, n * N:(n + 1) * N]))
                sync()
                for t in range(NT):
                    mark(dve.bn_aggr(mv[:, t, :], bn[:, t, :, :].rearrange("p a b -> p (a b)")))
                sync()
                dve.tensor_scalar(by(lss, h=1), mv[:, :, 1:2], LN_EPS, None, ALU.add).then_inc(S["var_made"], 1)
                dve.wait_ge(S["yroot_made"], 1)
                dve.reciprocal(rsg, rsg).then_inc(S["y_scale_made"], 1)
                dve.wait_ge(S["vroot_made"], 1)
                link(dve.reciprocal(lrs, lrs))
                for t in range(NT):
                    mark(dve.tensor_scalar(vs[:, t, :], vs[:, t, :], mv[:, t, 0:1], lrs[:, t:t + 1],
                                           ALU.subtract, ALU.mult))
                sync()
                for what, op in (("lng", ALU.mult), ("lnb", ALU.add)):
                    rest_mixer(NEEDED["gate_ssd01"])
                    for hh in range(2):
                        b = take(dve, f"{what}{hh}")
                        for t in range(NT):
                            if what == "lnb":
                                given(dve, f"lng{hh}")
                            cut = vs[:, t, hh * N:(hh + 1) * N]
                            ins = dve.tensor_tensor(cut, b, cut, op)
                            if t == 1:
                                give(f"{what}{hh}", ins)
                            else:
                                mark(ins)
                    sync()
                given(dve, "lnb0")
                given(dve, "lnb1")
                dve.tensor_copy(small[:, 510:511], mv[:, 0, 0:1]).then_inc(S["v_normed"], 2)
                for t in range(NT):
                    for hh in range(2):
                        b = take(dve, f"yT_ssd{t}{hh}")
                        give(f"yT_ssd{t}{hh}", dve.tensor_tensor(yT[:, 4 * hh:4 * hh + 4, t * P:(t + 1) * P], by(b, h=P),
                                                                 spread(col("ssd", 4 * hh, 4), P), ALU.mult))
                for t in range(NT):
                    for hh in range(2):
                        cut = (slice(None), slice(4 * hh, 4 * hh + 4), slice(t * P, (t + 1) * P))
                        dve.wait_ge(S["yT_hi_made"], 2 * t + hh + 1)
                        dve.tensor_tensor(yT_lo[cut], yT[cut], ssd_hi[cut].bitcast(F32), ALU.subtract
                                          ).then_inc(S["yT_lo_made"], 1)
                turned_so_far = [4]

                def turned(name):
                    for t, hh in halves(name):
                        cut = (slice(None), slice(4 * hh, 4 * hh + 4), slice(t * P, (t + 1) * P))
                        b = take(dve, f"{name}{t}{hh}")
                        turned_so_far[0] += 1
                        dve.wait_ge(S["yT_hi_made"], turned_so_far[0])
                        give(f"{name}{t}{hh}", dve.tensor_tensor(yT_lo[cut], by(b, h=P), yT_hi[cut].bitcast(F32),
                                                                 ALU.subtract))
                    given(dve, f"{name}11")
                    dve.tensor_copy(small[:, 509:510], small[:, 510:511]).then_inc(S["yT_lo_made"], 4)

                def merge(br, n):
                    for t in range(NT):
                        b = take(dve, f"br_{br}{n}{t}")
                        given(dve, f"gate_{br}{n}{t}")
                        cut = merged[:, t, n * N:(n + 1) * N]
                        if br == "ssd":
                            give(f"br_{br}{n}{t}", dve.tensor_tensor(cut, b, gate[:, t, :], ALU.mult))
                            given(dve, f"br_{br}{n}{t}")
                            dve.tensor_copy(small[:, 509:510], small[:, 510:511]).then_inc(S["gated"], 1)
                        else:
                            give(f"br_{br}{n}{t}", dve.tensor_tensor(gate[:, t, :], b, gate[:, t, :], ALU.mult))
                            given(dve, f"br_{br}{n}{t}")
                            dve.tensor_tensor(cut, cut, gate[:, t, :], ALU.add).then_inc(S["gated"], 1)

                def head_norm(i):
                    src, t = (q, k)[i // 2], i % 2
                    a = by(src[:, t, :], h=QK)
                    dve.wait_ge(S["hsq_made"], i + 1)
                    link(dve.tensor_reduce(ssh, by(tmp, h=QK), AX.X, ALU.add))
                    rest_mixer(norm_pieces(i, 0))
                    root_mean(ssh, QK, EPS, S["hmean_made"])
                    dve.wait_ge(S["hroot_made"], i + 1)
                    link(dve.reciprocal(rsh, rsh))
                    link(dve.tensor_tensor(a, a, spread(rsh, QK), ALU.mult))
                    rest_mixer(norm_pieces(i, 1))
                    link(dve.tensor_tensor(a, a, repeat(gain_b[:, i // 2, :], HEADS), ALU.mult))
                    rest_mixer(norm_pieces(i, 2))
                    x1, x2 = a[:, :, NOPE:NOPE + HALF_ROPE], a[:, :, NOPE + HALF_ROPE:QK]
                    cs_, sn_ = repeat(cos[:, t, :], HEADS), repeat(sin[:, t, :], HEADS)
                    r = tmp[:, 0:4 * HEADS * HALF_ROPE].rearrange("p (a h c) -> p a h c", a=4, h=HEADS)
                    for j, (m, n) in enumerate(((x1, cs_), (x2, sn_), (x1, sn_), (x2, cs_))):
                        mark(dve.tensor_tensor(r[:, j], m, n, ALU.mult))
                    sync()
                    mark(dve.tensor_tensor(x1, r[:, 0], r[:, 1], ALU.subtract))
                    dve.tensor_tensor(x2, r[:, 2], r[:, 3], ALU.add).then_inc(S["hnorm_made"], 1)
                    rest_mixer(norm_pieces(i, 3))

                head_norm(0)
                head_norm(1)
                merge("ssd", 0)
                keep_ahead(dve, "gate_ssd11")
                head_norm(2)
                merge("ssd", 1)
                head_norm(3)
                for t in range(NT):
                    for n in range(2):
                        given(dve, f"u{n}{t}")
                    for hh in range(2):
                        b = take(dve, f"mx{t}{hh}")
                        for i in range(4):
                            g = 4 * hh + i
                            cut = u[:, t, g * P:(g + 1) * P]
                            ins = dve.scalar_tensor_tensor(cut, b[:, i * P:(i + 1) * P], col("sgu_b", g), cut,
                                                           ALU.add, ALU.mult)
                            if i == 3:
                                give(f"mx{t}{hh}", ins)
                for kind, i in attention_order():
                    if kind == "close":
                        if i == 1:
                            turned("yT_sgu")
                        if i in (2, 4):
                            merge("sgu", i // 2 - 1)
                        continue
                    if kind == "pt":
                        continue
                    t, h0, nh = GROUPS[i]
                    keys = (t + 1) * P
                    if kind == "sc":
                        b = take(dve, f"sc{i}")
                        if i >= 2:
                            dve.wait_ge(bank_full, JOB[f"pt{i - 2}"] + 1)
                        pr = by(prob[:, i % 2, :], h=keys)
                        give(f"sc{i}", dve.tensor_tensor(pr, by(b, h=keys), repeat(mask[:, 2 * P - keys:], nh), ALU.add))
                        given(dve, f"sc{i}")
                        link(dve.tensor_reduce(mx[:, 0:nh], pr, AX.X, ALU.max))
                        if i >= 2:
                            dve.wait_ge(S["prob_made"], i - 1)
                        dve.tensor_scalar(nmx[:, i % 2, 0:nh], mx[:, 0:nh], -SCALE, None, ALU.mult
                                          ).then_inc(S["max_made"], 1)
                        dve.wait_ge(S["max_made"], i + 1)
                    else:
                        dve.wait_ge(S["prob_made"], i + 1)
                        link(dve.reciprocal(rinv[:, t, h0:h0 + nh], rsum[:, t, h0:h0 + nh]))
                        b = take(dve, f"o{i}")
                        give(f"o{i}", dve.tensor_tensor(by(o[:, t, h0 * HD:(h0 + nh) * HD], h=HD), by(b[:, 0:nh * HD], h=HD),
                                                        spread(rinv[:, t, h0:h0 + nh], HD), ALU.mult))
                        given(dve, f"o{i}")
                        dve.tensor_copy(small[:, 509:510], small[:, 510:511]).then_inc(S["o_made"], 1)
                turned("yT_mla")
                merge("mla", 0)
                merge("mla", 1)
                turned("mT")
                for n in range(2):
                    for t in range(NT):
                        b = take(dve, f"out{n}{t}")
                        cut = x[:, t, n * N:(n + 1) * N]
                        give(f"out{n}{t}", dve.tensor_tensor(cut, b, cut, ALU.add))
                dve.wait_ge(S["fsquared"], 2)
                root_mean(ss[:], D, EPS, S["fmean_made"])
                dve.wait_ge(S["frooted"], 1)
                link(dve.reciprocal(rs[:], rs[:]))
                for t in range(NT):
                    dve.tensor_scalar(fn[:, t, :], x[:, t, :], rs[:, t:t + 1], None, ALU.mult).then_inc(S["fnormed"], 1)
                for t in range(NT):
                    for hh in range(2):
                        b = take(dve, f"ft{t}{hh}")
                        give(f"ft{t}{hh}", dve.tensor_tensor(hT[:, 4 * hh:4 * hh + 4, t * P:(t + 1) * P], by(b, h=P),
                                                             spread(col("ffn", 4 * hh, 4), P), ALU.mult))
                steps = chain.n
                with dve.If(L < 1):
                    for half in range(2):
                        cut = (slice(None), slice(4 * half, 4 * half + 4))
                        dve.wait_ge(S["hT_hi_made"], half + 1)
                        dve.tensor_tensor(hT_lo[cut], hT[cut], hT_hi[cut].bitcast(F32), ALU.subtract
                                          ).then_inc(S["hT_lo_made"], 1)
                    ffn(DENSE, NT, dense_slot)
                    dve.wait_ge(S["panel_done"], len(DENSE.order))
                    for t in range(NT):
                        for half in range(2):
                            cut = x[:, t, half * N:(half + 1) * N]
                            dve.tensor_tensor(cut, ps[:, 4 + 2 * t + half], cut, ALU.add)
                assert chain.n == steps
                link(dve.tensor_copy(small[:, 509:510], small[:, 510:511]))
                dve.sem_inc(arrived, 1)

            chain.n = 0
            begin(dve, DEPTH + 1)
            rest_early(0)

            def r(n):
                return route[:, n]

            expert2 = by(cst("expert", NT * EXPERTS), h=EXPERTS)
            dve.wait_ge(S["logits"], 1)
            link(dve.tensor_copy(r(0), by(ps[:, 0, 0:NT * EXPERTS], h=EXPERTS)))
            m1, m2, low = (r(n)[:, :, 0:1] for n in (1, 2, 5))

            def wide(a):
                return a.to_broadcast([P, NT, EXPERTS])

            def choose(logits, top, out_):
                link(dve.tensor_reduce(top, logits, AX.X, ALU.max))
                link(dve.tensor_tensor(r(6), logits, wide(top), ALU.is_equal))
                link(dve.scalar_tensor_tensor(r(7), expert2, float(EXPERTS), r(6), ALU.subtract, ALU.mult))
                link(dve.tensor_reduce(low, r(7), AX.X, ALU.min))
                link(dve.tensor_tensor(out_, r(7), wide(low), ALU.is_equal))

            choose(r(0), m1, r(8))
            link(dve.scalar_tensor_tensor(r(9), r(8), -1e30, r(0), ALU.mult, ALU.add))
            choose(r(9), m2, r(10))
            dve.tensor_tensor(r(3)[:, :, 0:1], m2, m1, ALU.subtract).then_inc(S["gap_made"], 1)
            dve.tensor_tensor(chosen, r(8), r(10), ALU.add).then_inc(S["chosen"], 1)
            e_, w1, w2 = r(4)[:, :, 0:1], r(4)[:, :, 1:2], r(4)[:, :, 2:3]
            dve.wait_ge(S["gap_exp"], 1)
            link(dve.tensor_scalar(w1, e_, 1.0, None, ALU.add))
            link(dve.reciprocal(w1, w1))
            link(dve.tensor_tensor(w2, e_, w1, ALU.mult))
            mark(dve.tensor_tensor(r(8), r(8), wide(w1), ALU.mult))
            mark(dve.tensor_tensor(r(10), r(10), wide(w2), ALU.mult))
            sync()
            link(dve.tensor_tensor(r(9), r(8), r(10), ALU.add))
            dve.wait_ge(S["ranks"], 1)
            E8 = EXPERTS
            link(dve.tensor_scalar(r(0), by(ps[:, 1, 0:NT * E8], h=E8), 1.0, None, ALU.add))
            link(dve.tensor_tensor(r(0), r(0), chosen, ALU.mult))
            link(dve.tensor_scalar(r(0), r(0), -1.0, None, ALU.add))
            big, start = r(6)[:, 0, :], r(6)[:, 1, :]
            link(dve.tensor_scalar(big, ps[:, 1, 2 * E8:3 * E8], float(P), None, ALU.is_gt))
            link(dve.tensor_copy(start, cst("expert", E8)))
            for e in range(1, E8):
                link(dve.tensor_tensor(start[:, e:E8], start[:, e:E8], big[:, e - 1:e].to_broadcast([P, E8 - e]), ALU.add))
            grid = [by(items[:, n, :], h=E8) for n in range(8)]
            number = by(cst("item", ITEM_SLOTS * E8), h=E8)
            which = by(cst("expert", ITEM_SLOTS * E8), h=E8)
            expert_of = items[:, 4, 0:ITEM_SLOTS]
            block_of = items[:, 5, 0:ITEM_SLOTS]
            mark(dve.tensor_tensor(grid[0], number, repeat(start, ITEM_SLOTS), ALU.is_ge))
            mark(dve.tensor_tensor(grid[1], number, repeat(start, ITEM_SLOTS), ALU.is_equal))
            sync()
            mark(dve.tensor_reduce(expert_of, grid[0], AX.X, ALU.add))
            mark(dve.tensor_reduce(block_of, grid[1], AX.X, ALU.add))
            sync()
            mark(dve.tensor_scalar(expert_of, expert_of, -1.0, None, ALU.add))
            mark(dve.tensor_scalar(block_of, block_of, -float(P), float(P), ALU.mult, ALU.add))
            sync()
            link(dve.tensor_tensor(grid[2], which, spread(expert_of, E8), ALU.is_equal))
            for t in range(NT):
                link(dve.tensor_tensor(grid[3], grid[2], repeat(r(0)[:, t, :], ITEM_SLOTS), ALU.mult))
                link(dve.tensor_reduce(pos_item[:, t, :], grid[3], AX.X, ALU.add))
                link(dve.tensor_tensor(pos_item[:, t, :], pos_item[:, t, :], block_of, ALU.subtract))
                link(dve.tensor_tensor(grid[3], grid[2], repeat(r(9)[:, t, :], ITEM_SLOTS), ALU.mult))
                link(dve.tensor_reduce(w_item[:, t, :], grid[3], AX.X, ALU.add))
            link(dve.tensor_reduce(items[:, 6, 0:1], big, AX.X, ALU.add))
            link(dve.tensor_scalar(items[:, 6, 0:1], items[:, 6, 0:1], float(EXPERTS), None, ALU.add))
            link(dve.tensor_copy(item_tab[0:1, 0:ITEM_SLOTS], expert_of[0:1, :]))
            dve.tensor_copy(item_tab[0:1, ITEM_SLOTS:ITEM_SLOTS + 1], items[0:1, 6, 0:1]).then_inc(routed, 1)

            def pick_tokens(i):
                for t in range(NT):
                    ins = dve.tensor_scalar(pick[:, t, :], slot_no, pos_item[:, t, i], None, ALU.is_equal)
                ins.then_inc(S["picked"], 1)

            def take_tokens():
                for hh in range(2):
                    dve.wait_ge(S["gathered"], hh + 1)
                    dve.tensor_tensor(xg[:, 4 * hh:4 * hh + 4, :], by(ps[:, 6 + hh], h=P), spread(col("ffn", 4 * hh, 4), P),
                                      ALU.mult).then_inc(S["xg_made"], 1)

            def rest_of_tokens():
                dve.wait_ge(S["xg_hi_made"], 1)
                dve.tensor_tensor(xg_lo[:], xg, xg_hi[:].bitcast(F32), ALU.subtract).then_inc(S["xg_lo_made"], 1)

            def add_outputs(signal):
                for j in range(4):
                    t, half = j // 2, j % 2
                    dve.wait_ge(S["scattered"], j + 1)
                    cut = x[:, t, half * N:(half + 1) * N]
                    ins = dve.tensor_tensor(cut, ps[:, SCATTER_BANKS[j]], cut, ALU.add)
                    if half:
                        ins.then_inc(signal, 1)

            pick_tokens(slice(0, 1))
            dve.memset(ps[:, 4:6, :], 0.0)
            dve.memset(wpickT, 0.0).then_inc(S["zeroed"], 1)
            take_tokens()
            rest_of_tokens()
            dve.wait_ge(S["zeroed"], 1)
            dve.wait_ge(S["xg_lo_made"], 1)
            dve.wait_ge(routed, 1)
            n_items = dve.value_load(item_tab[0:1, ITEM_SLOTS:ITEM_SLOTS + 1], min_val=EXPERTS, max_val=MAX_ITEMS)
            dve.sem_inc(arrived, 1)

            with dve.Fori(0, n_items) as item:
                begin(dve, item + (DEPTH + 2))
                dve.tensor_copy(ysb[:, N:2 * N], ps[:, 5]).then_inc(S["y_copied"], 1)

                def after(i):
                    if i == 0:
                        add_outputs(S["added"])
                    if i == len(MOE_PANELS) - 3:
                        pick_tokens(bass.ds(item + 1, 1))
                        for t in range(NT):
                            ins = dve.tensor_scalar(wpick[:, t, :], slot_no, pos_item[:, t, bass.ds(item, 1)],
                                                    w_item[:, t, bass.ds(item, 1)], ALU.is_equal, ALU.mult)
                        ins.then_inc(S["picked"], 1)
                    if i == len(MOE_PANELS) - 1:
                        rest_of_tokens()

                ffn(MOE, 1, moe_slot, after, take_tokens, EARLY)
                with dve.If(item < n_items - 1):
                    rest_early(len(MOE.pieces) - EARLY)
                dve.wait_ge(S["xg_lo_made"], 1)
                dve.wait_ge(S["panel_done"], len(MOE.order))
                dve.sem_inc(arrived, 1)
            begin(dve, n_items + (DEPTH + 2))
            dve.tensor_copy(ysb[:, N:2 * N], ps[:, 5]).then_inc(S["y_copied"], 1)
            add_outputs(finished)


_INS = ["x", "mix_norm_g", "w_in", "conv_w", "conv_b", "dt_bias", "a_log", "d_skip", "ssd_norm_g", "sgu_ln_g",
        "sgu_ln_b", "sgu_w", "sgu_b", "q_norm_g", "w_uq", "kv_norm_g", "w_ukv", "q_head_g", "k_head_g", "w_br_ssd",
        "w_br_sgu", "w_br_mla", "w_out", "ffn_norm_g", "ffn_w_gate", "ffn_w_up", "ffn_w_down", "router_w",
        "moe_w_gate", "moe_w_up", "moe_w_down"]


def constant_table():
    import numpy as np

    c = np.zeros((P, N_CONST), np.float32)
    p, f = np.arange(P)[:, None], np.arange(P)[None, :]
    c[:, CONST["ident"]:][:, :P] = p == f
    c[:, CONST["tri"]:][:, :P] = p <= f
    c[:, CONST["before"]:][:, :P] = p < f
    c[:, CONST["slot"]:][:, :P] = f
    c[:, CONST["mask"] + P:][:, :P] = np.where(f <= p, 0.0, -1e30)
    inv = (1.0 / (np.float32(10000.0) ** (np.arange(0, 2 * HALF_ROPE, 2, dtype=np.float32) / np.float32(2 * HALF_ROPE)))
           ).astype(np.float32)
    for t in range(NT):
        ang = ((t * P + np.arange(P)).astype(np.float32)[:, None] * inv[None, :]).astype(np.float32)
        c[:, CONST["cos"] + HALF_ROPE * t:][:, :HALF_ROPE] = np.cos(ang)
        c[:, CONST["sin"] + HALF_ROPE * t:][:, :HALF_ROPE] = np.sin(ang)
    i = np.arange(ITEM_SLOTS * EXPERTS)
    c[:, CONST["item"]:][:, :i.size] = i // EXPERTS
    c[:, CONST["expert"]:][:, :i.size] = i % EXPERTS
    return c


def kernel(**inputs):
    import numpy as np
    import concourse.bacc as bacc
    from concourse.bass_utils import run_bass_kernel_spmd as run

    nc = bacc.Bacc("TRN2", target_bir_lowering=False, num_devices=1)
    arrays, aps = {}, {}
    for name in _INS + ["const"]:
        a = constant_table() if name == "const" else np.ascontiguousarray(inputs[name])
        arrays[f"in_{name}"] = a
        aps[name] = nc.dram_tensor(f"in_{name}", a.shape, mybir.dt.from_np(a.dtype), kind="ExternalInput").ap()
    out = nc.dram_tensor("out_0", (1, NT * P, D), F32, kind="ExternalOutput").ap()
    hybrid_trunk(nc, aps, out)
    return run(nc, [arrays], core_ids=[0]).results[0]["out_0"]
```
